# Optimizing a Trainium2 kernel written in Bass

```python
import math
import jax, jax.numpy as jnp
from jax import lax
import numpy as np

D_MODEL = 1024
BATCH = 1
SEQ = 256
DEPTH = 2

N_MIXERS = 2
N_RET_LAYERS = (DEPTH + 1) // 2
N_MLA_LAYERS = DEPTH // 2
MIX_WIDTH = D_MODEL
MEM_LEN = 256
MEM_HEADS = 4
MEM_HEAD_DIM = 64
MEM_WIDTH = MEM_HEADS * MEM_HEAD_DIM
TOK_WIDTH = MIX_WIDTH - MEM_WIDTH
RET_HEADS = 6
RET_DK = 128
RET_DV = TOK_WIDTH // RET_HEADS
RET_CHUNK = 128
RET_IN = 4 * TOK_WIDTH + MEM_WIDTH
MLA_HEADS = 6
MLA_NOPE = 64
MLA_ROPE = 32
MLA_DV = TOK_WIDTH // MLA_HEADS
MLA_Q_RANK = 256
MLA_KV_RANK = 128
MLA_IN = MLA_Q_RANK + MLA_KV_RANK + MLA_ROPE + MEM_WIDTH
MLA_SCALE = (MLA_NOPE + MLA_ROPE) ** -0.5
Q_BLOCK = 128
D_FF = 2816
FFN_RES_WEIGHT = 0.5
ROPE_THETA = 10000.0
NORM_EPS = 1e-6


def rms_norm(x, g):
    xf = x.astype(jnp.float32)
    y = xf * lax.rsqrt(jnp.mean(xf * xf, axis=-1, keepdims=True) + NORM_EPS)
    return (y * g.astype(jnp.float32)).astype(x.dtype)

def head_layer_norm(y, g):
    mu = jnp.mean(y, axis=-1, keepdims=True)
    var = jnp.mean(jnp.square(y - mu), axis=-1, keepdims=True)
    return (y - mu) * lax.rsqrt(var + NORM_EPS) * g.astype(jnp.float32)

def rope_tables(positions, dim):
    inv = 1.0 / (ROPE_THETA ** (jnp.arange(0, dim, 2, dtype=jnp.float32) / dim))
    ang = positions.astype(jnp.float32)[..., None] * inv
    return jnp.cos(ang), jnp.sin(ang)

def apply_rope(x, cos, sin):
    half = x.shape[-1] // 2
    x1, x2 = x[..., :half], x[..., half:]
    c = cos[:, :, None, :].astype(x.dtype)
    s = sin[:, :, None, :].astype(x.dtype)
    return jnp.concatenate([x1 * c - x2 * s, x1 * s + x2 * c], axis=-1)

def swiglu(h, w_gu, w_down):
    g, u = jnp.split(h @ w_gu, 2, axis=-1)
    return (jax.nn.silu(g) * u) @ w_down

def retention_chunkwise(q, k, v, log_gamma, strict):
    B, S, H, dk = q.shape
    dv = v.shape[-1]
    n = S // RET_CHUNK
    C = RET_CHUNK
    q = q.astype(jnp.float32).reshape(B, n, C, H, dk)
    k = k.astype(jnp.float32).reshape(B, n, C, H, dk)
    v = v.astype(jnp.float32).reshape(B, n, C, H, dv)
    lg = log_gamma.astype(jnp.float32)
    idx = jnp.arange(C, dtype=jnp.float32)
    diff = idx[:, None] - idx[None, :]
    mask = diff > 0 if strict else diff >= 0
    decay = jnp.where(mask[None], jnp.exp(jnp.where(mask, diff, 0.0)[None] * lg[:, None, None]), 0.0)
    scores = jnp.einsum('bnihd,bnjhd->bnhij', q, k) * decay[None, None]
    intra = jnp.einsum('bnhij,bnjhv->bnihv', scores, v)
    k_w = k * jnp.exp((C - 1.0 - idx)[:, None] * lg[None, :])[None, None, :, :, None]
    chunk_kv = jnp.einsum('bnjhd,bnjhv->bnhdv', k_w, v)
    g_chunk = jnp.exp(C * lg)[None, :, None, None]

    def step(state, kv_n):
        return state * g_chunk + kv_n, state

    init = jnp.zeros((B, H, dk, dv), jnp.float32)
    _, states = lax.scan(step, init, jnp.moveaxis(chunk_kv, 1, 0))
    states = jnp.moveaxis(states, 0, 1)
    q_w = q * jnp.exp((idx + 1.0)[:, None] * lg[None, :])[None, None, :, :, None]
    cross = jnp.einsum('bnihd,bnhdv->bnihv', q_w, states)
    return (intra + cross).reshape(B, S, H, dv)

def retention_mixer(h, w_in, log_decay, head_norm, cos, sin):
    B, S, _ = h.shape
    T = TOK_WIDTH
    q, k, v, g, qm = jnp.split(h @ w_in, [T, 2 * T, 3 * T, 4 * T], axis=-1)
    q = apply_rope(q.reshape(B, S, RET_HEADS, RET_DK), cos, sin)
    k = apply_rope(k.reshape(B, S, RET_HEADS, RET_DK), cos, sin) * (RET_DK ** -0.5)
    v = v.reshape(B, S, RET_HEADS, RET_DV)
    y_fwd = retention_chunkwise(q, k, v, log_decay[0], strict=False)
    y_bwd = retention_chunkwise(q[:, ::-1], k[:, ::-1], v[:, ::-1], log_decay[1], strict=True)[:, ::-1]
    y = head_layer_norm(y_fwd + y_bwd, head_norm).reshape(B, S, T).astype(h.dtype)
    return jax.nn.silu(g) * y, qm

def dense_attention_blocked(q, k, v, scale):
    B, S, H, dq = q.shape
    dv = v.shape[-1]
    n = S // Q_BLOCK
    qb = q.reshape(B, n, Q_BLOCK, H, dq).transpose(1, 0, 2, 3, 4)

    def one_block(q_blk):
        s = jnp.einsum('bqhd,bkhd->bhqk', q_blk, k).astype(jnp.float32) * scale
        p = jax.nn.softmax(s, axis=-1).astype(v.dtype)
        return jnp.einsum('bhqk,bkhv->bqhv', p, v)

    o = lax.map(one_block, qb)
    return o.transpose(1, 0, 2, 3, 4).reshape(B, S, H * dv)

def mla_mixer(h, w_in, q_norm, kv_norm, w_uq, w_ukv, cos, sin):
    B, S, _ = h.shape
    c_q, c_kv, k_r, qm = jnp.split(
        h @ w_in, [MLA_Q_RANK, MLA_Q_RANK + MLA_KV_RANK, MLA_Q_RANK + MLA_KV_RANK + MLA_ROPE], axis=-1)
    c_q = rms_norm(c_q, q_norm)
    c_kv = rms_norm(c_kv, kv_norm)
    q = (c_q @ w_uq).reshape(B, S, MLA_HEADS, MLA_NOPE + MLA_ROPE)
    q = jnp.concatenate([q[..., :MLA_NOPE], apply_rope(q[..., MLA_NOPE:], cos, sin)], axis=-1)
    kv = (c_kv @ w_ukv).reshape(B, S, MLA_HEADS, MLA_NOPE + MLA_DV)
    k_nope, v = kv[..., :MLA_NOPE], kv[..., MLA_NOPE:]
    k_rope = apply_rope(k_r.reshape(B, S, 1, MLA_ROPE), cos, sin)
    k = jnp.concatenate([k_nope, jnp.broadcast_to(k_rope, (B, S, MLA_HEADS, MLA_ROPE))], axis=-1)
    return dense_attention_blocked(q, k, v, MLA_SCALE), qm

def memory_attention(qm, mem_n, w_kv):
    B, S, _ = qm.shape
    L = mem_n.shape[1]
    q = qm.reshape(B, S, MEM_HEADS, MEM_HEAD_DIM)
    mk, mv = jnp.split(mem_n @ w_kv, 2, axis=-1)
    mk = mk.reshape(B, L, MEM_HEADS, MEM_HEAD_DIM)
    mv = mv.reshape(B, L, MEM_HEADS, MEM_HEAD_DIM)
    s = jnp.einsum('bshd,bmhd->bhsm', q, mk).astype(jnp.float32) * (MEM_HEAD_DIM ** -0.5)
    p = jax.nn.softmax(s, axis=-1).astype(mv.dtype)
    return jnp.einsum('bhsm,bmhd->bshd', p, mv).reshape(B, S, MEM_WIDTH)

def first_inputs(seed: int = 0) -> dict:
    key = jax.random.key(seed)
    ks = jax.random.split(key, 17)
    f32 = jnp.float32

    def w(k, shape, fan_in):
        return jax.random.normal(k, shape, f32) * (fan_in ** -0.5)

    def gain(k, shape):
        return 1.0 + 0.02 * jax.random.normal(k, shape, f32)

    x = jax.random.normal(ks[0], (BATCH, SEQ, D_MODEL), f32)
    mem = jax.random.normal(ks[1], (BATCH, MEM_LEN, D_MODEL), f32)
    offsets = jax.random.randint(ks[2], (BATCH, 1), 0, 1024, dtype=jnp.int32)
    positions = (offsets + jnp.arange(SEQ, dtype=jnp.int32)[None, :]).astype(jnp.int32)
    base_decay = jnp.log(1.0 - 2.0 ** (-5.0 - jnp.arange(RET_HEADS, dtype=f32)))
    ret_log_decay = base_decay[None, None, :] * (1.0 + 0.05 * jax.random.normal(ks[10], (N_RET_LAYERS, 2, RET_HEADS), f32))
    return {
        "x": x,
        "mem": mem,
        "positions": positions,
        "norm_gains": gain(ks[3], (DEPTH, 6, D_MODEL)),
        "ffn_w_gu": w(ks[4], (DEPTH, 2, D_MODEL, 2 * D_FF), D_MODEL),
        "ffn_w_down": w(ks[5], (DEPTH, 2, D_FF, D_MODEL), D_FF),
        "w_o": w(ks[6], (DEPTH, MIX_WIDTH, D_MODEL), MIX_WIDTH),
        "mem_norm": gain(ks[7], (D_MODEL,)),
        "mem_w_kv": w(ks[8], (DEPTH, D_MODEL, 2 * MEM_WIDTH), D_MODEL),
        "ret_w_in": w(ks[9], (N_RET_LAYERS, D_MODEL, RET_IN), D_MODEL),
        "ret_log_decay": ret_log_decay,
        "ret_head_norm": gain(ks[11], (N_RET_LAYERS, RET_HEADS, RET_DV)),
        "mla_w_in": w(ks[12], (N_MLA_LAYERS, D_MODEL, MLA_IN), D_MODEL),
        "mla_q_norm": gain(ks[13], (N_MLA_LAYERS, MLA_Q_RANK)),
        "mla_kv_norm": gain(ks[14], (N_MLA_LAYERS, MLA_KV_RANK)),
        "mla_w_uq": w(ks[15], (N_MLA_LAYERS, MLA_Q_RANK, MLA_HEADS * (MLA_NOPE + MLA_ROPE)), MLA_Q_RANK),
        "mla_w_ukv": w(ks[16], (N_MLA_LAYERS, MLA_KV_RANK, MLA_HEADS * (MLA_NOPE + MLA_DV)), MLA_KV_RANK),
    }

def first_block(x, mem, positions, norm_gains, ffn_w_gu, ffn_w_down, w_o, mem_norm, mem_w_kv,
              ret_w_in, ret_log_decay, ret_head_norm,
              mla_w_in, mla_q_norm, mla_kv_norm, mla_w_uq, mla_w_ukv):
    cos_ret, sin_ret = rope_tables(positions, RET_DK)
    cos_mla, sin_mla = rope_tables(positions, MLA_ROPE)
    mem_n = rms_norm(mem, mem_norm)

    for l in range(DEPTH):
        ng = norm_gains[l]
        x = x + FFN_RES_WEIGHT * rms_norm(swiglu(rms_norm(x, ng[0]), ffn_w_gu[l, 0], ffn_w_down[l, 0]), ng[1])
        h = rms_norm(x, ng[2])
        r = l // N_MIXERS
        if l % N_MIXERS == 0:
            tok, qm = retention_mixer(h, ret_w_in[r], ret_log_decay[r], ret_head_norm[r], cos_ret, sin_ret)
        else:
            tok, qm = mla_mixer(h, mla_w_in[r], mla_q_norm[r], mla_kv_norm[r], mla_w_uq[r], mla_w_ukv[r],
                                cos_mla, sin_mla)
        mem_out = memory_attention(qm, mem_n, mem_w_kv[l])
        mix = jnp.concatenate([tok, mem_out], axis=-1) @ w_o[l]
        x = x + rms_norm(mix, ng[3])
        x = x + FFN_RES_WEIGHT * rms_norm(swiglu(rms_norm(x, ng[4]), ffn_w_gu[l, 1], ffn_w_down[l, 1]), ng[5])
    return x


MIX_WIDTH_2 = D_MODEL
ATTN_HEADS = 8
ATTN_HEAD_DIM = 64
ATTN_DIM = ATTN_HEADS * ATTN_HEAD_DIM
CONV_DIM = D_MODEL // 4
CONV_WIDTH = 3
POOL_WINDOWS = (2, 4, 8, 16)
N_POOL_GROUPS = len(POOL_WINDOWS)
POOL_DIM = D_MODEL // 4
POOL_GD = POOL_DIM // N_POOL_GROUPS
RMS_EPS = 1e-6
SPLIT_SIZES = (ATTN_DIM, ATTN_DIM, ATTN_DIM, CONV_DIM, CONV_DIM, CONV_DIM, POOL_DIM)
IN_PROJ_WIDTH = sum(SPLIT_SIZES)
SPLIT_POINTS = tuple(int(v) for v in np.cumsum(SPLIT_SIZES)[:-1])


def _rmsnorm(x, g):
    x32 = x.astype(jnp.float32)
    y = x32 * lax.rsqrt(jnp.mean(x32 * x32, axis=-1, keepdims=True) + RMS_EPS)
    return (y * g.astype(jnp.float32)).astype(x.dtype)

def _swiglu(h, w_gate, w_up, w_down):
    return (jax.nn.silu(h @ w_gate) * (h @ w_up)) @ w_down

def _stick_breaking_attention(q, k, v):
    B, S, H, dh = q.shape
    nb = S // Q_BLOCK
    scale = 1.0 / math.sqrt(dh)
    kh = k.transpose(0, 2, 1, 3)
    vh = v.transpose(0, 2, 1, 3)
    q_blocks = q.transpose(0, 2, 1, 3).reshape(B, H, nb, Q_BLOCK, dh).transpose(2, 0, 1, 3, 4)
    k_pos = jnp.arange(S)

    def block(args):
        q_blk, start = args
        q_pos = start + jnp.arange(Q_BLOCK)
        z = jnp.einsum('bhqd,bhkd->bhqk', q_blk, kh).astype(jnp.float32) * scale
        mask = k_pos[None, :] < q_pos[:, None]
        log_keep = jnp.where(mask, jax.nn.log_sigmoid(-z), 0.0)
        between = lax.cumsum(log_keep, axis=3, reverse=True) - log_keep
        a = jnp.where(mask, jnp.exp(jax.nn.log_sigmoid(z) + between), 0.0)
        return jnp.einsum('bhqk,bhkd->bhqd', a.astype(vh.dtype), vh)

    out = lax.map(block, (q_blocks, jnp.arange(nb) * Q_BLOCK))
    return out.transpose(1, 0, 3, 2, 4).reshape(B, S, H * dh)

def _short_conv(gate_b, gate_c, h, conv_w):
    S = h.shape[1]
    u = gate_c * h
    u_pad = jnp.pad(u, ((0, 0), (CONV_WIDTH - 1, 0), (0, 0)))
    y = conv_w[0] * u_pad[:, 0:S] + conv_w[1] * u_pad[:, 1:S + 1] + conv_w[2] * u_pad[:, 2:S + 2]
    return gate_b * y

def _multiscale_pool(p, pool_w, pool_scale):
    B, S, C = p.shape
    p32 = p.astype(jnp.float32).reshape(B, S, N_POOL_GROUPS, POOL_GD)
    cs0 = jnp.pad(jnp.cumsum(p32, axis=1), ((0, 0), (1, 0), (0, 0), (0, 0)))
    count_base = jnp.arange(1, S + 1, dtype=jnp.float32)
    outs = []
    for gi, w in enumerate(POOL_WINDOWS):
        lagged = jnp.pad(cs0[:, :S + 1 - w, gi], ((0, 0), (w - 1, 0), (0, 0)))
        mean = (cs0[:, 1:, gi] - lagged) / jnp.minimum(count_base, w)[None, :, None]
        outs.append(mean - p32[:, :, gi])
    d = jnp.stack(outs, axis=2).astype(p.dtype)
    y = jnp.einsum('bsgc,gcd->bsgd', d, pool_w).reshape(B, S, C)
    return y * pool_scale

def _mixer(h, w_in, conv_w, pool_w, pool_scale, w_out):
    B, S, _ = h.shape
    proj = h @ w_in
    q, k, v, gate_b, gate_c, conv_h, pool_in = jnp.split(proj, SPLIT_POINTS, axis=-1)
    q = q.reshape(B, S, ATTN_HEADS, ATTN_HEAD_DIM)
    k = k.reshape(B, S, ATTN_HEADS, ATTN_HEAD_DIM)
    v = v.reshape(B, S, ATTN_HEADS, ATTN_HEAD_DIM)
    attn = _stick_breaking_attention(q, k, v)
    conv = _short_conv(gate_b, gate_c, conv_h, conv_w)
    pool = _multiscale_pool(pool_in, pool_w, pool_scale)
    return jnp.concatenate([attn, conv, pool], axis=-1) @ w_out

def second_inputs(seed: int = 0) -> dict:
    key = jax.random.key(seed)
    ks = jax.random.split(key, 11)
    f32 = jnp.float32
    x = jax.random.normal(ks[0], (BATCH, SEQ, D_MODEL), f32)
    norm_g = 1.0 + 0.05 * jax.random.normal(ks[1], (DEPTH, 6, D_MODEL), f32)
    ffn_w_gate = jax.random.normal(ks[2], (DEPTH, 2, D_MODEL, D_FF), f32) * D_MODEL ** -0.5
    ffn_w_up = jax.random.normal(ks[3], (DEPTH, 2, D_MODEL, D_FF), f32) * D_MODEL ** -0.5
    ffn_w_down = jax.random.normal(ks[4], (DEPTH, 2, D_FF, D_MODEL), f32) * D_FF ** -0.5
    w_in = jax.random.normal(ks[5], (DEPTH, D_MODEL, IN_PROJ_WIDTH), f32) * D_MODEL ** -0.5
    conv_w = jax.random.normal(ks[6], (DEPTH, CONV_WIDTH, CONV_DIM), f32) * CONV_WIDTH ** -0.5
    pool_w = jax.random.normal(ks[7], (DEPTH, N_POOL_GROUPS, POOL_GD, POOL_GD), f32) * POOL_GD ** -0.5
    pool_scale = 1.0 + 0.05 * jax.random.normal(ks[8], (DEPTH, POOL_DIM), f32)
    w_out = jax.random.normal(ks[9], (DEPTH, MIX_WIDTH_2, D_MODEL), f32) * MIX_WIDTH_2 ** -0.5
    return {"x": x, "norm_g": norm_g, "ffn_w_gate": ffn_w_gate, "ffn_w_up": ffn_w_up,
            "ffn_w_down": ffn_w_down, "w_in": w_in, "conv_w": conv_w, "pool_w": pool_w,
            "pool_scale": pool_scale, "w_out": w_out}

def second_block(x, norm_g, ffn_w_gate, ffn_w_up, ffn_w_down, w_in, conv_w, pool_w, pool_scale, w_out):
    for l in range(DEPTH):
        g = norm_g[l]
        f = _swiglu(_rmsnorm(x, g[0]), ffn_w_gate[l, 0], ffn_w_up[l, 0], ffn_w_down[l, 0])
        x = x + 0.5 * _rmsnorm(f, g[1])
        m = _mixer(_rmsnorm(x, g[2]), w_in[l], conv_w[l], pool_w[l], pool_scale[l], w_out[l])
        x = x + _rmsnorm(m, g[3])
        f = _swiglu(_rmsnorm(x, g[4]), ffn_w_gate[l, 1], ffn_w_up[l, 1], ffn_w_down[l, 1])
        x = x + 0.5 * _rmsnorm(f, g[5])
    return x


def setup_inputs(seed=0):
    out = dict(first_inputs(seed))
    for name, value in second_inputs(seed + 1).items():
        if name != "x":
            out[name + "_2"] = value
    return out


def reference(
    x, mem, positions, norm_gains, ffn_w_gu, ffn_w_down, w_o, mem_norm, mem_w_kv, ret_w_in,
    ret_log_decay, ret_head_norm, mla_w_in, mla_q_norm, mla_kv_norm, mla_w_uq, mla_w_ukv,
    norm_g_2, ffn_w_gate_2, ffn_w_up_2, ffn_w_down_2, w_in_2, conv_w_2, pool_w_2, pool_scale_2,
    w_out_2,
):
    x = first_block(
        x, mem, positions, norm_gains, ffn_w_gu, ffn_w_down, w_o, mem_norm, mem_w_kv, ret_w_in,
        ret_log_decay, ret_head_norm, mla_w_in, mla_q_norm, mla_kv_norm, mla_w_uq, mla_w_ukv,
    )
    return second_block(
        x, norm_g_2, ffn_w_gate_2, ffn_w_up_2, ffn_w_down_2, w_in_2, conv_w_2, pool_w_2,
        pool_scale_2, w_out_2,
    )


_drawn_inputs = setup_inputs


def setup_inputs(seed=0):
    import zlib

    import numpy as np

    out = dict(_drawn_inputs(seed))
    spreads = {}
    factors = {'mem_norm': 6.028,
     'ret_head_norm': 7.554,
     'mla_q_norm': 4.536,
     'mla_kv_norm': 3.075,
     'pool_scale_2': 3.431}
    for name, (base, spread) in spreads.items():
        noise = np.random.default_rng([zlib.crc32(name.encode()), seed]).standard_normal(out[name].shape)
        drawn = base * np.exp(spread * noise) if base else spread * noise
        out[name] = __import__('jax').numpy.asarray(drawn.astype(out[name].dtype))
    for name, factor in factors.items():
        out[name] = (out[name] * factor).astype(out[name].dtype)
    return out
```

```python
import math
from contextlib import ExitStack

import numpy as np

import concourse.bass as bass
from concourse import mybir

P = 128
S = 256
T = S // P
D = 1024
KD = D // P
FF = 2816
SLOT = 2048
SC = SLOT // KD
RING = 3
CHUNKS = FF // SC
EPS = 1e-6
HEADS_R, HEADS_M, NOPE, ROPE, DV = 6, 6, 64, 32, 128
QR, KVR = 256, 128
QKW = NOPE + ROPE
MH, MD = 4, 64
TOK = 768
AH, AD = 8, 64
CAUSAL = 384
WINDOWS = (2, 4, 8, 16)
N_MEM, N_FFN, N_RET, N_MLA, N_STICK, N_WO = 4, 3 * CHUNKS, 13, 5, 10, 4
SUBLAYERS = ("ffn", "ret", "ffn", "ffn", "mla", "ffn", "ffn", "stick", "ffn", "ffn", "stick", "ffn")
SLOTS_OF = {"ffn": N_FFN, "ret": N_RET + N_WO, "mla": N_MLA + N_WO, "stick": N_STICK + N_WO}

CONST = {}
_at = 0
for _name, _width in (("ident", P), ("tri", P), ("ones", P),
                      ("negmask", CAUSAL), ("addmask", CAUSAL), ("poolrc", 2 * S), ("minhalf", 16),
                      ("invret", 1), ("sign", 1), ("invmla", 16),
                      ("fwd", 2 * S), ("bwd", 2 * S)):
    CONST[_name] = (_at, _at + _width)
    _at += _width
N_CONST = _at
KEPT = CONST["fwd"][0]
BIG = 11264


def constants():
    c = np.zeros((P, N_CONST), np.float32)

    def put(name, value):
        a, b = CONST[name]
        c[:, a:b] = np.asarray(value, np.float32).reshape(P, b - a)

    p = np.arange(P)[:, None]
    put("ident", np.eye(P))
    s = p[:, :, None] + P * np.arange(2)[None, :, None]
    t = np.arange(S)[None, None, :]
    put("fwd", np.maximum(t - s, 0))
    put("bwd", np.maximum(s - t, 0))
    put("tri", p >= np.arange(P)[None, :])
    put("ones", np.ones((P, P)))
    diag = p < np.arange(P)[None, :]
    live = np.concatenate([diag, np.ones((P, P), bool), diag], axis=1)
    put("negmask", np.where(live, -1.0, 0.0))
    put("addmask", np.where(live, 0.0, -1e30))
    group = (p[:, :, None] + P * np.arange(2)[None, :, None]) // 64
    put("poolrc", 1.0 / np.minimum(t + 1, np.array(WINDOWS)[group]))
    put("minhalf", np.full((P, 16), -0.5))
    inv = lambda dim: (1.0 / (np.float32(10000.0) ** (np.arange(0, dim, 2, dtype=np.float32) / dim))).astype(np.float32)
    put("invret", inv(P)[np.arange(P) % 64])
    put("sign", np.where(np.arange(P) < 64, -1.0, 1.0))
    put("invmla", np.tile(inv(ROPE), (P, 1)))
    return c


def build(nc, ins, out):
    f32, f32r, i32 = mybir.dt.float32, mybir.dt.float32r, mybir.dt.int32
    ACT, ALU, AX = mybir.ActivationFunctionType, mybir.AluOpType, mybir.AxisListType
    ctx = ExitStack()
    with ctx:
        sb = lambda name, shape, dt=f32: ctx.enter_context(nc.sbuf_tensor(name, shape, dt))
        ps = lambda name, n: ctx.enter_context(nc.psum_tensor(name, [P, n], f32))
        sem = lambda name: ctx.enter_context(nc.semaphore(name))

        raw = sb("raw", [P, RING, SLOT])
        w_hi = sb("w_hi", [P, RING, SLOT], f32r)
        w_lo = sb("w_lo", [P, RING, SLOT], f32r)
        x = sb("x", [P, T, D])
        xn = sb("xn", [P, T, D])
        h_hi = sb("h_hi", [P, KD, S], f32r)
        h_lo = sb("h_lo", [P, KD, S], f32r)
        m_hi = sb("m_hi", [P, KD, S], f32r)
        m_lo = sb("m_lo", [P, KD, S], f32r)
        act_hi, act_lo = m_hi[:, 0:2, :], m_lo[:, 0:2, :]
        junk = sb("junk", [P, D], mybir.dt.bfloat16)
        upd = sb("upd", [P, D])
        pre_gain = sb("pre_gain", [P, D])
        post_gain = sb("post_gain", [P, D])
        stat = sb("stat", [P, 32])
        const = sb("const", [P, KEPT])
        mk_T = sb("mk_T", [P, 2, 2, S])
        mv = sb("mv", [P, 2, 2, S])
        nat = xn
        pos_row = sb("pos_row", [P, S], i32)
        pos_col = sb("pos_col", [P, T], i32)
        trig = sb("trig", [P, 2, S + 2 * 16])
        lgd = sb("lgd", [P, 2 * HEADS_R])
        big = sb("big", [P, BIG])

        cst = lambda name: const[:, CONST[name][0]:CONST[name][1]]
        ident = cst("ident")

        class Area:
            def __init__(self):
                self.at = 0

            def take(self, *shape):
                n = int(np.prod(shape))
                v = big[:, self.at:self.at + n]
                self.at += n
                assert self.at <= BIG
                if len(shape) == 2:
                    v = v.rearrange("p (a b) -> p a b", a=shape[0])
                if len(shape) == 3:
                    v = v.rearrange("p (a b c) -> p a b c", a=shape[0], b=shape[1])
                return v

        ar = Area()
        decay = ar.take(HEADS_R, 2 * S)
        r_q, r_k = ar.take(HEADS_R, S), ar.take(HEADS_R, S)
        r_v, r_g = ar.take(T, TOK), ar.take(T, TOK)
        r_sc = ar.take(2, 2 * S)
        ar_soft = ar.at
        qm_T = ar.take(2, S)
        prob = r_sc[:, 0, :].rearrange("p (a b) -> p a b", a=2)
        af = Area()
        af.take(HEADS_R, 2 * S)
        silu_g, act = af.take(2 * S), af.take(2 * S)
        mem_rows = af.take(T, D)
        ang = af.take(4, S + 2 * 16)
        posf = af.take(S + T)
        offsets = af.take(2, 2 * S)
        am = Area()
        q_nat = am.take(T, HEADS_M * QKW)
        kv_nat = am.take(T, HEADS_M * (NOPE + DV))
        k_nat = am.take(T, HEADS_M * QKW)
        mq_T, mk2_T = am.take(HEADS_M, S), am.take(HEADS_M, S)
        c_nat = am.take(T, QR + KVR)
        kr = am.take(T, ROPE)
        rt = am.take(4, HEADS_M * 16)
        assert am.at <= ar_soft
        prob_T = upd[:, 0:2 * S].rearrange("p (a b) -> p a b", a=2)
        as_ = Area()
        s_q, s_k = as_.take(4, S), as_.take(4, S)
        s_v = as_.take(T, AH * AD)
        gate_b, gate_c, conv_h, pool_p = (as_.take(2, S) for _ in range(4))
        z_abs = as_.take(2, CAUSAL)
        z_ln = as_.take(2, CAUSAL)
        z_lk = as_.take(2, CAUSAL)
        z_a = as_.take(2, CAUSAL)
        conv_u, conv_y = as_.take(2, S), as_.take(2, S)
        pool_a, pool_b, pool_c, pool_e = (as_.take(2, S) for _ in range(4))
        small = sb("small", [P, 2, 8])
        pool_w = sb("pool_w", [P, 2, P])
        c_gain = sb("c_gain", [P, QR + KVR])
        rope_sw = sb("rope_sw", [P, 2 * S])
        rope_t = sb("rope_t", [P, 2 * S])
        bn = sb("bn", [P, 2 * HEADS_R, 6])
        mean_var = sb("mean_var", [P, 2 * HEADS_R, 2])
        r_rs = sb("r_rs", [P, 2 * HEADS_R])
        sm = sb("sm", [P, 2, 8])
        c_hi, c_lo = h_hi[:, 0:3, :], h_lo[:, 0:3, :]
        hgain = sb("hgain", [P, TOK])

        bank0, bank1 = ps("bank0", 512), ps("bank1", 512)
        down = [ps("down0", 1024), ps("down1", 1024)]
        bank6, bank7 = ps("bank6", 512), ps("bank7", 512)
        gemm_bank = [bank0, bank1]
        mid = [down[0][:, 0:512], down[0][:, 512:1024], down[1][:, 0:512], down[1][:, 512:1024]]

        raw_in = [sem(f"raw_in{r}") for r in range(RING)]
        hi_ready, lo_ready = sem("hi_ready"), sem("lo_ready")
        slot_done = sem("slot_done")
        silu_done, prod_done = sem("silu_done"), sem("prod_done")
        act_hi_done, act_lo_done = sem("act_hi_done"), sem("act_lo_done")
        down_done = sem("down_done")
        post_ss, post_var, post_rs, x_new = sem("post_ss"), sem("post_var"), sem("post_rs"), sem("x_new")
        pre_ss, pre_var, pre_rs, pre_xn = sem("pre_ss"), sem("pre_var"), sem("pre_rs"), sem("pre_xn")
        turned, h_hi_done, h_lo_done = sem("turned"), sem("h_hi_done"), sem("h_lo_done")
        const_in, x_in, mem_in, small_in = sem("const_in"), sem("x_in"), sem("mem_in"), sem("small_in")
        pre_in, post_in = sem("pre_in"), sem("post_in")
        out_done = sem("out_done")
        dve_link, pool_link, act_link = sem("dve_link"), sem("pool_link"), sem("act_link")
        ang_ready, trig_ready, table_ready = sem("ang_ready"), sem("trig_ready"), sem("table_ready")
        expo_ready, decay_ready = sem("expo_ready"), sem("decay_ready")
        evac = sem("evac")
        rope_swapped, rope_cos, roped = sem("rope_swapped"), sem("rope_cos"), sem("roped")
        g_scaled = sem("g_scaled")
        r_scores, r_decayed, r_out, r_copied = sem("r_scores"), sem("r_decayed"), sem("r_out"), sem("r_copied")
        r_var, r_rs_ready, r_mix = sem("r_var"), sem("r_rs_ready"), sem("r_mix")
        m_turned, m_hi_done, m_lo_done = sem("m_turned"), sem("m_hi_done"), sem("m_lo_done")
        a_scores, a_max, a_exp, a_norm = sem("a_scores"), sem("a_max"), sem("a_exp"), sem("a_norm")
        a_turned, a_probT, a_out, a_hi, a_lo = (sem(n) for n in ("a_turned", "a_probT", "a_out", "a_hi", "a_lo"))
        c_ss, c_var, c_rs, c_xn = sem("c_ss"), sem("c_var"), sem("c_rs"), sem("c_xn")
        c_turned, c_hi_done, c_lo_done = sem("c_turned"), sem("c_hi_done"), sem("c_lo_done")
        uq_mm, uq_out, ukv_mm, ukv_out = sem("uq_mm"), sem("uq_out"), sem("ukv_mm"), sem("ukv_out")
        qk_ready, qk_turned, qk_T = sem("qk_ready"), sem("qk_turned"), sem("qk_T")
        s_z, s_abs, s_ln, s_lk = sem("s_z"), sem("s_abs"), sem("s_ln"), sem("s_lk")
        s_cs, s_min, s_exp, s_out, s_hi, s_lo = (sem(n) for n in ("s_cs", "s_min", "s_exp", "s_out", "s_hi", "s_lo"))
        conv_done, conv_hi, conv_lo = sem("conv_done"), sem("conv_hi"), sem("conv_lo")
        pool_d, pool_mm, pool_hi, pool_lo = sem("pool_d"), sem("pool_mm"), sem("pool_hi"), sem("pool_lo")
        pool_w_zero = sem("pool_w_zero")

        block = ctx.enter_context(nc.Block())

        first_slot, n = [], N_MEM
        for kind in SUBLAYERS:
            first_slot.append(n)
            n += SLOTS_OF[kind]
        N_SLOTS = n
        U = len(SUBLAYERS)

        def wait(eng, s, value):
            if value > 0:
                eng.wait_ge(s, value)

        def linker(eng, s):
            count = [0]

            def link(instruction):
                count[0] += 1
                instruction.then_inc(s, 1)
                eng.wait_ge(s, count[0])
            return link

        def cols(w, c0, width):
            return w[:, c0:c0 + width].rearrange("(k p) c -> p k c", p=P)

        @block.sync
        def _(sp):
            def slot(n, src, width=SLOT, at=None):
                r = n % RING
                m = n if at is None else at
                if at is not None or n >= RING:
                    sp.wait_ge(lo_ready, m - RING + 1)
                dst = raw[:, r, 0:width]
                if len(src.shape) == 3:
                    dst = dst.rearrange("p (a b) -> p a b", a=src.shape[1])
                sp.dma_start(dst, src).then_inc(raw_in[r], 16)

            for t in range(T):
                sp.dma_start(mem_rows[:, t, :], ins["mem"][0, t * P:(t + 1) * P, :]).then_inc(mem_in, 16)
            sp.dma_start(const[:, :], ins["const"][:, 0:KEPT]).then_inc(const_in, 16)
            for j in range(3):
                w = ins["mem_w_kv"][j // 2]
                slot(j, cols(w, (j % 2) * SC, SC))
            for t in range(T):
                sp.dma_start(x[:, t, :], ins["x"][0, t * P:(t + 1) * P, :]).then_inc(x_in, 16)
            sp.dma_start(offsets, ins["const"][:, KEPT:N_CONST].rearrange("p (a b) -> p a b", a=2)).then_inc(small_in, 16)
            sp.dma_start(pos_row[:, :], ins["positions"][0, :].partition_broadcast(P)).then_inc(small_in, 16)
            sp.dma_start(pos_col[:, :], ins["positions"][0, :].rearrange("(t p) -> p t", p=P), allow_slow_non_contiguous=True).then_inc(small_in, 16)
            sp.dma_start(lgd[:, :], ins["ret_log_decay"].rearrange("a b c -> (a b c)").partition_broadcast(P)).then_inc(small_in, 16)
            sp.dma_start(hgain[:, :], ins["ret_head_norm"].rearrange("a b c -> (a b c)").partition_broadcast(P)).then_inc(small_in, 16)
            sp.dma_start(c_gain[:, 0:QR], ins["mla_q_norm"][0, :].partition_broadcast(P)).then_inc(small_in, 16)
            sp.dma_start(c_gain[:, QR:QR + KVR], ins["mla_kv_norm"][0, :].partition_broadcast(P)).then_inc(small_in, 16)
            slot(3, cols(ins["mem_w_kv"][1], SC, SC))

            stick = 0
            for u, kind in enumerate(SUBLAYERS):
                b = first_slot[u]
                l = u // 3
                if kind == "ffn":
                    f = (u % 3) // 2
                    if l < 2:
                        gu = ins["ffn_w_gu"][l, f]
                        wg, wu, wd = gu[:, 0:FF], gu[:, FF:2 * FF], ins["ffn_w_down"][l, f]
                    else:
                        wg, wu, wd = ins["ffn_w_gate_2"][l - 2, f], ins["ffn_w_up_2"][l - 2, f], ins["ffn_w_down_2"][l - 2, f]
                    wgv = wg.rearrange("(k p) c -> p k c", p=P)
                    wuv = wu.rearrange("(k p) c -> p k c", p=P)
                    wdv = wd.rearrange("(i j p) c -> p i j c", j=2, p=P)
                    slot(b, wgv[:, :, 0:SC])
                    slot(b + 1, wuv[:, :, 0:SC])
                    with sp.Fori(0, CHUNKS - 1) as i:
                        slot(b + 2, wgv[:, :, bass.ds((i + 1) * SC, SC)], at=b + 2 + 3 * i)
                        slot(b + 3, wdv[:, bass.ds(i, 1), :, :].rearrange("p a j c -> p (a j) c"), at=b + 3 + 3 * i)
                        slot(b + 4, wuv[:, :, bass.ds((i + 1) * SC, SC)], at=b + 4 + 3 * i)
                    slot(b + 3 * CHUNKS - 1, wdv[:, CHUNKS - 1, :, :])
                    continue
                if kind == "ret":
                    w, wo = ins["ret_w_in"][0], ins["w_o"][l]
                    for j in range(N_RET):
                        slot(b + j, cols(w, j * SC, SC))
                    b += N_RET
                elif kind == "mla":
                    w, wo = ins["mla_w_in"][0], ins["w_o"][l]
                    slot(b, cols(w, 0, QR))
                    slot(b + 1, cols(w, QR, KVR + ROPE), KD * (KVR + ROPE))
                    slot(b + 2, cols(w, QR + KVR + ROPE, SC))
                    slot(b + 3, cols(ins["mla_w_uq"][0], 0, HEADS_M * QKW), 2 * HEADS_M * QKW)
                    slot(b + 4, ins["mla_w_ukv"][0], HEADS_M * (NOPE + DV))
                    b += N_MLA
                else:
                    w, wo = ins["w_in_2"][l - 2], ins["w_out_2"][l - 2]
                    for a in range(3):
                        if stick:
                            wait(sp, conv_done, 2 * stick)
                        sp.dma_start(small[:, :, a:a + 1], ins["conv_w_2"][l - 2, a, :].rearrange("(j p) -> p j", p=P).unsqueeze(2), allow_slow_non_contiguous=True).then_inc(small_in, 16)
                    if stick:
                        wait(sp, pool_lo, 2 * stick)
                    sp.dma_start(small[:, :, 3:4], ins["pool_scale_2"][l - 2, :].rearrange("(j p) -> p j", p=P).unsqueeze(2), allow_slow_non_contiguous=True).then_inc(small_in, 16)
                    sp.wait_ge(pool_w_zero, 1)
                    for g in range(4):
                        o = 64 * (g % 2)
                        sp.dma_start(pool_w[o:o + 64, g // 2, o:o + 64], ins["pool_w_2"][l - 2, g]).then_inc(small_in, 16)
                    stick += 1
                    for j in range(N_STICK):
                        slot(b + j, cols(w, j * SC, SC))
                    b += N_STICK
                wov = wo.rearrange("(i j p) c -> p i j c", j=2, p=P)
                for j in range(N_WO):
                    slot(b + j, wov[:, j, :, :])
            for t in range(T):
                sp.wait_ge(x_new, 2 * (U - 1) + t + 1)
                sp.dma_start(out[0, t * P:(t + 1) * P, :], x[:, t, :]).then_inc(out_done, 16)
            sp.wait_ge(out_done, 16 * T)

        SMALL_FIRST = 7 * 16
        SMALL_STICK = 8 * 16

        @block.tensor
        def _(pe):
            mm, tr = nc.tensor.matmul, nc.tensor.transpose

            def take(n, at=None):
                pe.wait_ge(lo_ready, (n if at is None else at) + 1)

            def gemm_cols(n, bank, at=None, hi=h_hi, lo=h_lo):
                take(n, at)
                r = n % RING
                for j in range(2):
                    o = bank[:, j * S:(j + 1) * S]
                    for k in range(KD):
                        c = k * SC + j * P
                        mm(o, w_hi[:, r, c:c + P], hi[:, k, :], start=(k == 0), stop=False)
                        mm(o, w_hi[:, r, c:c + P], lo[:, k, :], start=False, stop=False)
                        last = mm(o, w_lo[:, r, c:c + P], hi[:, k, :], start=False, stop=(k == KD - 1))
                last.then_inc(slot_done, 1)

            def gemm_rows_into(n, o, t, k_tiles, width, c0, n_cols, hi, lo):
                r = n % RING
                for i, k in enumerate(k_tiles):
                    c = i * width + c0
                    ts = slice(t * P, (t + 1) * P)
                    first, end = i == 0, i == len(k_tiles) - 1
                    mm(o, hi[:, k, ts], w_hi[:, r, c:c + n_cols], start=first, stop=False)
                    mm(o, hi[:, k, ts], w_lo[:, r, c:c + n_cols], start=False, stop=False)
                    last = mm(o, lo[:, k, ts], w_hi[:, r, c:c + n_cols], start=False, stop=end)
                return last

            def gemm_rows(n, bank, width=SC):
                take(n)
                for t in range(T):
                    last = gemm_rows_into(n, bank[:, t * S:t * S + width], t, range(KD), width, 0, width, h_hi, h_lo)
                last.then_inc(slot_done, 1)

            def gemm_down(n, k0, hi, lo, first, last_one, at=None):
                take(n, at)
                r = n % RING
                for t in range(T):
                    ts = slice(t * P, (t + 1) * P)
                    for j in range(2):
                        end = last_one and j == 1
                        for part, (a, w) in enumerate(((hi, w_hi), (hi, w_lo), (lo, w_hi))):
                            for c in range(2):
                                last = mm(down[t][:, c * 512:(c + 1) * 512], a[:, k0 + j, ts],
                                          w[:, r, j * D + c * 512:j * D + (c + 1) * 512],
                                          start=(first and j == 0 and part == 0), stop=(end and part == 2))
                    if last_one and t == 0:
                        last.then_inc(down_done, 1)
                last.then_inc(slot_done, 1)

            def turn(p):
                for t in range(T):
                    pe.wait_ge(pre_xn, 2 * p + t + 1)
                    banks = (bank6, bank7) if t == 0 else (bank0, bank1)
                    for k in range(KD):
                        last = tr(banks[k // 4][:, (k % 4) * P:(k % 4 + 1) * P], xn[:, t, k * P:(k + 1) * P], ident)
                    last.then_inc(turned, 1)
                pe.wait_ge(h_lo_done, 4 * (p + 1))

            def soft_scores(a, heads_q, heads_k):
                bank = mid[a % 2]
                for t in range(T):
                    last = mm(bank[:, t * S:(t + 1) * S], heads_q[:, t * P:(t + 1) * P], heads_k, start=True, stop=True)
                last.then_inc(a_scores, 1)

            def soft_turn(a):
                pe.wait_ge(a_norm, a + 1)
                wait(pe, a_probT, a - 1)
                for kt in range(2):
                    for t in range(T):
                        last = tr(mid[2 + a % 2][:, kt * S + t * P:kt * S + (t + 1) * P], prob[:, t, kt * P:(kt + 1) * P], ident)
                last.then_inc(a_turned, 1)

            def soft_out(a, o0, o1, value):
                pe.wait_ge(a_probT, a + 1)
                wait(pe, a_lo, a - 1)
                for kt in range(2):
                    last = mm((bank6, bank7)[a % 2][o0:o1, 0:S], value(kt), prob_T[:, kt, :], start=(kt == 0), stop=(kt == 1))
                last.then_inc(a_out, 1)

            def soft(heads):
                for a, q, k, v, o in heads:
                    soft_scores(a, q, k)
                    soft_turn(a)
                    soft_out(a, o[0], o[1], v)

            def mem_heads(l, a0):
                for h in range(MH):
                    o = 64 * (h % 2)
                    yield (a0 + h, qm_T[o:o + 64, h // 2, :], mk_T[o:o + 64, l, h // 2, :],
                           lambda kt, h=h: mv[:, l, kt, h * MD:(h + 1) * MD], (o, o + 64))

            evacs = [0]

            def next_bank():
                e = evacs[0]
                evacs[0] += 1
                wait(pe, evac, e - 1)
                return gemm_bank[e % 2]

            pe.wait_ge(const_in, 16)
            turn(0)
            for l in range(2):
                gemm_cols(2 * l, next_bank())
                gemm_rows(2 * l + 1, next_bank())
            pe.wait_ge(evac, evacs[0])

            downs = [0]
            ffns, sticks = 0, 0
            for u, kind in enumerate(SUBLAYERS):
                b = first_slot[u]
                turn(u + 1)
                if kind == "ffn":
                    e = CHUNKS * ffns
                    gemm_cols(b, bank0)
                    gemm_cols(b + 1, bank1)

                    def down_chunk(n, i, first, last_one, at=None):
                        pe.wait_ge(act_lo_done, e + i + 1)
                        gemm_down(n, 0, act_hi, act_lo, first, last_one, at)

                    pe.wait_ge(silu_done, e + 1)
                    gemm_cols(b + 2, bank0)
                    down_chunk(b + 3, 0, True, False)
                    gemm_cols(b + 4, bank1)
                    with pe.Fori(1, CHUNKS - 1) as i:
                        n = b + 2 + 3 * i
                        pe.wait_ge(silu_done, e + 1 + i)
                        gemm_cols(b + 2, bank0, at=n)
                        down_chunk(b + 3, i, False, False, at=n + 1)
                        gemm_cols(b + 4, bank1, at=n + 2)
                    down_chunk(b + 3 * CHUNKS - 1, CHUNKS - 1, False, True)
                    ffns += 1
                    continue
                if kind == "ret":
                    for j in range(N_RET):
                        if 2 <= j < 8:
                            pe.wait_ge(rope_cos, j - 1)
                        (gemm_rows if 6 <= j < 12 else gemm_cols)(b + j, next_bank())
                    pe.wait_ge(roped, 6)
                    pe.wait_ge(evac, evacs[0])
                    for h in range(HEADS_R + 1):
                        if h < HEADS_R:
                            wait(pe, r_decayed, h - 1)
                            for s in range(2):
                                last = mm(mid[h % 2][:, s * S:(s + 1) * S], r_k[:, h, s * P:(s + 1) * P], r_q[:, h, :], start=True, stop=True)
                            last.then_inc(r_scores, 1)
                        if h:
                            g = h - 1
                            pe.wait_ge(r_decayed, g + 1)
                            wait(pe, r_copied, g - 1)
                            for t in range(T):
                                for s in range(2):
                                    last = mm(mid[2 + g % 2][:, t * P:(t + 1) * P], r_sc[:, g % 2, s * S + t * P:s * S + (t + 1) * P],
                                              r_v[:, s, g * DV:(g + 1) * DV], start=(s == 0), stop=(s == 1))
                            last.then_inc(r_out, 1)
                    pe.wait_ge(r_copied, HEADS_R)
                    pe.wait_ge(r_mix, 2)
                    for t in range(T):
                        banks = (bank6, bank7) if t == 0 else (bank0, bank1)
                        for k in range(HEADS_R):
                            last = tr(banks[k // 4][:, (k % 4) * P:(k % 4 + 1) * P], nat[:, t, k * P:(k + 1) * P], ident)
                        last.then_inc(m_turned, 1)
                    pe.wait_ge(m_lo_done, 4)
                    soft(mem_heads(0, 0))
                    pe.wait_ge(a_lo, MH)
                    b += N_RET
                elif kind == "mla":
                    gemm_rows(b, next_bank())
                    gemm_rows(b + 1, next_bank(), KVR + ROPE)
                    gemm_cols(b + 2, next_bank())
                    pe.wait_ge(c_xn, 2)
                    for t in range(T):
                        for k in range(3):
                            bank, kk = (bank6, k) if k < 2 else (bank7, 0)
                            last = tr(bank[:, kk * S + t * P:kk * S + (t + 1) * P], c_nat[:, t, k * P:(k + 1) * P], ident)
                    last.then_inc(c_turned, 1)
                    pe.wait_ge(c_lo_done, 2)
                    take(b + 3)
                    half = HEADS_M * QKW // 2
                    for t in range(T):
                        for c in range(2):
                            last = gemm_rows_into(b + 3, mid[2 * t + c][:, 0:half], t, range(2), 2 * half, c * half, half, c_hi, c_lo)
                    last.then_inc(slot_done, 1)
                    pe.wait_ge(uq_out, 4)
                    pe.wait_ge(evac, evacs[0])
                    take(b + 4)
                    third = HEADS_M * (NOPE + DV) // 3
                    for t in range(T):
                        for c in range(3):
                            bank = (mid + [bank0, bank1])[3 * t + c]
                            last = gemm_rows_into(b + 4, bank[:, 0:third], t, (2,), 3 * third, c * third, third, c_hi, c_lo)
                    last.then_inc(slot_done, 1)
                    pe.wait_ge(ukv_out, 6)
                    pe.wait_ge(qk_ready, 2)
                    for i in range(6):
                        src = q_nat if i < 3 else k_nat
                        bank = (mid + [bank6, bank7])[i]
                        for g in range(2):
                            h = 2 * (i % 3) + g
                            for t in range(T):
                                last = tr(bank[0:QKW, g * S + t * P:g * S + (t + 1) * P], src[:, t, h * QKW:(h + 1) * QKW], ident)
                        last.then_inc(qk_turned, 1)
                    pe.wait_ge(qk_T, 6)
                    tok_heads = [(MH + h, mq_T[0:QKW, h, :], mk2_T[0:QKW, h, :],
                                  lambda kt, h=h: kv_nat[:, kt, h * (NOPE + DV) + NOPE:(h + 1) * (NOPE + DV)], (0, P))
                                 for h in range(HEADS_M)]
                    soft(tok_heads + list(mem_heads(1, MH + HEADS_M)))
                    pe.wait_ge(a_lo, 2 * MH + HEADS_M)
                    b += N_MLA
                else:
                    c0 = 4 * sticks

                    def logits(s, banks, start, stop):
                        for g in range(2):
                            o = 64 * g
                            k, q = s_k[o:o + 64, s, :], s_q[o:o + 64, s, :]
                            yield g, 0, mm(banks[g][:, 0:S], k[:, 0:P], q, start=start, stop=stop)
                            yield g, 1, mm(banks[g][:, S:CAUSAL], k[:, P:S], q[:, P:S], start=start, stop=stop)

                    def pair_logits(s):
                        for _, _, last in logits(s, mid[0:2], True, True):
                            pass
                        last.then_inc(s_z, 1)

                    def pair_sums(s):
                        pe.wait_ge(s_lk, c0 + s + 1)
                        wait(pe, s_min, c0 + s)
                        tri, ones = cst("tri"), cst("ones")
                        for g in range(2):
                            o = 64 * g
                            k, q = s_k[o:o + 64, s, :], s_q[o:o + 64, s, :]
                            lk = z_lk[:, g, :]
                            first, second = mid[2 + g][:, 0:S], mid[2 + g][:, S:CAUSAL]
                            mm(first, k[:, 0:P], q, start=True, stop=False)
                            mm(first, tri, lk[:, 0:S], start=False, stop=False)
                            mm(mid[2 + g][:, P:S], ones, lk[:, S:CAUSAL], start=False, stop=True)
                            mm(second, k[:, P:S], q[:, P:S], start=True, stop=False)
                            last = mm(second, tri, lk[:, S:CAUSAL], start=False, stop=True)
                        last.then_inc(s_cs, 1)

                    def pair_out(s):
                        pe.wait_ge(s_exp, c0 + s + 1)
                        wait(pe, s_lo, c0 + s - 1)
                        bank = (bank6, bank7)[s % 2]
                        for g in range(2):
                            h = 2 * s + g
                            o = slice(64 * g, 64 * g + 64)
                            mm(bank[o, 0:S], s_v[:, 0, h * AD:(h + 1) * AD], z_a[:, g, 0:S], start=True, stop=False)
                            last = mm(bank[o, P:S], s_v[:, 1, h * AD:(h + 1) * AD], z_a[:, g, S:CAUSAL], start=False, stop=True)
                        last.then_inc(s_out, 1)

                    for j in range(6):
                        (gemm_rows if j >= 4 else gemm_cols)(b + j, next_bank())
                    pe.wait_ge(evac, evacs[0])
                    for s in range(4):
                        pair_logits(s)
                        gemm_cols(b + 6 + s, next_bank())
                        if s:
                            pair_out(s - 1)
                        pair_sums(s)
                    pair_out(3)
                    pe.wait_ge(s_lo, c0 + 4)
                    pe.wait_ge(evac, evacs[0])
                    pe.wait_ge(pool_d, sticks + 1)
                    pe.wait_ge(small_in, SMALL_FIRST + SMALL_STICK * (sticks + 1))
                    for j in range(2):
                        last = mm(bank0[:, j * S:(j + 1) * S], pool_w[:, j, :], pool_e[:, j, :], start=True, stop=True)
                    last.then_inc(pool_mm, 1)
                    pe.wait_ge(pool_lo, 2 * (sticks + 1))
                    pe.wait_ge(conv_lo, sticks + 1)
                    sticks += 1
                    b += N_STICK
                for j in range(N_WO):
                    gemm_down(b + j, 2 * j, m_hi, m_lo, j == 0, j == N_WO - 1)

        @block.scalar
        def _(sc):
            act_fn = nc.scalar.activation
            link = linker(sc, act_link)

            last_square = [None, 0]

            def square_sum(src, dst, s):
                if last_square[0] is not None:
                    sc.wait_ge(last_square[0], last_square[1])
                act_fn(junk[:, 0:src.shape[1]], src, ACT.Square, accum_out=dst).then_inc(s, 1)
                squares[s] = squares.get(s, 0) + 1
                last_square[:] = [s, squares[s]]

            squares = {}

            def high(n, at=None, base=None):
                m = n if at is None else at
                if at is None:
                    sc.wait_ge(raw_in[n % RING], 16 * (n // RING + 1))
                    wait(sc, slot_done, n - RING + 1)
                else:
                    i, n0 = base
                    sc.wait_ge(raw_in[n0 % RING], i * 16 + 16 * (n0 // RING + 1))
                    sc.wait_ge(slot_done, m - RING + 1)
                r = n % RING
                act_fn(w_hi[:, r, :], raw[:, r, :], ACT.Copy).then_inc(hi_ready, 1)

            def pre_norm(p):
                src = mem_rows if p == 0 else x
                for t in range(T):
                    if p == 0:
                        sc.wait_ge(mem_in, 16 * T)
                    elif p == 1:
                        sc.wait_ge(x_in, 16 * T)
                    else:
                        sc.wait_ge(x_new, 2 * (p - 2) + t + 1)
                    square_sum(src[:, t, :], stat[:, t:t + 1], pre_ss)
                for t in range(T):
                    sc.wait_ge(turned, 2 * p + t + 1)
                    banks = (bank6, bank7) if t == 0 else (bank0, bank1)
                    for c in range(2):
                        act_fn(h_hi[:, 4 * c:4 * c + 4, t * P:(t + 1) * P],
                               banks[c][:, :].rearrange("p (k t) -> p k t", k=4), ACT.Copy).then_inc(h_hi_done, 1)

            def post_norm(u):
                for t in range(T):
                    if t == 0:
                        sc.wait_ge(down_done, u + 1)
                    else:
                        sc.wait_ge(slot_done, first_slot[u] + SLOTS_OF[SUBLAYERS[u]])
                    square_sum(down[t][:, :], stat[:, 8 + t:9 + t], post_ss)

            evacs = [0]

            def copy_out(n, dst, func=ACT.Copy, scale=1.0, width=SC):
                sc.wait_ge(slot_done, n + 1)
                src = gemm_bank[evacs[0] % 2][:, :].rearrange("p (a b) -> p a b", a=2)[:, :, 0:width]
                act_fn(dst, src, func, scale=scale).then_inc(evac, 1)
                evacs[0] += 1

            def soft(heads):
                for a, scale, parts, k in heads:
                    sc.wait_ge(a_max, a + 1)
                    wait(sc, a_turned, a)
                    for t in range(T):
                        act_fn(prob[:, t, :], mid[a % 2][:, t * S:(t + 1) * S], ACT.Exp, bias=sm[:, t, 1:2],
                               scale=scale, accum_out=sm[:, t, 2:3]).then_inc(a_exp, 1)
                    sc.wait_ge(a_turned, a + 1)
                    wait(sc, a_out, a)
                    act_fn(prob_T[:, :, :], mid[2 + a % 2].rearrange("p (a b) -> p a b", a=2), ACT.Copy).then_inc(a_probT, 1)
                    sc.wait_ge(a_out, a + 1)
                    act_fn(m_hi[parts, k, :], (bank6, bank7)[a % 2][parts, 0:S], ACT.Copy).then_inc(a_hi, 1)

            def mem_heads(a0):
                return [(a0 + h, 1.0, slice(64 * (h % 2), 64 * (h % 2) + 64), 6 + h // 2) for h in range(MH)]

            for n in range(RING):
                high(n)
            pre_norm(0)
            for l in range(2):
                copy_out(2 * l, mk_T[:, l, :, :])
                high(2 * l + 3)
                copy_out(2 * l + 1, mv[:, l, :, :])
                if l == 0:
                    high(4)
            sc.wait_ge(ang_ready, 1)
            act_fn(trig[:, 0, :], ang[:, 3, :], ACT.Sin).then_inc(trig_ready, 1)
            act_fn(trig[:, 1, :], ang[:, 2, :], ACT.Sin).then_inc(trig_ready, 1)
            sc.wait_ge(expo_ready, HEADS_R)
            act_fn(decay, decay, ACT.Exp).then_inc(decay_ready, 1)
            pre_norm(1)
            high(N_MEM + 2)

            ffns, sticks = 0, 0
            for u, kind in enumerate(SUBLAYERS):
                b = first_slot[u]
                if kind == "ffn":
                    e = CHUNKS * ffns
                    sc.wait_ge(slot_done, b + 1)
                    act_fn(silu_g, bank0[:, :], ACT.Silu).then_inc(silu_done, 1)
                    high(b + 3)
                    sc.wait_ge(prod_done, e + 1)
                    act_fn(act_hi, act.rearrange("p (a b) -> p a b", a=2), ACT.Copy).then_inc(act_hi_done, 1)
                    high(b + 4)

                    def chunk(i, split):
                        sc.wait_ge(slot_done, b + 3 + 3 * i)
                        act_fn(silu_g, bank0[:, :], ACT.Silu).then_inc(silu_done, 1)
                        split(5)
                        split(6)
                        sc.wait_ge(prod_done, e + 2 + i)
                        act_fn(act_hi, act.rearrange("p (a b) -> p a b", a=2), ACT.Copy).then_inc(act_hi_done, 1)
                        split(7)

                    with sc.Fori(0, CHUNKS - 2) as i:
                        chunk(i, lambda j: high(b + j, b + j + 3 * i, (i, b + j)))
                    i = CHUNKS - 2
                    chunk(i, lambda j: high(b + j + 3 * i) if b + j + 3 * i < N_SLOTS else None)
                    b += N_FFN
                    ffns += 1
                else:
                    if kind == "ret":
                        for j in range(N_RET):
                            if j < 6:
                                sc.wait_ge(slot_done, b + j + 1)
                                wait(sc, roped, j)
                                bank = gemm_bank[evacs[0] % 2]
                                act_fn(rope_sw[0:64, :], bank[64:P, :], ACT.Copy).then_inc(rope_swapped, 1)
                                act_fn(rope_sw[64:P, :], bank[0:64, :], ACT.Copy).then_inc(evac, 1)
                                evacs[0] += 1
                            elif j < 9:
                                copy_out(b + j, r_v[:, :, (j - 6) * SC:(j - 5) * SC])
                            elif j < 12:
                                copy_out(b + j, r_g[:, :, (j - 9) * SC:(j - 8) * SC], ACT.Silu)
                            else:
                                copy_out(b + j, qm_T, scale=MD ** -0.5)
                            high(b + j + 3)
                        for h in range(HEADS_R):
                            sc.wait_ge(r_out, h + 1)
                            act_fn(nat[:, :, h * DV:(h + 1) * DV], mid[2 + h % 2][:, 0:2 * P].rearrange("p (t d) -> p t d", t=2),
                                   ACT.Copy).then_inc(r_copied, 1)
                        for t in range(T):
                            sc.wait_ge(m_turned, t + 1)
                            banks = (bank6, bank7) if t == 0 else (bank0, bank1)
                            for c, n_k in ((0, 4), (1, 2)):
                                act_fn(m_hi[:, 4 * c:4 * c + n_k, t * P:(t + 1) * P],
                                       banks[c][:, 0:n_k * P].rearrange("p (k t) -> p k t", k=n_k), ACT.Copy).then_inc(m_hi_done, 1)
                        soft(mem_heads(0))
                        b += N_RET
                    elif kind == "mla":
                        copy_out(b, c_nat[:, :, 0:QR])
                        high(b + 3)
                        sc.wait_ge(slot_done, b + 2)
                        src = gemm_bank[evacs[0] % 2][:, :].rearrange("p (a b) -> p a b", a=2)
                        link(act_fn(c_nat[:, :, QR:QR + KVR], src[:, :, 0:KVR], ACT.Copy))
                        act_fn(kr, src[:, :, KVR:KVR + ROPE], ACT.Copy).then_inc(evac, 1)
                        evacs[0] += 1
                        sc.wait_ge(evac, evacs[0])
                        for t in range(T):
                            square_sum(c_nat[:, t, 0:QR], stat[:, 16 + t:17 + t], c_ss)
                            square_sum(c_nat[:, t, QR:QR + KVR], stat[:, 18 + t:19 + t], c_ss)
                        high(b + 4)
                        copy_out(b + 2, qm_T, scale=MD ** -0.5)
                        high(b + 5)
                        sc.wait_ge(c_turned, 1)
                        act_fn(c_hi[:, 0:2, :], bank6[:, :].rearrange("p (a b) -> p a b", a=2), ACT.Copy).then_inc(c_hi_done, 1)
                        act_fn(c_hi[:, 2, :], bank7[:, 0:S], ACT.Copy).then_inc(c_hi_done, 1)
                        half = HEADS_M * QKW // 2
                        sc.wait_ge(slot_done, b + 4)
                        for t in range(T):
                            for c in range(2):
                                act_fn(q_nat[:, t, c * half:(c + 1) * half], mid[2 * t + c][:, 0:half], ACT.Copy).then_inc(uq_out, 1)
                        high(b + 6)
                        third = HEADS_M * (NOPE + DV) // 3
                        sc.wait_ge(slot_done, b + 5)
                        for t in range(T):
                            for c in range(3):
                                act_fn(kv_nat[:, t, c * third:(c + 1) * third], (mid + [bank0, bank1])[3 * t + c][:, 0:third],
                                       ACT.Copy).then_inc(ukv_out, 1)
                        high(b + 7)
                        for i in range(6):
                            sc.wait_ge(qk_turned, i + 1)
                            dst = (mq_T if i < 3 else mk2_T)[0:QKW, 2 * (i % 3):2 * (i % 3) + 2, :]
                            act_fn(dst, (mid + [bank6, bank7])[i][0:QKW, :].rearrange("p (a b) -> p a b", a=2), ACT.Copy).then_inc(qk_T, 1)
                        soft([(MH + h, QKW ** -0.5, slice(0, P), h) for h in range(HEADS_M)] + mem_heads(MH + HEADS_M))
                        b += N_MLA
                    else:
                        c0 = 4 * sticks
                        for j in range(6):
                            if j < 2:
                                copy_out(b + j, s_q[:, 2 * j:2 * j + 2, :], scale=AD ** -0.5)
                            elif j < 4:
                                copy_out(b + j, s_k[:, 2 * j - 4:2 * j - 2, :])
                            else:
                                copy_out(b + j, s_v[:, :, (j - 4) * SC:(j - 3) * SC])
                            high(b + j + 3)

                        def pair_exp(s):
                            sc.wait_ge(s_min, c0 + s + 1)
                            wait(sc, s_out, c0 + s)
                            act_fn(z_a, z_abs, ACT.Exp).then_inc(s_exp, 1)

                        def pair_high(s):
                            sc.wait_ge(s_out, c0 + s + 1)
                            act_fn(m_hi[:, s, :], (bank6, bank7)[s % 2][:, 0:S], ACT.Copy).then_inc(s_hi, 1)

                        for s in range(4):
                            if s:
                                pair_exp(s - 1)
                            sc.wait_ge(s_z, c0 + s + 1)
                            z = down[0][:, :].rearrange("p (a b) -> p a b", a=2)[:, :, 0:CAUSAL]
                            if s:
                                sc.wait_ge(s_exp, c0 + s)
                            act_fn(z_abs, z, ACT.Abs).then_inc(s_abs, 1)
                            sc.wait_ge(s_abs, 3 * (c0 + s) + 1)
                            act_fn(z_abs, z_abs, ACT.Exp, scale=-1.0).then_inc(s_abs, 1)
                            sc.wait_ge(s_abs, 3 * (c0 + s) + 2)
                            wait(sc, s_lk, c0 + s)
                            act_fn(z_ln, z_abs, ACT.Ln, bias=1.0).then_inc(s_abs, 1)
                            copy_out(b + 6 + s, (gate_b, gate_c, conv_h, pool_p)[s])
                            if s:
                                pair_high(s - 1)
                            if s < 3:
                                high(b + 9 + s)
                        pair_exp(3)
                        high(b + 12)
                        pair_high(3)
                        sc.wait_ge(conv_done, 2 * (sticks + 1))
                        act_fn(m_hi[:, 4:6, :], conv_y, ACT.Copy).then_inc(conv_hi, 1)
                        sc.wait_ge(small_in, SMALL_FIRST + SMALL_STICK * (sticks + 1))
                        sc.wait_ge(pool_mm, sticks + 1)
                        for j in range(2):
                            act_fn(m_hi[:, 6 + j, :], bank0[:, j * S:(j + 1) * S], ACT.Copy, scale=small[:, j, 3:4]).then_inc(pool_hi, 1)
                        sticks += 1
                        b += N_STICK
                    for j in range(N_WO - 1):
                        high(b + j + 3)
                    b += N_WO
                post_norm(u)
                if u + 1 < U:
                    pre_norm(u + 2)
                    high(b + 2)

        @block.vector
        def _(ve):
            v = nc.vector
            link = linker(ve, dve_link)

            def low(n, at=None):
                ve.wait_ge(hi_ready, (n if at is None else at) + 1)
                r = n % RING
                v.tensor_tensor(w_lo[:, r, :], raw[:, r, :], w_hi[:, r, :].bitcast(f32), ALU.subtract).then_inc(lo_ready, 1)

            def pre_norm(p):
                src = mem_rows if p == 0 else x
                for t in range(T):
                    ve.wait_ge(pre_ss, 2 * p + t + 1)
                    v.tensor_scalar(stat[:, 2 + t:3 + t], stat[:, t:t + 1], 1.0 / D, EPS, ALU.mult, ALU.add).then_inc(pre_var, 1)
                ve.wait_ge(pre_in, 16 * (p + 1))
                for t in range(T):
                    ve.wait_ge(pre_rs, 2 * p + t + 1)
                    wait(ve, turned, 2 * (p - 1) + t + 1)
                    v.scalar_tensor_tensor(xn[:, t, :], src[:, t, :], stat[:, 4 + t:5 + t], pre_gain[:, :],
                                           ALU.mult, ALU.mult).then_inc(pre_xn, 1)
                for t in range(T):
                    banks = (bank6, bank7) if t == 0 else (bank0, bank1)
                    for c in range(2):
                        ve.wait_ge(h_hi_done, 4 * p + 2 * t + c + 1)
                        sl = (slice(None), slice(4 * c, 4 * c + 4), slice(t * P, (t + 1) * P))
                        v.tensor_tensor(h_lo[sl], banks[c][:, :].rearrange("p (k t) -> p k t", k=4),
                                        h_hi[sl].bitcast(f32), ALU.subtract).then_inc(h_lo_done, 1)

            def post_norm(u):
                half = 1.0 if u % 3 == 1 else 0.5
                for t in range(T):
                    ve.wait_ge(post_ss, 2 * u + t + 1)
                    v.tensor_scalar(stat[:, 10 + t:11 + t], stat[:, 8 + t:9 + t], 1.0 / (D * half * half), EPS / (half * half),
                                    ALU.mult, ALU.add).then_inc(post_var, 1)
                    ve.wait_ge(post_in, 16 * (u + 1))
                    ve.wait_ge(post_rs, 2 * u + t + 1)
                    link(v.scalar_tensor_tensor(upd[:, :], down[t][:, :], stat[:, 12 + t:13 + t], post_gain[:, :],
                                                ALU.mult, ALU.mult))
                    v.tensor_tensor(x[:, t, :], x[:, t, :], upd[:, :], ALU.add).then_inc(x_new, 1)

            def soft(heads):
                for a, scale, parts, k in heads:
                    ve.wait_ge(a_scores, a + 1)
                    link(v.reduce_max(sm[:, :, 0], mid[a % 2].rearrange("p (a b) -> p a b", a=2), AX.X))
                    v.tensor_scalar(sm[:, :, 1], sm[:, :, 0], -scale, None, ALU.mult).then_inc(a_max, 1)
                    ve.wait_ge(a_exp, 2 * a + 2)
                    link(v.reciprocal(sm[:, :, 3], sm[:, :, 2]))
                    for t in range(T):
                        last = v.tensor_scalar(prob[:, t, :], prob[:, t, :], sm[:, t, 3:4], None, ALU.mult)
                    last.then_inc(a_norm, 1)
                    ve.wait_ge(a_hi, a + 1)
                    v.tensor_tensor(m_lo[parts, k, :], (bank6, bank7)[a % 2][parts, 0:S], m_hi[parts, k, :].bitcast(f32),
                                    ALU.subtract).then_inc(a_lo, 1)

            def mem_heads(a0):
                return [(a0 + h, 1.0, slice(64 * (h % 2), 64 * (h % 2) + 64), 6 + h // 2) for h in range(MH)]

            for n in range(RING):
                low(n)
            pre_norm(0)
            low(3)
            low(4)
            ve.wait_ge(small_in, SMALL_FIRST)
            ve.wait_ge(const_in, 16)
            link(v.tensor_copy(posf[:, 0:S], pos_row[:, :]))
            link(v.tensor_copy(posf[:, S:S + T], pos_col[:, :]))
            a0, a1, a2, a3 = (ang[:, j, :] for j in range(4))
            link(v.tensor_scalar(a0[:, 0:S], posf[:, 0:S], cst("invret"), None, ALU.mult))
            for t in range(T):
                link(v.tensor_scalar(a0[:, S + 16 * t:S + 16 * t + 16], cst("invmla"), posf[:, S + t:S + t + 1], None, ALU.mult))
            magic = 1.5 * 2.0 ** 23
            link(v.tensor_scalar(a1, a0, 1.0 / (2.0 * math.pi), magic, ALU.mult, ALU.add))
            link(v.tensor_scalar(a1, a1, magic, None, ALU.subtract))
            turn1 = 6.28125
            turn2 = round((2.0 * math.pi - turn1) * 2.0 ** 21) / 2.0 ** 21
            turn3 = 2.0 * math.pi - turn1 - turn2
            link(v.scalar_tensor_tensor(a2, a1, -turn1, a0, ALU.mult, ALU.add))
            link(v.scalar_tensor_tensor(a0, a1, -turn2, a2, ALU.mult, ALU.add))
            link(v.scalar_tensor_tensor(a2, a1, -turn3, a0, ALU.mult, ALU.add))
            pi = float(np.nextafter(np.float32(math.pi), np.float32(0)))
            link(v.tensor_scalar(a2, a2, -pi, pi, ALU.max, ALU.min))
            link(v.tensor_scalar(a1, a2, -1.0, None, ALU.mult))
            link(v.tensor_tensor(a1, a1, a2, ALU.max))
            v.tensor_scalar(a3, a1, -1.0, math.pi / 2, ALU.mult, ALU.add).then_inc(ang_ready, 1)
            ve.wait_ge(trig_ready, 2)
            v.tensor_scalar(trig[:, 1, 0:S], trig[:, 1, 0:S], cst("sign"), None, ALU.mult).then_inc(table_ready, 1)
            low(5)
            pre_norm(1)
            low(N_MEM + 2)

            ffns, sticks = 0, 0
            for u, kind in enumerate(SUBLAYERS):
                b = first_slot[u]
                if kind == "ffn":
                    e = CHUNKS * ffns

                    def product():
                        v.tensor_tensor(act, bank1[:, :], silu_g, ALU.mult).then_inc(prod_done, 1)

                    def act_low():
                        v.tensor_tensor(act_lo, act.rearrange("p (a b) -> p a b", a=2),
                                        act_hi.bitcast(f32), ALU.subtract).then_inc(act_lo_done, 1)

                    low(b + 3)
                    ve.wait_ge(silu_done, e + 1)
                    ve.wait_ge(slot_done, b + 2)
                    product()
                    ve.wait_ge(act_hi_done, e + 1)
                    act_low()
                    low(b + 4)

                    def chunk(i, split):
                        split(5)
                        split(6)
                        ve.wait_ge(silu_done, e + 2 + i)
                        ve.wait_ge(slot_done, b + 5 + 3 * i)
                        product()
                        ve.wait_ge(act_hi_done, e + 2 + i)
                        act_low()
                        split(7)

                    with ve.Fori(0, CHUNKS - 2) as i:
                        chunk(i, lambda j: low(b + j, b + j + 3 * i))
                    i = CHUNKS - 2
                    chunk(i, lambda j: low(b + j + 3 * i) if b + j + 3 * i < N_SLOTS else None)
                    b += N_FFN
                    ffns += 1
                else:
                    if kind == "ret":
                        for j in range(N_RET):
                            if j < 6:
                                ve.wait_ge(slot_done, b + j + 1)
                                ve.wait_ge(table_ready, 1)
                                wait(ve, roped, j)
                                ve.wait_ge(rope_swapped, j + 1)
                                ve.wait_ge(evac, N_MEM + j + 1)
                                v.tensor_tensor(rope_t[:, :].rearrange("p (a b) -> p a b", a=2),
                                                gemm_bank[j % 2][:, :].rearrange("p (a b) -> p a b", a=2),
                                                trig[:, 0:1, 0:S].broadcast_to([P, 2, S]), ALU.mult).then_inc(rope_cos, 1)
                            low(b + j + 3)
                        for h in range(HEADS_R + 1):
                            if h < HEADS_R:
                                ve.wait_ge(r_scores, h + 1)
                                if h == 0:
                                    ve.wait_ge(decay_ready, 1)
                                wait(ve, r_out, h - 1)
                                v.scalar_tensor_tensor(r_sc[:, h % 2, :], mid[h % 2], P ** -0.5, decay[:, h, :],
                                                       ALU.mult, ALU.mult).then_inc(r_decayed, 1)
                            if h:
                                g = h - 1
                                ve.wait_ge(r_copied, g + 1)
                                for t in range(T):
                                    link(v.bn_stats(bn[:, 2 * g + t, :], nat[:, t, g * DV:(g + 1) * DV]))
                                    last = v.bn_aggr(mean_var[:, 2 * g + t, :], bn[:, 2 * g + t, :])
                                link(last)
                        v.tensor_scalar(r_rs[:, :], mean_var[:, :, 1], EPS, None, ALU.add).then_inc(r_var, 1)
                        ve.wait_ge(r_rs_ready, 1)
                        ve.wait_ge(g_scaled, 2)
                        for t in range(T):
                            for h in range(HEADS_R):
                                i = 2 * h + t
                                y = nat[:, t, h * DV:(h + 1) * DV]
                                last = v.tensor_scalar(y, y, mean_var[:, i, 0:1], r_rs[:, i:i + 1], ALU.subtract, ALU.mult)
                            link(last)
                            v.tensor_tensor(nat[:, t, 0:TOK], nat[:, t, 0:TOK], r_g[:, t, :], ALU.mult).then_inc(r_mix, 1)
                        for t in range(T):
                            banks = (bank6, bank7) if t == 0 else (bank0, bank1)
                            for c, n_k in ((0, 4), (1, 2)):
                                ve.wait_ge(m_hi_done, 2 * t + c + 1)
                                sl = (slice(None), slice(4 * c, 4 * c + n_k), slice(t * P, (t + 1) * P))
                                v.tensor_tensor(m_lo[sl], banks[c][:, 0:n_k * P].rearrange("p (k t) -> p k t", k=n_k),
                                                m_hi[sl].bitcast(f32), ALU.subtract).then_inc(m_lo_done, 1)
                        soft(mem_heads(0))
                        b += N_RET
                    elif kind == "mla":
                        low(b + 3)
                        ve.wait_ge(c_ss, 4)
                        link(v.tensor_scalar(stat[:, 20:22], stat[:, 16:18], 1.0 / QR, EPS, ALU.mult, ALU.add))
                        v.tensor_scalar(stat[:, 22:24], stat[:, 18:20], 1.0 / KVR, EPS, ALU.mult, ALU.add).then_inc(c_var, 1)
                        ve.wait_ge(c_rs, 1)
                        for t in range(T):
                            v.scalar_tensor_tensor(c_nat[:, t, 0:QR], c_nat[:, t, 0:QR], stat[:, 24 + t:25 + t], c_gain[:, 0:QR], ALU.mult, ALU.mult)
                            last = v.scalar_tensor_tensor(c_nat[:, t, QR:QR + KVR], c_nat[:, t, QR:QR + KVR], stat[:, 26 + t:27 + t],
                                                          c_gain[:, QR:QR + KVR], ALU.mult, ALU.mult)
                            last.then_inc(c_xn, 1)
                        low(b + 4)
                        low(b + 5)
                        ve.wait_ge(c_hi_done, 1)
                        v.tensor_tensor(c_lo[:, 0:2, :], bank6[:, :].rearrange("p (a b) -> p a b", a=2), c_hi[:, 0:2, :].bitcast(f32), ALU.subtract).then_inc(c_lo_done, 1)
                        ve.wait_ge(c_hi_done, 2)
                        v.tensor_tensor(c_lo[:, 2, :], bank7[:, 0:S], c_hi[:, 2, :].bitcast(f32), ALU.subtract).then_inc(c_lo_done, 1)

                        def rotate(x1, x2, t, heads):
                            n = heads * 16
                            tmp = [rt[:, j, 0:n].rearrange("p (a b) -> p a b", a=heads) for j in range(4)]
                            at = S + 16 * t
                            c = trig[:, 0:1, at:at + 16].broadcast_to([P, heads, 16])
                            s = trig[:, 1:2, at:at + 16].broadcast_to([P, heads, 16])
                            v.tensor_tensor(tmp[0], x1, c, ALU.mult)
                            v.tensor_tensor(tmp[1], x2, s, ALU.mult)
                            v.tensor_tensor(tmp[2], x1, s, ALU.mult)
                            link(v.tensor_tensor(tmp[3], x2, c, ALU.mult))
                            v.tensor_tensor(x1, tmp[0], tmp[1], ALU.subtract)
                            link(v.tensor_tensor(x2, tmp[2], tmp[3], ALU.add))

                        for t in range(T):
                            rotate(kr[:, t:t + 1, 0:16], kr[:, t:t + 1, 16:32], t, 1)
                        ve.wait_ge(uq_out, 4)
                        for t in range(T):
                            q = q_nat[:, t, :].rearrange("p (h d) -> p h d", h=HEADS_M)
                            rotate(q[:, :, NOPE:NOPE + 16], q[:, :, NOPE + 16:QKW], t, HEADS_M)
                        v.tensor_copy(k_nat[:, 0, 0:1], q_nat[:, 0, 0:1]).then_inc(qk_ready, 1)
                        low(b + 6)
                        ve.wait_ge(ukv_out, 6)
                        ve.wait_ge(qk_ready, 1)
                        for t in range(T):
                            k = k_nat[:, t, :].rearrange("p (h d) -> p h d", h=HEADS_M)
                            kv = kv_nat[:, t, :].rearrange("p (h d) -> p h d", h=HEADS_M)
                            v.tensor_copy(k[:, :, 0:NOPE], kv[:, :, 0:NOPE])
                            last = v.tensor_copy(k[:, :, NOPE:QKW], kr[:, t:t + 1, :].broadcast_to([P, HEADS_M, ROPE]))
                        last.then_inc(qk_ready, 1)
                        low(b + 7)
                        soft([(MH + h, QKW ** -0.5, slice(0, P), h) for h in range(HEADS_M)] + mem_heads(MH + HEADS_M))
                        b += N_MLA
                    else:
                        c0 = 4 * sticks
                        for j in range(6):
                            low(b + j + 3)

                        def pair_min(s):
                            ve.wait_ge(s_cs, c0 + s + 1)
                            cs = down[1][:, :].rearrange("p (a b) -> p a b", a=2)
                            for g in range(2):
                                last = v.scalar_tensor_tensor(z_abs[:, g, :], cs[:, g, 0:CAUSAL], 0.0, cst("addmask"), ALU.min, ALU.add)
                            last.then_inc(s_min, 1)

                        def pair_low(s):
                            ve.wait_ge(s_hi, c0 + s + 1)
                            v.tensor_tensor(m_lo[:, s, :], (bank6, bank7)[s % 2][:, 0:S], m_hi[:, s, :].bitcast(f32), ALU.subtract).then_inc(s_lo, 1)

                        for s in range(4):
                            ve.wait_ge(s_abs, 3 * (c0 + s) + 3)
                            z = down[0][:, :].rearrange("p (a b) -> p a b", a=2)
                            for g in range(2):
                                last = v.scalar_tensor_tensor(z_ln[:, g, :], z[:, g, 0:CAUSAL], 0.0, z_ln[:, g, :], ALU.max, ALU.add)
                            link(last)
                            for g in range(2):
                                last = v.tensor_tensor(z_lk[:, g, :], z_ln[:, g, :], cst("negmask"), ALU.mult)
                            last.then_inc(s_lk, 1)
                            if s:
                                pair_low(s - 1)
                            if s < 3:
                                pair_min(s)
                                low(b + 9 + s)
                        pair_min(3)
                        low(b + 12)
                        pair_low(3)
                        ve.wait_ge(evac, 4 + N_RET + 3 + 10 * sticks + 9)
                        ve.wait_ge(small_in, SMALL_FIRST + SMALL_STICK * (sticks + 1))
                        link(v.tensor_tensor(conv_u, gate_c, conv_h, ALU.mult))
                        for j in range(2):
                            link(v.tensor_scalar(conv_y[:, j, :], conv_u[:, j, :], small[:, j, 2:3], None, ALU.mult))
                            for tap, shift in ((1, 1), (0, 2)):
                                link(v.scalar_tensor_tensor(conv_y[:, j, shift:S], conv_u[:, j, 0:S - shift], small[:, j, tap:tap + 1],
                                                            conv_y[:, j, shift:S], ALU.mult, ALU.add))
                            v.tensor_tensor(conv_y[:, j, :], conv_y[:, j, :], gate_b[:, j, :], ALU.mult).then_inc(conv_done, 1)
                        ve.wait_ge(conv_hi, sticks + 1)
                        v.tensor_tensor(m_lo[:, 4:6, :], conv_y, m_hi[:, 4:6, :].bitcast(f32), ALU.subtract).then_inc(conv_lo, 1)
                        ve.wait_ge(pool_hi, 2 * (sticks + 1))
                        for j in range(2):
                            v.scalar_tensor_tensor(m_lo[:, 6 + j, :], bank0[:, j * S:(j + 1) * S], small[:, j, 3:4],
                                                   m_hi[:, 6 + j, :].bitcast(f32), ALU.mult, ALU.subtract).then_inc(pool_lo, 1)
                        sticks += 1
                        b += N_STICK
                    for j in range(N_WO - 1):
                        low(b + j + 3)
                    b += N_WO
                post_norm(u)
                if u + 1 < U:
                    pre_norm(u + 2)
                    low(b + 2)

        @block.gpsimd
        def _(gp):
            g = nc.gpsimd
            link = linker(gp, pool_link)
            half = cst("minhalf")

            def pre_norm(p):
                for t in range(T):
                    gp.wait_ge(pre_var, 2 * p + t + 1)
                    g.tensor_tensor(stat[:, 4 + t:5 + t], stat[:, 2 + t:3 + t], half[:, 0:1], ALU.pow).then_inc(pre_rs, 1)

            def post_norm(u):
                for t in range(T):
                    gp.wait_ge(post_var, 2 * u + t + 1)
                    g.tensor_tensor(stat[:, 12 + t:13 + t], stat[:, 10 + t:11 + t], half[:, 0:1], ALU.pow).then_inc(post_rs, 1)

            def load_gain(buf, s, src):
                gp.dma_start(buf[:, :], src.partition_broadcast(P)).then_inc(s, 16)

            def gain_row(u, i):
                l, f = u // 3, u % 3
                return ins["norm_gains"][l, 2 * f + i, :] if l < 2 else ins["norm_g_2"][l - 2, 2 * f + i, :]

            def load_pre_gain(p):
                wait(gp, pre_xn, 2 * p)
                load_gain(pre_gain, pre_in, gain_row(p - 1, 0) if p else ins["mem_norm"])

            def load_post_gain(u):
                wait(gp, x_new, 2 * u)
                load_gain(post_gain, post_in, gain_row(u, 1))

            load_pre_gain(0)
            gp.wait_ge(const_in, 16)
            pre_norm(0)
            load_pre_gain(1)
            gp.wait_ge(small_in, SMALL_FIRST)
            for h in range(HEADS_R):
                e = decay[:, h, :]
                g.tensor_scalar(e, offsets[:, 0, :], lgd[:, h:h + 1], None, ALU.mult)
                link(g.tensor_scalar(rope_t[:, :], offsets[:, 1, :], lgd[:, HEADS_R + h:HEADS_R + h + 1], None, ALU.mult))
                last = g.tensor_tensor(e, e, rope_t[:, :], ALU.add)
                last.then_inc(expo_ready, 1)
                gp.wait_ge(expo_ready, h + 1)
            g.memset(pool_w[:, :, :], 0.0).then_inc(pool_w_zero, 1)
            pre_norm(1)
            load_post_gain(0)
            load_pre_gain(2)
            sticks = 0
            for u, kind in enumerate(SUBLAYERS):
                if kind == "ret":
                    for j in range(6):
                        gp.wait_ge(rope_swapped, j + 1)
                        gp.wait_ge(evac, N_MEM + j + 1)
                        gp.wait_ge(table_ready, 1)
                        link(g.tensor_tensor(rope_sw[:, :].rearrange("p (a b) -> p a b", a=2), rope_sw[:, :].rearrange("p (a b) -> p a b", a=2),
                                             trig[:, 1:2, 0:S].broadcast_to([P, 2, S]), ALU.mult))
                        gp.wait_ge(rope_cos, j + 1)
                        dst = (r_q if j < 3 else r_k)[:, 2 * (j % 3):2 * (j % 3) + 2, :]
                        g.tensor_tensor(dst, rope_t[:, :].rearrange("p (a b) -> p a b", a=2),
                                        rope_sw[:, :].rearrange("p (a b) -> p a b", a=2), ALU.add).then_inc(roped, 1)
                    gp.wait_ge(evac, 4 + 12)
                    for t in range(T):
                        g.tensor_tensor(r_g[:, t, :], r_g[:, t, :], hgain[:, :], ALU.mult).then_inc(g_scaled, 1)
                    gp.wait_ge(r_var, 1)
                    g.tensor_tensor(r_rs[:, :], r_rs[:, :], half[:, 0:2 * HEADS_R], ALU.pow).then_inc(r_rs_ready, 1)
                elif kind == "mla":
                    gp.wait_ge(c_var, 1)
                    g.tensor_tensor(stat[:, 24:28], stat[:, 20:24], half[:, 0:4], ALU.pow).then_inc(c_rs, 1)
                elif kind == "stick":
                    gp.wait_ge(evac, 4 + N_RET + 3 + 10 * (sticks + 1))
                    wait(gp, pool_mm, sticks)
                    sums = [pool_p, pool_a, pool_b, pool_a, pool_b]
                    for i, w in enumerate(WINDOWS):
                        src, dst, sh = sums[i], sums[i + 1], w // 2
                        g.tensor_copy(dst[:, :, 0:sh], src[:, :, 0:sh])
                        link(g.tensor_tensor(dst[:, :, sh:S], src[:, :, sh:S], src[:, :, 0:S - sh], ALU.add))
                        o = slice(64 * (i % 2), 64 * (i % 2) + 64)
                        link(g.tensor_copy(pool_c[o, i // 2, :], dst[o, i // 2, :]))
                    link(g.tensor_tensor(pool_c, pool_c, cst("poolrc").rearrange("p (a b) -> p a b", a=2), ALU.mult))
                    g.tensor_tensor(pool_e, pool_c, pool_p, ALU.subtract).then_inc(pool_d, 1)
                    sticks += 1
                post_norm(u)
                if u + 1 < U:
                    pre_norm(u + 2)
                    load_post_gain(u + 1)
                if u + 2 < U:
                    load_pre_gain(u + 3)


NAMES = ("x", "mem", "positions", "norm_gains", "ffn_w_gu", "ffn_w_down", "w_o", "mem_norm", "mem_w_kv", "ret_w_in",
         "ret_log_decay", "ret_head_norm", "mla_w_in", "mla_q_norm", "mla_kv_norm", "mla_w_uq", "mla_w_ukv",
         "norm_g_2", "ffn_w_gate_2", "ffn_w_up_2", "ffn_w_down_2", "w_in_2", "conv_w_2", "pool_w_2", "pool_scale_2",
         "w_out_2")


def kernel(**inputs):
    import concourse.bacc as bacc
    from concourse.bass_utils import run_bass_kernel_spmd

    nc = bacc.Bacc("TRN2", target_bir_lowering=False, num_devices=1)
    arrays = {f"in_{name}": np.ascontiguousarray(inputs[name]) for name in NAMES}
    arrays["in_const"] = constants()
    ins = {key[3:]: nc.dram_tensor(key, a.shape, mybir.dt.from_np(a.dtype), kind="ExternalInput").ap()
           for key, a in arrays.items()}
    out = nc.dram_tensor("out", (1, S, D), mybir.dt.float32, kind="ExternalOutput").ap()
    build(nc, ins, out)
    return run_bass_kernel_spmd(nc, [arrays], core_ids=[0]).results[0]["out"]
```

```python
import math
from contextlib import ExitStack

import numpy as np

import concourse.bass as bass
from concourse import mybir

P = 128
S = 256
T = S // P
D = 1024
KD = D // P
FF = 2816
SLOT = 2048
SC = SLOT // KD
RING = 3
CHUNKS = FF // SC
EPS = 1e-6
HEADS_R, HEADS_M, NOPE, ROPE, DV = 6, 6, 64, 32, 128
QR, KVR = 256, 128
QKW = NOPE + ROPE
MH, MD = 4, 64
TOK = 768
AH, AD = 8, 64
CAUSAL = 384
WINDOWS = (2, 4, 8, 16)
N_MEM, N_FFN, N_RET, N_MLA, N_STICK, N_WO = 4, 3 * CHUNKS, 13, 5, 10, 4
SUBLAYERS = ("ffn", "ret", "ffn", "ffn", "mla", "ffn", "ffn", "stick", "ffn", "ffn", "stick", "ffn")
SLOTS_OF = {"ffn": N_FFN, "ret": N_RET + N_WO, "mla": N_MLA + N_WO, "stick": N_STICK + N_WO}

CONST = {}
_at = 0
for _name, _width in (("ident", P), ("tri", P), ("ones", P),
                      ("negmask", CAUSAL), ("addmask", CAUSAL), ("poolrc", 2 * S), ("minhalf", 16),
                      ("invret", 1), ("sign", 1), ("invmla", 16),
                      ("fwd", 2 * S), ("bwd", 2 * S)):
    CONST[_name] = (_at, _at + _width)
    _at += _width
N_CONST = _at
TAIL = 3
KEPT = CONST["fwd"][0]
RET_ORDER = (6, 7, 8, 12, 0, 1, 2, 3, 4, 5, 9, 10, 11)
SOFT_AFTER = {4: (0,), 5: (1,), 6: (2,), 7: (3, 4), 8: (5, 6)}
RET_AFTER = {9: (0, 1), 10: (2, 3), 11: (4, 5), 12: (6,)}
WO_ORDER = {"ret": (0, 1, 3, 2), "mla": (0, 1, 2, 3), "stick": (0, 1, 2, 3)}
STICK_ORDER = (4, 5, 0, 1, 2, 3, 6, 7, 8, 9)
BIG = 11264


def constants():
    c = np.zeros((P, N_CONST), np.float32)

    def put(name, value):
        a, b = CONST[name]
        c[:, a:b] = np.asarray(value, np.float32).reshape(P, b - a)

    p = np.arange(P)[:, None]
    put("ident", np.eye(P))
    s = p[:, :, None] + P * np.arange(2)[None, :, None]
    t = np.arange(S)[None, None, :]
    put("fwd", np.maximum(t - s, 0))
    put("bwd", np.maximum(s - t, 0))
    put("tri", p >= np.arange(P)[None, :])
    put("ones", np.ones((P, P)))
    diag = p < np.arange(P)[None, :]
    live = np.concatenate([diag, np.ones((P, P), bool), diag], axis=1)
    put("negmask", np.where(live, -1.0, 0.0))
    put("addmask", np.where(live, 0.0, -1e30))
    group = (p[:, :, None] + P * np.arange(2)[None, :, None]) // 64
    put("poolrc", 1.0 / np.minimum(t + 1, np.array(WINDOWS)[group]))
    put("minhalf", np.full((P, 16), -0.5))
    inv = lambda dim: (1.0 / (np.float32(10000.0) ** (np.arange(0, dim, 2, dtype=np.float32) / dim))).astype(np.float32)
    put("invret", inv(P)[np.arange(P) % 64])
    put("sign", np.where(np.arange(P) < 64, -1.0, 1.0))
    put("invmla", np.tile(inv(ROPE), (P, 1)))
    return c


def build(nc, ins, out):
    f32, f32r, i32 = mybir.dt.float32, mybir.dt.float32r, mybir.dt.int32
    ACT, ALU, AX = mybir.ActivationFunctionType, mybir.AluOpType, mybir.AxisListType
    ctx = ExitStack()
    with ctx:
        sb = lambda name, shape, dt=f32: ctx.enter_context(nc.sbuf_tensor(name, shape, dt))
        ps = lambda name, n: ctx.enter_context(nc.psum_tensor(name, [P, n], f32))
        sem = lambda name: ctx.enter_context(nc.semaphore(name))

        raw = sb("raw", [P, RING, SLOT])
        w_hi = sb("w_hi", [P, RING, SLOT], f32r)
        w_lo = sb("w_lo", [P, RING, SLOT], f32r)
        x = sb("x", [P, T, D])
        xn = sb("xn", [P, T, D])
        h_hi = sb("h_hi", [P, KD, S], f32r)
        h_lo = sb("h_lo", [P, KD, S], f32r)
        m_hi = sb("m_hi", [P, KD, S], f32r)
        m_lo = sb("m_lo", [P, KD, S], f32r)
        act_hi, act_lo = m_hi[:, 0:2, :], m_lo[:, 0:2, :]
        junk = sb("junk", [P, D], mybir.dt.bfloat16)
        upd = sb("upd", [P, D])
        pre_gain = sb("pre_gain", [P, D])
        post_gain = sb("post_gain", [P, D])
        stat = sb("stat", [P, 32])
        const = sb("const", [P, KEPT])
        mk_T = sb("mk_T", [P, 2, 2, S])
        mv = sb("mv", [P, 2, 2, S])
        nat = xn
        pos_row = sb("pos_row", [P, S], i32)
        pos_col = sb("pos_col", [P, T], i32)
        trig = sb("trig", [P, 2, S + 2 * 16])
        lgd = sb("lgd", [P, 2 * HEADS_R])
        big = sb("big", [P, BIG])

        cst = lambda name: const[:, CONST[name][0]:CONST[name][1]]
        ident = cst("ident")

        class Area:
            def __init__(self):
                self.at = 0

            def take(self, *shape):
                n = int(np.prod(shape))
                v = big[:, self.at:self.at + n]
                self.at += n
                assert self.at <= BIG
                if len(shape) == 2:
                    v = v.rearrange("p (a b) -> p a b", a=shape[0])
                if len(shape) == 3:
                    v = v.rearrange("p (a b c) -> p a b c", a=shape[0], b=shape[1])
                return v

        ar = Area()
        decay = ar.take(HEADS_R, 2 * S)
        r_q, r_k = ar.take(HEADS_R, S), ar.take(HEADS_R, S)
        r_v, r_g = ar.take(T, TOK), ar.take(T, TOK)
        r_sc = ar.take(2, 2 * S)
        ar_soft = ar.at
        qm_T = ar.take(2, S)
        prob = r_sc
        af = Area()
        af.take(HEADS_R, 2 * S)
        silu_g, act = af.take(2 * S), af.take(2 * S)
        mem_rows = af.take(T, D)
        ang = af.take(4, S + 2 * 16)
        posf = af.take(S + T)
        offsets = af.take(2, 2 * S)
        am = Area()
        q_nat = am.take(T, HEADS_M * QKW)
        kv_nat = am.take(T, HEADS_M * (NOPE + DV))
        k_nat = am.take(T, HEADS_M * QKW)
        mq_T, mk2_T = am.take(HEADS_M, S), am.take(HEADS_M, S)
        c_nat = am.take(T, QR + KVR)
        kr = am.take(T, ROPE)
        rt = am.take(4, HEADS_M * 16)
        assert am.at <= ar_soft
        prob_T = upd[:, :].rearrange("p (a b) -> p a b", a=2)
        as_ = Area()
        s_q, s_k = as_.take(4, S), as_.take(4, S)
        s_v = as_.take(T, AH * AD)
        gate_b, gate_c, conv_h, pool_p = (as_.take(2, S) for _ in range(4))
        z_abs = as_.take(2, CAUSAL)
        z_ln = as_.take(2, CAUSAL)
        z_lk = as_.take(2, CAUSAL)
        z_a = as_.take(2, CAUSAL)
        conv_u, conv_y = as_.take(2, S), as_.take(2, S)
        pool_a, pool_b, pool_c, pool_e = (as_.take(2, S) for _ in range(4))
        small = sb("small", [P, 2, 8])
        pool_w = sb("pool_w", [P, 2, P])
        c_gain = sb("c_gain", [P, QR + KVR])
        rope_sw = sb("rope_sw", [P, 2 * S])
        rope_t = sb("rope_t", [P, 2 * S])
        bn = sb("bn", [P, 2 * HEADS_R, 6])
        mean_var = sb("mean_var", [P, 2 * HEADS_R, 2])
        r_rs = sb("r_rs", [P, 2 * HEADS_R])
        sm = sb("sm", [P, 2, 2, 4])
        c_hi, c_lo = h_hi[:, 0:3, :], h_lo[:, 0:3, :]
        hgain = sb("hgain", [P, TOK])

        bank0, bank1 = ps("bank0", 512), ps("bank1", 512)
        down = [ps("down0", 1024), ps("down1", 1024)]
        bank6, bank7 = ps("bank6", 512), ps("bank7", 512)
        gemm_bank = [bank0, bank1]
        mid = [down[0][:, 0:512], down[0][:, 512:1024], down[1][:, 0:512], down[1][:, 512:1024]]

        raw_in = [sem(f"raw_in{r}") for r in range(RING)]
        hi_ready, lo_ready = sem("hi_ready"), sem("lo_ready")
        slot_done = sem("slot_done")
        silu_done, prod_done = sem("silu_done"), sem("prod_done")
        act_hi_done, act_lo_done, act_turned = sem("act_hi_done"), sem("act_lo_done"), sem("act_turned")
        down_done = sem("down_done")
        square, update = sem("square"), sem("update")
        post_ss, post_rs, x_new = sem("post_ss"), sem("post_rs"), sem("x_new")
        pre_ss, pre_rs, pre_xn = sem("pre_ss"), sem("pre_rs"), sem("pre_xn")
        turned, h_hi_done, h_lo_done = sem("turned"), sem("h_hi_done"), sem("h_lo_done")
        const_in, x_in, mem_in, small_in = sem("const_in"), sem("x_in"), sem("mem_in"), sem("small_in")
        pre_in, post_in = sem("pre_in"), sem("post_in")
        out_done = sem("out_done")
        dve_link, pool_link, act_link = sem("dve_link"), sem("pool_link"), sem("act_link")
        ang_ready, trig_ready, table_ready = sem("ang_ready"), sem("trig_ready"), sem("table_ready")
        expo_ready, decay_ready = sem("expo_ready"), sem("decay_ready")
        evac = sem("evac")
        rope_swapped, rope_cos, roped = sem("rope_swapped"), sem("rope_cos"), sem("roped")
        g_scaled = sem("g_scaled")
        r_scores, r_decayed, r_out, r_copied = sem("r_scores"), sem("r_decayed"), sem("r_out"), sem("r_copied")
        r_var, r_rs_ready, r_mix = sem("r_var"), sem("r_rs_ready"), sem("r_mix")
        m_turned, m_hi_done, m_lo_done = sem("m_turned"), sem("m_hi_done"), sem("m_lo_done")
        a_scores, a_max, a_exp, a_norm = sem("a_scores"), sem("a_max"), sem("a_exp"), sem("a_norm")
        a_turned, a_probT, a_out, a_hi, a_lo = (sem(n) for n in ("a_turned", "a_probT", "a_out", "a_hi", "a_lo"))
        c_ss, c_rs, c_xn = sem("c_ss"), sem("c_rs"), sem("c_xn")
        c_turned, c_hi_done, c_lo_done = sem("c_turned"), sem("c_hi_done"), sem("c_lo_done")
        uq_mm, uq_out, ukv_mm, ukv_out = sem("uq_mm"), sem("uq_out"), sem("ukv_mm"), sem("ukv_out")
        qk_ready, qk_turned, qk_T = sem("qk_ready"), sem("qk_turned"), sem("qk_T")
        s_z, s_abs, s_ln, s_lk = sem("s_z"), sem("s_abs"), sem("s_ln"), sem("s_lk")
        s_cs, s_min, s_exp, s_out, s_hi, s_lo = (sem(n) for n in ("s_cs", "s_min", "s_exp", "s_out", "s_hi", "s_lo"))
        conv_done, conv_hi, conv_lo = sem("conv_done"), sem("conv_hi"), sem("conv_lo")
        pool_d, pool_mm, pool_hi, pool_lo = sem("pool_d"), sem("pool_mm"), sem("pool_hi"), sem("pool_lo")
        pool_w_zero = sem("pool_w_zero")

        block = ctx.enter_context(nc.Block())

        first_slot, n = [], N_MEM
        for kind in SUBLAYERS:
            first_slot.append(n)
            n += SLOTS_OF[kind]
        N_SLOTS = n
        U = len(SUBLAYERS)

        def wait(eng, s, value):
            if value > 0:
                eng.wait_ge(s, value)

        def linker(eng, s):
            count = [0]

            def link(instruction):
                count[0] += 1
                instruction.then_inc(s, 1)
                eng.wait_ge(s, count[0])
            return link

        def cols(w, c0, width):
            return w[:, c0:c0 + width].rearrange("(k p) c -> p k c", p=P)

        @block.sync
        def _(sp):
            def slot(n, src, width=SLOT, at=None):
                r = n % RING
                m = n if at is None else at
                if at is not None or n >= RING:
                    sp.wait_ge(lo_ready, m - RING + 1)
                dst = raw[:, r, 0:width]
                if len(src.shape) == 3:
                    dst = dst.rearrange("p (a b) -> p a b", a=src.shape[1])
                sp.dma_start(dst, src).then_inc(raw_in[r], 16)

            def mem_w(j):
                return cols(ins["mem_w_kv"][j % 2], SC if j < 2 else 0, SC)

            for t in range(T):
                sp.dma_start(mem_rows[:, t, :], ins["mem"][0, t * P:(t + 1) * P, :]).then_inc(mem_in, 16)
            sp.dma_start(const[:, :], ins["const"][:, 0:KEPT]).then_inc(const_in, 16)
            for j in range(3):
                slot(j, mem_w(j))
            for t in range(T):
                sp.dma_start(x[:, t, :], ins["x"][0, t * P:(t + 1) * P, :]).then_inc(x_in, 16)
            sp.dma_start(offsets, ins["const"][:, KEPT:N_CONST].rearrange("p (a b) -> p a b", a=2)).then_inc(small_in, 16)
            sp.dma_start(pos_row[:, :], ins["positions"][0, :].partition_broadcast(P)).then_inc(small_in, 16)
            sp.dma_start(pos_col[:, :], ins["positions"][0, :].rearrange("(t p) -> p t", p=P), allow_slow_non_contiguous=True).then_inc(small_in, 16)
            sp.dma_start(lgd[:, :], ins["ret_log_decay"].rearrange("a b c -> (a b c)").partition_broadcast(P)).then_inc(small_in, 16)
            sp.dma_start(hgain[:, :], ins["ret_head_norm"].rearrange("a b c -> (a b c)").partition_broadcast(P)).then_inc(small_in, 16)
            sp.dma_start(c_gain[:, 0:QR], ins["mla_q_norm"][0, :].partition_broadcast(P)).then_inc(small_in, 16)
            sp.dma_start(c_gain[:, QR:QR + KVR], ins["mla_kv_norm"][0, :].partition_broadcast(P)).then_inc(small_in, 16)
            slot(3, mem_w(3))

            stick = 0
            for u, kind in enumerate(SUBLAYERS):
                b = first_slot[u]
                l = u // 3
                if kind == "ffn":
                    f = (u % 3) // 2
                    if l < 2:
                        gu = ins["ffn_w_gu"][l, f]
                        wg, wu, wd = gu[:, 0:FF], gu[:, FF:2 * FF], ins["ffn_w_down"][l, f]
                    else:
                        wg, wu, wd = ins["ffn_w_gate_2"][l - 2, f], ins["ffn_w_up_2"][l - 2, f], ins["ffn_w_down_2"][l - 2, f]
                    wgv = wg.rearrange("(k p) c -> p k c", p=P)
                    wuv = wu.rearrange("(k p) c -> p k c", p=P)
                    wdv = wd.rearrange("(i j p) c -> p i j c", j=2, p=P)
                    gate = lambda n, i, at=None: slot(n, wgv[:, :, bass.ds(i * SC, SC)], at=at)
                    up = lambda n, i, at=None: slot(n, wuv[:, :, bass.ds(i * SC, SC)], at=at)
                    lower = lambda n, i, at=None: slot(n, wdv[:, bass.ds(i, 1), :, :].rearrange("p a j c -> p (a j) c"), at=at)
                    gate(b, 0)
                    up(b + 1, 0)
                    gate(b + 2, 1)
                    up(b + 3, 1)
                    lower(b + 4, 0)
                    with sp.Fori(1, CHUNKS - TAIL) as i:
                        gate(b + 2, i + 1, b + 2 + 3 * i)
                        lower(b + 3, i, b + 3 + 3 * i)
                        up(b + 4, i + 1, b + 4 + 3 * i)
                    n = b + 2 + 3 * (CHUNKS - TAIL)
                    for i in range(CHUNKS - TAIL + 1, CHUNKS):
                        gate(n, i)
                        up(n + 1, i)
                        n += 2
                    for i in range(CHUNKS - TAIL, CHUNKS):
                        lower(n, i)
                        n += 1
                    continue
                if kind == "ret":
                    w, wo = ins["ret_w_in"][0], ins["w_o"][l]
                    for j in range(N_RET):
                        slot(b + j, cols(w, RET_ORDER[j] * SC, SC))
                    b += N_RET
                elif kind == "mla":
                    w, wo = ins["mla_w_in"][0], ins["w_o"][l]
                    slot(b, cols(w, 0, QR))
                    slot(b + 1, cols(w, QR, SC))
                    slot(b + 2, cols(w, QR + KVR + ROPE, SC))
                    slot(b + 3, cols(ins["mla_w_uq"][0], 0, HEADS_M * QKW), 2 * HEADS_M * QKW)
                    slot(b + 4, ins["mla_w_ukv"][0], HEADS_M * (NOPE + DV))
                    b += N_MLA
                else:
                    w, wo = ins["w_in_2"][l - 2], ins["w_out_2"][l - 2]
                    for a in range(3):
                        if stick:
                            wait(sp, conv_done, 2 * stick)
                        sp.dma_start(small[:, :, a:a + 1], ins["conv_w_2"][l - 2, a, :].rearrange("(j p) -> p j", p=P).unsqueeze(2), allow_slow_non_contiguous=True).then_inc(small_in, 16)
                    if stick:
                        wait(sp, pool_lo, 2 * stick)
                    sp.dma_start(small[:, :, 3:4], ins["pool_scale_2"][l - 2, :].rearrange("(j p) -> p j", p=P).unsqueeze(2), allow_slow_non_contiguous=True).then_inc(small_in, 16)
                    sp.wait_ge(pool_w_zero, 1)
                    for g in range(4):
                        o = 64 * (g % 2)
                        sp.dma_start(pool_w[o:o + 64, g // 2, o:o + 64], ins["pool_w_2"][l - 2, g]).then_inc(small_in, 16)
                    stick += 1
                    for j in range(N_STICK):
                        slot(b + j, cols(w, STICK_ORDER[j] * SC, SC))
                    b += N_STICK
                wov = wo.rearrange("(i j p) c -> p i j c", j=2, p=P)
                for j in range(N_WO):
                    slot(b + j, wov[:, WO_ORDER[kind][j], :, :])
            for t in range(T):
                sp.wait_ge(x_new, 4 * (U - 1) + 2 * t + 2)
                sp.dma_start(out[0, t * P:(t + 1) * P, :], x[:, t, :]).then_inc(out_done, 16)
            sp.wait_ge(out_done, 16 * T)

        SMALL_FIRST = 7 * 16
        SMALL_STICK = 8 * 16

        @block.tensor
        def _(pe):
            mm, tr = nc.tensor.matmul, nc.tensor.transpose

            def take(n, at=None):
                pe.wait_ge(lo_ready, (n if at is None else at) + 1)

            def cols_of(n, bank, hi=h_hi, lo=h_lo):
                r = n % RING
                for j in range(2):
                    o = bank[:, j * S:(j + 1) * S]
                    for k in range(KD):
                        c = k * SC + j * P
                        mm(o, w_hi[:, r, c:c + P], hi[:, k, :], start=(k == 0), stop=False)
                        mm(o, w_hi[:, r, c:c + P], lo[:, k, :], start=False, stop=False)
                        last = mm(o, w_lo[:, r, c:c + P], hi[:, k, :], start=False, stop=(k == KD - 1))
                return last

            def gemm_cols(n, bank, at=None):
                take(n, at)
                cols_of(n, bank).then_inc(slot_done, 1)

            def gemm_rows_into(n, o, t, k_tiles, width, c0, n_cols, hi, lo):
                r = n % RING
                for i, k in enumerate(k_tiles):
                    c = i * width + c0
                    ts = slice(t * P, (t + 1) * P)
                    first, end = i == 0, i == len(k_tiles) - 1
                    mm(o, hi[:, k, ts], w_hi[:, r, c:c + n_cols], start=first, stop=False)
                    mm(o, hi[:, k, ts], w_lo[:, r, c:c + n_cols], start=False, stop=False)
                    last = mm(o, lo[:, k, ts], w_hi[:, r, c:c + n_cols], start=False, stop=end)
                return last

            def rows_of(n, bank, t, hi=h_hi, lo=h_lo):
                return gemm_rows_into(n, bank[:, t * S:(t + 1) * S], t, range(KD), SC, 0, SC, hi, lo)

            def gemm_rows(n, bank):
                take(n)
                for t in range(T):
                    last = rows_of(n, bank, t)
                last.then_inc(slot_done, 1)

            def high_passes(n, bank, p, t, hi, lo):
                pe.wait_ge(hi_ready, n + 1)
                o, ts = bank[:, t * S:(t + 1) * S], slice(t * P, (t + 1) * P)
                for k in range(KD):
                    c = k * SC
                    if k % 4 == 0:
                        pe.wait_ge(h_lo_done, 4 * p + 2 * t + k // 4 + 1)
                    mm(o, hi[:, k, ts], w_hi[:, n % RING, c:c + SC], start=(k == 0), stop=False)
                    mm(o, lo[:, k, ts], w_hi[:, n % RING, c:c + SC], start=False, stop=False)

            def low_pass(n, bank, t, hi):
                take(n)
                o, ts = bank[:, t * S:(t + 1) * S], slice(t * P, (t + 1) * P)
                for k in range(KD):
                    c = k * SC
                    last = mm(o, hi[:, k, ts], w_lo[:, n % RING, c:c + SC], start=False, stop=(k == KD - 1))
                return last

            def first_slots(p, parts, hi=h_hi, lo=h_lo):
                if p <= 1:
                    turn(p, 0)
                for t in range(T):
                    for n, bank in parts:
                        high_passes(n, bank, p, t, hi, lo)
                        if t == T - 1:
                            low_pass(n, bank, t, hi).then_inc(slot_done, 1)
                    if t == 0:
                        turn(p, 1)
                        for n, bank in parts:
                            low_pass(n, bank, t, hi)

            def down_of(n, k0, t, hi, lo, first, end, halves=range(2)):
                r, ts = n % RING, slice(t * P, (t + 1) * P)
                for j in range(2):
                    for part, (a, w) in enumerate(((hi, w_hi), (hi, w_lo), (lo, w_hi))):
                        for c in halves:
                            last = mm(down[t][:, c * 512:(c + 1) * 512], a[:, k0 + j, ts],
                                      w[:, r, j * D + c * 512:j * D + (c + 1) * 512],
                                      start=(first and j == 0 and part == 0), stop=(end and j == 1 and part == 2))
                return last

            def gemm_down(n, k0, first, at=None):
                take(n, at)
                for t in range(T):
                    last = down_of(n, k0, t, m_hi, m_lo, first, False)
                last.then_inc(slot_done, 1)

            def down_tail(n, k0s, p, ready=lambda i: None):
                for t in range(T):
                    for i in range(TAIL - 1):
                        if t == 0:
                            take(n + i)
                            ready(i)
                        last = down_of(n + i, k0s[i], t, m_hi, m_lo, False, False)
                        if t == T - 1:
                            last.then_inc(slot_done, 1)
                    i = TAIL - 1
                    if t == 0:
                        take(n + i)
                        ready(i)
                    for c in range(2):
                        last = down_of(n + i, k0s[i], t, m_hi, m_lo, False, True, (c,))
                        last.then_inc(*((slot_done, 1) if (t, c) == (T - 1, 1) else (down_done, 1)))
                        if (t, c) == (T - 1, 0) and p <= U:
                            turn(p, 0)

            def turn(p, t):
                for c in range(2):
                    pe.wait_ge(pre_xn, 4 * p + 2 * t + c + 1)
                    for k in range(4):
                        last = tr((bank6, bank7)[c][:, k * P:(k + 1) * P], xn[:, t, (4 * c + k) * P:(4 * c + k + 1) * P], ident)
                    last.then_inc(turned, 1)

            def soft_step(heads, i):
                if i < len(heads):
                    a, q, k, _, _ = heads[i]
                    wait(pe, a_exp, 2 * (a - 1))
                    for t in range(T):
                        last = mm(mid[a % 2][:, t * S:(t + 1) * S], q[:, t * P:(t + 1) * P], k, start=True, stop=True)
                    last.then_inc(a_scores, 1)
                if 0 <= i - 2 < len(heads):
                    a = heads[i - 2][0]
                    pe.wait_ge(a_norm, a + 1)
                    wait(pe, a_probT, a - 1)
                    for kt in range(2):
                        for t in range(T):
                            last = tr(mid[2 + a % 2][:, kt * S + t * P:kt * S + (t + 1) * P],
                                      prob[:, a % 2, t * S + kt * P:t * S + (kt + 1) * P], ident)
                    last.then_inc(a_turned, 1)
                if 0 <= i - 3 < len(heads):
                    a, _, _, value, (o0, o1) = heads[i - 3]
                    pe.wait_ge(a_probT, a + 1)
                    wait(pe, a_lo, a - 1)
                    for kt in range(2):
                        last = mm((bank6, bank7)[a % 2][o0:o1, 0:S], value(kt), prob_T[:, a % 2, kt * S:(kt + 1) * S],
                                  start=(kt == 0), stop=(kt == 1))
                    last.then_inc(a_out, 1)

            def ret_step(h):
                if h < HEADS_R:
                    pe.wait_ge(roped, 3 + h // 2 + 1)
                    wait(pe, r_decayed, h - 1)
                    for s in range(2):
                        last = mm(mid[h % 2][:, s * S:(s + 1) * S], r_k[:, h, s * P:(s + 1) * P], r_q[:, h, :], start=True, stop=True)
                    last.then_inc(r_scores, 1)
                if h:
                    g = h - 1
                    pe.wait_ge(r_decayed, g + 1)
                    wait(pe, r_copied, g - 1)
                    for t in range(T):
                        for s in range(2):
                            last = mm(mid[2 + g % 2][:, t * P:(t + 1) * P], r_sc[:, g % 2, s * S + t * P:s * S + (t + 1) * P],
                                      r_v[:, s, g * DV:(g + 1) * DV], start=(s == 0), stop=(s == 1))
                    last.then_inc(r_out, 1)

            def turn_pair(p):
                pe.wait_ge(r_mix, p + 1)
                wait(pe, m_lo_done, p - 1)
                for k in range(2):
                    for t in range(T):
                        last = tr((bank6, bank7)[p % 2][:, k * S + t * P:k * S + (t + 1) * P],
                                  nat[:, t, (2 * p + k) * P:(2 * p + k + 1) * P], ident)
                last.then_inc(m_turned, 1)

            def wo_ready(i):
                pe.wait_ge(a_lo, MH) if i == 1 else pe.wait_ge(m_lo_done, 2 if i == 0 else 3)

            def mem_heads(l, a0):
                for h in range(MH):
                    o = 64 * (h % 2)
                    yield (a0 + h, qm_T[o:o + 64, h // 2, :], mk_T[o:o + 64, l, h // 2, :],
                           lambda kt, h=h: mv[:, l, kt, h * MD:(h + 1) * MD], (o, o + 64))

            evacs = [0]

            def next_bank():
                e = evacs[0]
                evacs[0] += 1
                wait(pe, evac, e - 1)
                return gemm_bank[e % 2]

            pe.wait_ge(const_in, 16)
            first_slots(0, [(n, next_bank()) for n in range(2)], m_hi, m_lo)
            for n in (2, 3):
                take(n)
                cols_of(n, next_bank(), m_hi, m_lo).then_inc(slot_done, 1)
            pe.wait_ge(evac, evacs[0])

            ffns, sticks = 0, 0
            for u, kind in enumerate(SUBLAYERS):
                b = first_slot[u]
                if kind == "ffn":
                    e = CHUNKS * ffns
                    first_slots(u + 1, [(b, bank0), (b + 1, bank1)])

                    def chunk(n, i, at=None):
                        pe.wait_ge(silu_done, e + 1 + i)
                        gemm_cols(n, bank0, at)
                        pe.wait_ge(act_lo_done, e + 1 + i)
                        gemm_down(n + 1, 0, False, at + 1)
                        gemm_cols(n + 2, bank1, at + 2)

                    pe.wait_ge(silu_done, e + 1)
                    gemm_cols(b + 2, bank0)
                    pe.wait_ge(prod_done, e + 1)
                    for j in range(2):
                        for t in range(T):
                            last = tr(bank6[:, j * S + t * P:j * S + (t + 1) * P], act[:, t * SC + j * P:t * SC + (j + 1) * P], ident)
                    last.then_inc(act_turned, 1)
                    gemm_cols(b + 3, bank1)
                    pe.wait_ge(act_lo_done, e + 1)
                    gemm_down(b + 4, 2, True)
                    with pe.Fori(1, CHUNKS - TAIL) as i:
                        chunk(b + 2, i, at=b + 2 + 3 * i)
                    n = b + 2 + 3 * (CHUNKS - TAIL)
                    for i in range(CHUNKS - TAIL + 1, CHUNKS):
                        pe.wait_ge(silu_done, e + i)
                        gemm_cols(n, bank0)
                        pe.wait_ge(prod_done, e + i)
                        gemm_cols(n + 1, bank1)
                        n += 2
                    down_tail(n, range(0, 2 * TAIL, 2), u + 2, lambda i: pe.wait_ge(act_lo_done, e + CHUNKS - TAIL + i + 1))
                    ffns += 1
                    continue
                if kind == "ret":
                    mem = list(mem_heads(0, 0))
                    first_slots(u + 1, [(b + j, next_bank()) for j in range(2)])
                    for j in range(2, N_RET):
                        if 6 <= j < 12:
                            pe.wait_ge(rope_cos, j - 5)
                        (gemm_rows if j < 3 or j >= 10 else gemm_cols)(b + j, next_bank())
                        for i in SOFT_AFTER.get(j, ()):
                            if i == 0:
                                pe.wait_ge(evac, N_MEM + 4)
                            soft_step(mem, i)
                        for i in RET_AFTER.get(j, ()):
                            ret_step(i)
                    turn_pair(0)
                    turn_pair(1)
                    pe.wait_ge(m_lo_done, 1)
                    b += N_RET
                elif kind == "mla":
                    first_slots(u + 1, [(b + j, next_bank()) for j in range(2)])
                    gemm_cols(b + 2, next_bank())
                    pe.wait_ge(c_xn, 2)
                    for t in range(T):
                        for k in range(3):
                            bank, kk = (bank6, k) if k < 2 else (bank7, 0)
                            last = tr(bank[:, kk * S + t * P:kk * S + (t + 1) * P], c_nat[:, t, k * P:(k + 1) * P], ident)
                    last.then_inc(c_turned, 1)
                    pe.wait_ge(c_lo_done, 2)
                    take(b + 3)
                    half = HEADS_M * QKW // 2
                    for t in range(T):
                        for c in range(2):
                            last = gemm_rows_into(b + 3, mid[2 * t + c][:, 0:half], t, range(2), 2 * half, c * half, half, c_hi, c_lo)
                    last.then_inc(slot_done, 1)
                    pe.wait_ge(uq_out, 4)
                    pe.wait_ge(evac, evacs[0])
                    take(b + 4)
                    third = HEADS_M * (NOPE + DV) // 3
                    for t in range(T):
                        for c in range(3):
                            bank = (mid + [bank0, bank1])[3 * t + c]
                            last = gemm_rows_into(b + 4, bank[:, 0:third], t, (2,), 3 * third, c * third, third, c_hi, c_lo)
                    last.then_inc(slot_done, 1)
                    pe.wait_ge(ukv_out, 6)
                    pe.wait_ge(qk_ready, 2)
                    for i in range(6):
                        src = q_nat if i < 3 else k_nat
                        bank = (mid + [bank6, bank7])[i]
                        for g in range(2):
                            h = 2 * (i % 3) + g
                            for t in range(T):
                                last = tr(bank[0:QKW, g * S + t * P:g * S + (t + 1) * P], src[:, t, h * QKW:(h + 1) * QKW], ident)
                        last.then_inc(qk_turned, 1)
                    pe.wait_ge(qk_T, 6)
                    heads = [(MH + h, mq_T[0:QKW, h, :], mk2_T[0:QKW, h, :],
                                  lambda kt, h=h: kv_nat[:, kt, h * (NOPE + DV) + NOPE:(h + 1) * (NOPE + DV)], (0, P))
                                 for h in range(HEADS_M)]
                    heads += mem_heads(1, MH + HEADS_M)
                    for i in range(len(heads) + 3):
                        soft_step(heads, i)
                    pe.wait_ge(a_lo, 2 * MH + HEADS_M)
                    b += N_MLA
                else:
                    c0 = 4 * sticks

                    def logits(s, banks, start, stop):
                        for g in range(2):
                            o = 64 * g
                            k, q = s_k[o:o + 64, s, :], s_q[o:o + 64, s, :]
                            yield g, 0, mm(banks[g][:, 0:S], k[:, 0:P], q, start=start, stop=stop)
                            yield g, 1, mm(banks[g][:, S:CAUSAL], k[:, P:S], q[:, P:S], start=start, stop=stop)

                    def pair_logits(s):
                        for _, _, last in logits(s, mid[0:2], True, True):
                            pass
                        last.then_inc(s_z, 1)

                    def pair_sums(s):
                        pe.wait_ge(s_lk, c0 + s + 1)
                        wait(pe, s_min, c0 + s)
                        tri, ones = cst("tri"), cst("ones")
                        for g in range(2):
                            o = 64 * g
                            k, q = s_k[o:o + 64, s, :], s_q[o:o + 64, s, :]
                            lk = z_lk[:, g, :]
                            first, second = mid[2 + g][:, 0:S], mid[2 + g][:, S:CAUSAL]
                            mm(first, k[:, 0:P], q, start=True, stop=False)
                            mm(first, tri, lk[:, 0:S], start=False, stop=False)
                            mm(mid[2 + g][:, P:S], ones, lk[:, S:CAUSAL], start=False, stop=True)
                            mm(second, k[:, P:S], q[:, P:S], start=True, stop=False)
                            last = mm(second, tri, lk[:, S:CAUSAL], start=False, stop=True)
                        last.then_inc(s_cs, 1)

                    def pair_out(s):
                        pe.wait_ge(s_exp, c0 + s + 1)
                        wait(pe, s_lo, c0 + s - 1)
                        bank = (bank6, bank7)[s % 2]
                        for g in range(2):
                            h = 2 * s + g
                            o = slice(64 * g, 64 * g + 64)
                            mm(bank[o, 0:S], s_v[:, 0, h * AD:(h + 1) * AD], z_a[:, g, 0:S], start=True, stop=False)
                            last = mm(bank[o, P:S], s_v[:, 1, h * AD:(h + 1) * AD], z_a[:, g, S:CAUSAL], start=False, stop=True)
                        last.then_inc(s_out, 1)

                    first_slots(u + 1, [(b + j, next_bank()) for j in range(2)])
                    for j in range(2, 6):
                        gemm_cols(b + j, next_bank())
                    pe.wait_ge(evac, evacs[0])
                    for s in range(4):
                        pair_logits(s)
                        gemm_cols(b + 6 + s, next_bank())
                        if s:
                            pair_out(s - 1)
                        pair_sums(s)
                    pair_out(3)
                    pe.wait_ge(s_lo, c0 + 4)
                    pe.wait_ge(evac, evacs[0])
                    pe.wait_ge(pool_d, sticks + 1)
                    pe.wait_ge(small_in, SMALL_FIRST + SMALL_STICK * (sticks + 1))
                    for j in range(2):
                        last = mm(bank0[:, j * S:(j + 1) * S], pool_w[:, j, :], pool_e[:, j, :], start=True, stop=True)
                    last.then_inc(pool_mm, 1)
                    pe.wait_ge(pool_lo, 2 * (sticks + 1))
                    pe.wait_ge(conv_lo, sticks + 1)
                    sticks += 1
                    b += N_STICK
                gemm_down(b, 2 * WO_ORDER[kind][0], True)
                if kind == "ret":
                    turn_pair(2)
                down_tail(b + 1, [2 * k for k in WO_ORDER[kind][1:]], u + 2,
                          wo_ready if kind == "ret" else lambda i: None)

        @block.scalar
        def _(sc):
            act_fn = nc.scalar.activation
            link = linker(sc, act_link)

            def square_sum(src, dst, s, scale, bias):
                junk_free()
                act_fn(junk[:, 0:src.shape[1]], src, ACT.Square, scale=scale, accum_out=dst).then_inc(square, 1)
                squares[0] += 1
                junk_free()
                act_fn(dst, dst, ACT.Copy, bias=bias).then_inc(s, 1)

            def half_sum(src, c, parts, scale, bias):
                junk_free()
                act_fn(junk[:, c * 512:(c + 1) * 512], src[:, c * 512:(c + 1) * 512], ACT.Square, scale=scale,
                       accum_out=parts[c]).then_inc(square, 1)
                squares[0] += 1
                if c == 0:
                    junk_free()
                    act_fn(parts[0], parts[0], ACT.Copy, bias=bias).then_inc(square, 1)
                    squares[0] += 1

            def both_halves(parts, dst, s):
                junk_free()
                act_fn(dst, parts[1], ACT.Identity, bias=parts[0]).then_inc(s, 1)

            def junk_free():
                wait(sc, square, squares[0])

            squares = [0]

            def high(n, at=None, base=None):
                m = n if at is None else at
                if at is None:
                    sc.wait_ge(raw_in[n % RING], 16 * (n // RING + 1))
                    wait(sc, slot_done, n - RING + 1)
                else:
                    i, n0 = base
                    sc.wait_ge(raw_in[n0 % RING], i * 16 + 16 * (n0 // RING + 1))
                    sc.wait_ge(slot_done, m - RING + 1)
                r = n % RING
                act_fn(w_hi[:, r, :], raw[:, r, :], ACT.Copy).then_inc(hi_ready, 1)

            def pre_sum(p, t):
                parts = [stat[:, i + t:i + t + 1] for i in (2, 6)]
                for c in range(2):
                    if p == 0:
                        sc.wait_ge(mem_in, 16 * T)
                    elif p == 1:
                        sc.wait_ge(x_in, 16 * T)
                    else:
                        sc.wait_ge(x_new, 4 * (p - 2) + 2 * t + c + 1)
                    half_sum((mem_rows if p == 0 else x)[:, t, :], c, parts, D ** -0.5, EPS)
                both_halves(parts, stat[:, t:t + 1], pre_ss)

            def pre_high(p, t):
                dst = m_hi if p == 0 else h_hi
                for c in range(2):
                    sc.wait_ge(turned, 4 * p + 2 * t + c + 1)
                    act_fn(dst[:, 4 * c:4 * c + 4, t * P:(t + 1) * P],
                           (bank6, bank7)[c][:, :].rearrange("p (k t) -> p k t", k=4), ACT.Copy).then_inc(h_hi_done, 1)

            def post_half(u, t, c):
                if (t, c) == (T - 1, 1):
                    sc.wait_ge(slot_done, first_slot[u] + SLOTS_OF[SUBLAYERS[u]])
                else:
                    sc.wait_ge(down_done, 3 * u + 2 * t + c + 1)
                half = 1.0 if u % 3 == 1 else 0.5
                parts = [stat[:, i + t:i + t + 1] for i in (10, 14)]
                half_sum(down[t][:, :], c, parts, D ** -0.5 / half, EPS / half ** 2)
                if c == 1:
                    both_halves(parts, stat[:, 8 + t:9 + t], post_ss)

            def between(u):
                b = first_slot[u] + SLOTS_OF[SUBLAYERS[u]]
                post_half(u, 0, 0)
                post_half(u, 0, 1)
                if u + 1 == U:
                    post_half(u, 1, 0)
                    post_half(u, 1, 1)
                    return
                pre_sum(u + 2, 0)
                high(b)
                post_half(u, 1, 0)
                pre_high(u + 2, 0)
                post_half(u, 1, 1)
                high(b + 1)
                pre_sum(u + 2, 1)
                high(b + 2)
                pre_high(u + 2, 1)

            evacs = [0]

            def copy_out(n, dst, func=ACT.Copy, scale=1.0, width=SC):
                sc.wait_ge(slot_done, n + 1)
                src = gemm_bank[evacs[0] % 2][:, :].rearrange("p (a b) -> p a b", a=2)[:, :, 0:width]
                act_fn(dst, src, func, scale=scale).then_inc(evac, 1)
                evacs[0] += 1

            def soft_step(heads, i):
                if i < len(heads):
                    a, scale, _, _ = heads[i]
                    sc.wait_ge(a_max, a + 1)
                    wait(sc, a_turned, a - 1)
                    for t in range(T):
                        act_fn(prob[:, a % 2, t * S:(t + 1) * S], mid[a % 2][:, t * S:(t + 1) * S], ACT.Exp,
                               bias=sm[:, a % 2, t, 1:2], scale=scale, accum_out=sm[:, a % 2, t, 2:3]).then_inc(a_exp, 1)
                if 0 <= i - 2 < len(heads):
                    a = heads[i - 2][0]
                    sc.wait_ge(a_turned, a + 1)
                    wait(sc, a_out, a - 1)
                    act_fn(prob_T[:, a % 2, :], mid[2 + a % 2], ACT.Copy).then_inc(a_probT, 1)
                if 0 <= i - 3 < len(heads):
                    a, _, parts, k = heads[i - 3]
                    sc.wait_ge(a_out, a + 1)
                    act_fn(m_hi[parts, k, :], (bank6, bank7)[a % 2][parts, 0:S], ACT.Copy).then_inc(a_hi, 1)

            def mem_heads(a0):
                return [(a0 + h, 1.0, slice(64 * (h % 2), 64 * (h % 2) + 64), 6 + h // 2) for h in range(MH)]

            for t in range(T):
                pre_sum(0, t)
            high(0)
            high(1)
            for t in range(T):
                pre_high(0, t)
            high(2)
            for n in range(N_MEM):
                copy_out(n, (mv if n < 2 else mk_T)[:, n % 2, :, :])
                high(n + 3)
                if n == 1:
                    for t in range(T):
                        pre_sum(1, t)
            for t in range(T):
                pre_high(1, t)

            def tables():
                sc.wait_ge(ang_ready, 1)
                act_fn(trig[:, 0, :], ang[:, 3, :], ACT.Sin).then_inc(trig_ready, 1)
                act_fn(trig[:, 1, :], ang[:, 2, :], ACT.Sin).then_inc(trig_ready, 1)
                sc.wait_ge(expo_ready, HEADS_R)
                act_fn(decay, decay, ACT.Exp).then_inc(decay_ready, 1)

            ffns, sticks = 0, 0
            for u, kind in enumerate(SUBLAYERS):
                b = first_slot[u]
                if kind == "ffn":
                    e = CHUNKS * ffns

                    def silu(n):
                        sc.wait_ge(slot_done, n)
                        act_fn(silu_g, bank0[:, :], ACT.Silu).then_inc(silu_done, 1)

                    def act_high(i, k0=0):
                        sc.wait_ge(prod_done, e + 1 + i)
                        act_fn(m_hi[:, k0:k0 + 2, :], act.rearrange("p (a b) -> p a b", a=2), ACT.Copy).then_inc(act_hi_done, 1)

                    silu(b + 1)
                    high(b + 3)
                    high(b + 4)
                    sc.wait_ge(slot_done, b + 3)
                    sc.wait_ge(prod_done, e + 1)
                    silu(b + 3)
                    sc.wait_ge(act_turned, ffns + 1)
                    act_fn(m_hi[:, 2:4, :], bank6[:, :].rearrange("p (a b) -> p a b", a=2), ACT.Copy).then_inc(act_hi_done, 1)
                    high(b + 5)
                    high(b + 6)
                    act_high(1)
                    high(b + 7)
                    with sc.Fori(1, CHUNKS - TAIL) as i:
                        silu(b + 3 + 3 * i)
                        high(b + 5, b + 5 + 3 * i, (i, b + 5))
                        high(b + 6, b + 6 + 3 * i, (i, b + 6))
                        act_high(i + 1)
                        high(b + 7, b + 7 + 3 * i, (i, b + 7))
                    if u == 0:
                        tables()
                    n = b + 2 + 3 * (CHUNKS - TAIL)
                    for i in range(1, TAIL):
                        silu(n + 1)
                        high(n + 3)
                        if i == TAIL - 1:
                            high(n + 4)
                        act_high(CHUNKS - TAIL + i, 2 * i)
                        if i < TAIL - 1:
                            high(n + 4)
                        n += 2
                    b += N_FFN
                    ffns += 1
                else:
                    if kind == "ret":
                        mem = mem_heads(0)
                        for j in range(N_RET):
                            if 4 <= j < 10:
                                sc.wait_ge(slot_done, b + j + 1)
                                wait(sc, roped, j - 4)
                                bank = gemm_bank[evacs[0] % 2]
                                act_fn(rope_sw[0:64, :], bank[64:P, :], ACT.Copy).then_inc(rope_swapped, 1)
                                act_fn(rope_sw[64:P, :], bank[0:64, :], ACT.Copy).then_inc(evac, 1)
                                evacs[0] += 1
                            elif j < 3:
                                copy_out(b + j, r_v[:, :, j * SC:(j + 1) * SC])
                            elif j == 3:
                                copy_out(b + j, qm_T, scale=MD ** -0.5)
                            else:
                                copy_out(b + j, r_g[:, :, (j - 10) * SC:(j - 9) * SC], ACT.Silu)
                            high(b + j + 3)
                            for i in SOFT_AFTER.get(j, ()):
                                soft_step(mem, i)
                            for h in RET_AFTER.get(j, ()):
                                if h:
                                    g = h - 1
                                    sc.wait_ge(r_out, g + 1)
                                    act_fn(nat[:, :, g * DV:(g + 1) * DV], mid[2 + g % 2][:, 0:2 * P].rearrange("p (t d) -> p t d", t=2),
                                           ACT.Copy).then_inc(r_copied, 1)
                        for p in range(3):
                            sc.wait_ge(m_turned, p + 1)
                            act_fn(m_hi[:, 2 * p:2 * p + 2, :], (bank6, bank7)[p % 2][:, :].rearrange("p (k t) -> p k t", k=2),
                                   ACT.Copy).then_inc(m_hi_done, 1)
                        b += N_RET
                    elif kind == "mla":
                        copy_out(b, c_nat[:, :, 0:QR])
                        high(b + 3)
                        sc.wait_ge(slot_done, b + 2)
                        src = gemm_bank[evacs[0] % 2][:, :].rearrange("p (a b) -> p a b", a=2)
                        link(act_fn(c_nat[:, :, QR:QR + KVR], src[:, :, 0:KVR], ACT.Copy))
                        act_fn(kr, src[:, :, KVR:KVR + ROPE], ACT.Copy).then_inc(evac, 1)
                        evacs[0] += 1
                        sc.wait_ge(evac, evacs[0])
                        for t in range(T):
                            square_sum(c_nat[:, t, 0:QR], stat[:, 16 + t:17 + t], c_ss, QR ** -0.5, EPS)
                            square_sum(c_nat[:, t, QR:QR + KVR], stat[:, 18 + t:19 + t], c_ss, KVR ** -0.5, EPS)
                        high(b + 4)
                        copy_out(b + 2, qm_T, scale=MD ** -0.5)
                        high(b + 5)
                        sc.wait_ge(c_turned, 1)
                        act_fn(c_hi[:, 0:2, :], bank6[:, :].rearrange("p (a b) -> p a b", a=2), ACT.Copy).then_inc(c_hi_done, 1)
                        act_fn(c_hi[:, 2, :], bank7[:, 0:S], ACT.Copy).then_inc(c_hi_done, 1)
                        half = HEADS_M * QKW // 2
                        sc.wait_ge(slot_done, b + 4)
                        for t in range(T):
                            for c in range(2):
                                act_fn(q_nat[:, t, c * half:(c + 1) * half], mid[2 * t + c][:, 0:half], ACT.Copy).then_inc(uq_out, 1)
                        high(b + 6)
                        third = HEADS_M * (NOPE + DV) // 3
                        sc.wait_ge(slot_done, b + 5)
                        for t in range(T):
                            for c in range(3):
                                act_fn(kv_nat[:, t, c * third:(c + 1) * third], (mid + [bank0, bank1])[3 * t + c][:, 0:third],
                                       ACT.Copy).then_inc(ukv_out, 1)
                        high(b + 7)
                        for i in range(6):
                            sc.wait_ge(qk_turned, i + 1)
                            dst = (mq_T if i < 3 else mk2_T)[0:QKW, 2 * (i % 3):2 * (i % 3) + 2, :]
                            act_fn(dst, (mid + [bank6, bank7])[i][0:QKW, :].rearrange("p (a b) -> p a b", a=2), ACT.Copy).then_inc(qk_T, 1)
                        heads = [(MH + h, QKW ** -0.5, slice(0, P), h) for h in range(HEADS_M)] + mem_heads(MH + HEADS_M)
                        for i in range(len(heads) + 3):
                            soft_step(heads, i)
                        b += N_MLA
                    else:
                        c0 = 4 * sticks
                        for j in range(6):
                            if j < 2:
                                copy_out(b + j, s_v[:, :, j * SC:(j + 1) * SC])
                            elif j < 4:
                                copy_out(b + j, s_q[:, 2 * j - 4:2 * j - 2, :], scale=AD ** -0.5)
                            else:
                                copy_out(b + j, s_k[:, 2 * j - 8:2 * j - 6, :])
                            high(b + j + 3)

                        def pair_exp(s):
                            sc.wait_ge(s_min, c0 + s + 1)
                            wait(sc, s_out, c0 + s)
                            act_fn(z_a, z_abs, ACT.Exp).then_inc(s_exp, 1)

                        def pair_high(s):
                            sc.wait_ge(s_out, c0 + s + 1)
                            act_fn(m_hi[:, s, :], (bank6, bank7)[s % 2][:, 0:S], ACT.Copy).then_inc(s_hi, 1)

                        for s in range(4):
                            if s:
                                pair_exp(s - 1)
                            sc.wait_ge(s_z, c0 + s + 1)
                            z = down[0][:, :].rearrange("p (a b) -> p a b", a=2)[:, :, 0:CAUSAL]
                            if s:
                                sc.wait_ge(s_exp, c0 + s)
                            act_fn(z_abs, z, ACT.Abs).then_inc(s_abs, 1)
                            sc.wait_ge(s_abs, 3 * (c0 + s) + 1)
                            act_fn(z_abs, z_abs, ACT.Exp, scale=-1.0).then_inc(s_abs, 1)
                            sc.wait_ge(s_abs, 3 * (c0 + s) + 2)
                            wait(sc, s_lk, c0 + s)
                            act_fn(z_ln, z_abs, ACT.Ln, bias=1.0).then_inc(s_abs, 1)
                            copy_out(b + 6 + s, (gate_b, gate_c, conv_h, pool_p)[s])
                            if s:
                                pair_high(s - 1)
                            if s < 3:
                                high(b + 9 + s)
                        pair_exp(3)
                        high(b + 12)
                        pair_high(3)
                        sc.wait_ge(conv_done, 2 * (sticks + 1))
                        act_fn(m_hi[:, 4:6, :], conv_y, ACT.Copy).then_inc(conv_hi, 1)
                        sc.wait_ge(small_in, SMALL_FIRST + SMALL_STICK * (sticks + 1))
                        sc.wait_ge(pool_mm, sticks + 1)
                        for j in range(2):
                            act_fn(m_hi[:, 6 + j, :], bank0[:, j * S:(j + 1) * S], ACT.Copy, scale=small[:, j, 3:4]).then_inc(pool_hi, 1)
                        sticks += 1
                        b += N_STICK
                    high(b + 3)
                between(u)

        @block.vector
        def _(ve):
            v = nc.vector
            link = linker(ve, dve_link)

            def low(n, at=None):
                ve.wait_ge(hi_ready, (n if at is None else at) + 1)
                r = n % RING
                v.tensor_tensor(w_lo[:, r, :], raw[:, r, :], w_hi[:, r, :].bitcast(f32), ALU.subtract).then_inc(lo_ready, 1)

            def low_half(n, c):
                ve.wait_ge(hi_ready, n + 1)
                r, h = n % RING, slice(c * SLOT // 2, (c + 1) * SLOT // 2)
                last = v.tensor_tensor(w_lo[:, r, h], raw[:, r, h], w_hi[:, r, h].bitcast(f32), ALU.subtract)
                if c == 1:
                    last.then_inc(lo_ready, 1)

            def pre_scale(p, t):
                ve.wait_ge(pre_in, 16 * (p + 1))
                ve.wait_ge(pre_rs, 2 * p + t + 1)
                for c in range(2):
                    h = slice(c * 512, (c + 1) * 512)
                    wait(ve, turned, 4 * (p - 1) + 2 * t + c + 1)
                    v.scalar_tensor_tensor(xn[:, t, h], (mem_rows if p == 0 else x)[:, t, h], stat[:, 4 + t:5 + t],
                                           (post_gain if p == 0 else pre_gain)[:, h], ALU.mult, ALU.mult).then_inc(pre_xn, 1)

            def pre_low(p, t):
                hi, lo = (m_hi, m_lo) if p == 0 else (h_hi, h_lo)
                for c in range(2):
                    ve.wait_ge(h_hi_done, 4 * p + 2 * t + c + 1)
                    sl = (slice(None), slice(4 * c, 4 * c + 4), slice(t * P, (t + 1) * P))
                    v.tensor_tensor(lo[sl], (bank6, bank7)[c][:, :].rearrange("p (k t) -> p k t", k=4),
                                    hi[sl].bitcast(f32), ALU.subtract).then_inc(h_lo_done, 1)

            def post_norm(u, t):
                ve.wait_ge(post_in, 16 * (u + 1))
                ve.wait_ge(post_rs, 2 * u + t + 1)
                first_update = updates[0]
                for c in range(2):
                    h = slice(c * 512, (c + 1) * 512)
                    if t == 1:
                        ve.wait_ge(x_new, 4 * u + c + 1)
                    v.scalar_tensor_tensor(upd[:, h], down[t][:, h], stat[:, 12 + t:13 + t], post_gain[:, h],
                                           ALU.mult, ALU.mult).then_inc(update, 1)
                    updates[0] += 1
                for c in range(2):
                    h = slice(c * 512, (c + 1) * 512)
                    ve.wait_ge(update, first_update + c + 1)
                    v.tensor_tensor(x[:, t, h], x[:, t, h], upd[:, h], ALU.add).then_inc(x_new, 1)

            updates = [0]

            def between(u):
                b = first_slot[u] + SLOTS_OF[SUBLAYERS[u]]
                post_norm(u, 0)
                if u + 1 == U:
                    post_norm(u, 1)
                    return
                pre_scale(u + 2, 0)
                low_half(b, 0)
                pre_low(u + 2, 0)
                low_half(b, 1)
                post_norm(u, 1)
                low_half(b + 1, 0)
                pre_scale(u + 2, 1)
                low_half(b + 1, 1)
                pre_low(u + 2, 1)
                low(b + 2)

            def soft_step(heads, i):
                if i < len(heads):
                    a, scale, _, _ = heads[i]
                    ve.wait_ge(a_scores, a + 1)
                    link(v.reduce_max(sm[:, a % 2, :, 0], mid[a % 2].rearrange("p (a b) -> p a b", a=2), AX.X))
                    v.tensor_scalar(sm[:, a % 2, :, 1], sm[:, a % 2, :, 0], -scale, None, ALU.mult).then_inc(a_max, 1)
                if 0 <= i - 1 < len(heads):
                    a = heads[i - 1][0]
                    ve.wait_ge(a_exp, 2 * a + 2)
                    link(v.reciprocal(sm[:, a % 2, :, 3], sm[:, a % 2, :, 2]))
                    for t in range(T):
                        row = prob[:, a % 2, t * S:(t + 1) * S]
                        last = v.tensor_scalar(row, row, sm[:, a % 2, t, 3:4], None, ALU.mult)
                    last.then_inc(a_norm, 1)
                if 0 <= i - 3 < len(heads):
                    a, _, parts, k = heads[i - 3]
                    ve.wait_ge(a_hi, a + 1)
                    v.tensor_tensor(m_lo[parts, k, :], (bank6, bank7)[a % 2][parts, 0:S], m_hi[parts, k, :].bitcast(f32),
                                    ALU.subtract).then_inc(a_lo, 1)

            def mem_heads(a0):
                return [(a0 + h, 1.0, slice(64 * (h % 2), 64 * (h % 2) + 64), 6 + h // 2) for h in range(MH)]

            def angles():
                ve.wait_ge(small_in, SMALL_FIRST)
                ve.wait_ge(const_in, 16)
                link(v.tensor_copy(posf[:, 0:S], pos_row[:, :]))
                link(v.tensor_copy(posf[:, S:S + T], pos_col[:, :]))
                a0, a1, a2, a3 = (ang[:, j, :] for j in range(4))
                link(v.tensor_scalar(a0[:, 0:S], posf[:, 0:S], cst("invret"), None, ALU.mult))
                for t in range(T):
                    link(v.tensor_scalar(a0[:, S + 16 * t:S + 16 * t + 16], cst("invmla"), posf[:, S + t:S + t + 1], None, ALU.mult))
                magic = 1.5 * 2.0 ** 23
                link(v.tensor_scalar(a1, a0, 1.0 / (2.0 * math.pi), magic, ALU.mult, ALU.add))
                link(v.tensor_scalar(a1, a1, magic, None, ALU.subtract))
                turn1 = 6.28125
                turn2 = round((2.0 * math.pi - turn1) * 2.0 ** 21) / 2.0 ** 21
                turn3 = 2.0 * math.pi - turn1 - turn2
                link(v.scalar_tensor_tensor(a2, a1, -turn1, a0, ALU.mult, ALU.add))
                link(v.scalar_tensor_tensor(a0, a1, -turn2, a2, ALU.mult, ALU.add))
                link(v.scalar_tensor_tensor(a2, a1, -turn3, a0, ALU.mult, ALU.add))
                pi = float(np.nextafter(np.float32(math.pi), np.float32(0)))
                link(v.tensor_scalar(a2, a2, -pi, pi, ALU.max, ALU.min))
                link(v.tensor_scalar(a1, a2, -1.0, None, ALU.mult))
                link(v.tensor_tensor(a1, a1, a2, ALU.max))
                v.tensor_scalar(a3, a1, -1.0, math.pi / 2, ALU.mult, ALU.add).then_inc(ang_ready, 1)

            for t in range(T):
                pre_scale(0, t)
            low(0)
            low(1)
            for t in range(T):
                pre_low(0, t)
            low(2)
            low(3)
            low(4)
            for t in range(T):
                pre_scale(1, t)
            low(5)
            for t in range(T):
                pre_low(1, t)
            low(6)

            ffns, sticks = 0, 0
            for u, kind in enumerate(SUBLAYERS):
                b = first_slot[u]
                if kind == "ffn":
                    e = CHUNKS * ffns

                    def product(i, n):
                        ve.wait_ge(silu_done, e + 1 + i)
                        ve.wait_ge(slot_done, n)
                        v.tensor_tensor(act, bank1[:, :], silu_g, ALU.mult).then_inc(prod_done, 1)

                    def act_low(i, k0=0):
                        ve.wait_ge(act_hi_done, e + 1 + i)
                        v.tensor_tensor(m_lo[:, k0:k0 + 2, :], act.rearrange("p (a b) -> p a b", a=2),
                                        m_hi[:, k0:k0 + 2, :].bitcast(f32), ALU.subtract).then_inc(act_lo_done, 1)

                    product(0, b + 2)
                    low(b + 3)
                    low(b + 4)
                    ve.wait_ge(act_hi_done, e + 1)
                    v.tensor_tensor(m_lo[:, 2:4, :], bank6[:, :].rearrange("p (a b) -> p a b", a=2),
                                    m_hi[:, 2:4, :].bitcast(f32), ALU.subtract).then_inc(act_lo_done, 1)
                    low(b + 5)
                    product(1, b + 4)
                    low(b + 6)
                    act_low(1)
                    low(b + 7)
                    if u == 0:
                        angles()
                    with ve.Fori(1, CHUNKS - TAIL) as i:
                        low(b + 5, b + 5 + 3 * i)
                        low(b + 6, b + 6 + 3 * i)
                        product(i + 1, b + 5 + 3 * i)
                        act_low(i + 1)
                        low(b + 7, b + 7 + 3 * i)
                    n = b + 2 + 3 * (CHUNKS - TAIL)
                    for i in range(1, TAIL):
                        low(n + 3)
                        ve.wait_ge(act_lo_done, e + CHUNKS - TAIL + i)
                        product(CHUNKS - TAIL + i, n + 2)
                        if i == TAIL - 1:
                            low(n + 4)
                        act_low(CHUNKS - TAIL + i, 2 * i)
                        if i < TAIL - 1:
                            low(n + 4)
                        n += 2
                    b += N_FFN
                    ffns += 1
                else:
                    if kind == "ret":
                        mem = mem_heads(0)

                        def statistics(h):
                            ve.wait_ge(r_copied, h + 1)
                            for t in range(T):
                                last = v.bn_stats(bn[:, 2 * h + t, :], nat[:, t, h * DV:(h + 1) * DV])
                            link(last)
                            for t in range(T):
                                last = v.bn_aggr(mean_var[:, 2 * h + t, :], bn[:, 2 * h + t, :])
                            link(last)
                            if h % 2:
                                v.tensor_scalar(r_rs[:, 2 * h - 2:2 * h + 2], mean_var[:, 2 * h - 2:2 * h + 2, 1], EPS, None,
                                                ALU.add).then_inc(r_var, 1)

                        def gate_pair(p):
                            ve.wait_ge(r_rs_ready, p + 1)
                            for h in (2 * p, 2 * p + 1):
                                for t in range(T):
                                    i = 2 * h + t
                                    y = nat[:, t, h * DV:(h + 1) * DV]
                                    last = v.tensor_scalar(y, y, mean_var[:, i, 0:1], r_rs[:, i:i + 1], ALU.subtract, ALU.mult)
                            link(last)
                            ve.wait_ge(g_scaled, p + 1)
                            y = nat[:, :, p * SC:(p + 1) * SC]
                            v.tensor_tensor(y, y, r_g[:, :, p * SC:(p + 1) * SC], ALU.mult).then_inc(r_mix, 1)

                        def pair_low(p):
                            ve.wait_ge(m_hi_done, p + 1)
                            v.tensor_tensor(m_lo[:, 2 * p:2 * p + 2, :], (bank6, bank7)[p % 2][:, :].rearrange("p (k t) -> p k t", k=2),
                                            m_hi[:, 2 * p:2 * p + 2, :].bitcast(f32), ALU.subtract).then_inc(m_lo_done, 1)

                        for j in range(N_RET):
                            if 4 <= j < 10:
                                ve.wait_ge(slot_done, b + j + 1)
                                ve.wait_ge(table_ready, 1)
                                wait(ve, roped, j - 4)
                                ve.wait_ge(rope_swapped, j - 3)
                                ve.wait_ge(evac, N_MEM + j + 1)
                                v.tensor_tensor(rope_t[:, :].rearrange("p (a b) -> p a b", a=2),
                                                gemm_bank[j % 2][:, :].rearrange("p (a b) -> p a b", a=2),
                                                trig[:, 0:1, 0:S].broadcast_to([P, 2, S]), ALU.mult).then_inc(rope_cos, 1)
                            low(b + j + 3)
                            for i in SOFT_AFTER.get(j, ()):
                                soft_step(mem, i)
                            for h in RET_AFTER.get(j, ()):
                                if h < HEADS_R:
                                    ve.wait_ge(r_scores, h + 1)
                                    ve.wait_ge(decay_ready, 1)
                                    wait(ve, r_out, h - 1)
                                    v.scalar_tensor_tensor(r_sc[:, h % 2, :], mid[h % 2], P ** -0.5, decay[:, h, :],
                                                           ALU.mult, ALU.mult).then_inc(r_decayed, 1)
                                if h >= 2:
                                    statistics(h - 2)
                                if h in (4, 6):
                                    gate_pair((h - 4) // 2)
                        statistics(HEADS_R - 1)
                        pair_low(0)
                        gate_pair(2)
                        pair_low(1)
                        pair_low(2)
                        b += N_RET
                    elif kind == "mla":
                        low(b + 3)
                        ve.wait_ge(c_rs, 1)
                        for t in range(T):
                            v.scalar_tensor_tensor(c_nat[:, t, 0:QR], c_nat[:, t, 0:QR], stat[:, 24 + t:25 + t], c_gain[:, 0:QR], ALU.mult, ALU.mult)
                            last = v.scalar_tensor_tensor(c_nat[:, t, QR:QR + KVR], c_nat[:, t, QR:QR + KVR], stat[:, 26 + t:27 + t],
                                                          c_gain[:, QR:QR + KVR], ALU.mult, ALU.mult)
                            last.then_inc(c_xn, 1)
                        low(b + 4)
                        low(b + 5)
                        ve.wait_ge(c_hi_done, 1)
                        v.tensor_tensor(c_lo[:, 0:2, :], bank6[:, :].rearrange("p (a b) -> p a b", a=2), c_hi[:, 0:2, :].bitcast(f32), ALU.subtract).then_inc(c_lo_done, 1)
                        ve.wait_ge(c_hi_done, 2)
                        v.tensor_tensor(c_lo[:, 2, :], bank7[:, 0:S], c_hi[:, 2, :].bitcast(f32), ALU.subtract).then_inc(c_lo_done, 1)

                        def rotate(x1, x2, t, heads):
                            n = heads * 16
                            tmp = [rt[:, j, 0:n].rearrange("p (a b) -> p a b", a=heads) for j in range(4)]
                            at = S + 16 * t
                            c = trig[:, 0:1, at:at + 16].broadcast_to([P, heads, 16])
                            s = trig[:, 1:2, at:at + 16].broadcast_to([P, heads, 16])
                            v.tensor_tensor(tmp[0], x1, c, ALU.mult)
                            v.tensor_tensor(tmp[1], x2, s, ALU.mult)
                            v.tensor_tensor(tmp[2], x1, s, ALU.mult)
                            link(v.tensor_tensor(tmp[3], x2, c, ALU.mult))
                            v.tensor_tensor(x1, tmp[0], tmp[1], ALU.subtract)
                            link(v.tensor_tensor(x2, tmp[2], tmp[3], ALU.add))

                        for t in range(T):
                            rotate(kr[:, t:t + 1, 0:16], kr[:, t:t + 1, 16:32], t, 1)
                        ve.wait_ge(uq_out, 4)
                        for t in range(T):
                            q = q_nat[:, t, :].rearrange("p (h d) -> p h d", h=HEADS_M)
                            rotate(q[:, :, NOPE:NOPE + 16], q[:, :, NOPE + 16:QKW], t, HEADS_M)
                        v.tensor_copy(k_nat[:, 0, 0:1], q_nat[:, 0, 0:1]).then_inc(qk_ready, 1)
                        low(b + 6)
                        ve.wait_ge(ukv_out, 6)
                        ve.wait_ge(qk_ready, 1)
                        for t in range(T):
                            k = k_nat[:, t, :].rearrange("p (h d) -> p h d", h=HEADS_M)
                            kv = kv_nat[:, t, :].rearrange("p (h d) -> p h d", h=HEADS_M)
                            v.tensor_copy(k[:, :, 0:NOPE], kv[:, :, 0:NOPE])
                            last = v.tensor_copy(k[:, :, NOPE:QKW], kr[:, t:t + 1, :].broadcast_to([P, HEADS_M, ROPE]))
                        last.then_inc(qk_ready, 1)
                        low(b + 7)
                        heads = [(MH + h, QKW ** -0.5, slice(0, P), h) for h in range(HEADS_M)] + mem_heads(MH + HEADS_M)
                        for i in range(len(heads) + 3):
                            soft_step(heads, i)
                        b += N_MLA
                    else:
                        c0 = 4 * sticks
                        for j in range(6):
                            low(b + j + 3)

                        def pair_min(s):
                            ve.wait_ge(s_cs, c0 + s + 1)
                            cs = down[1][:, :].rearrange("p (a b) -> p a b", a=2)
                            for g in range(2):
                                last = v.scalar_tensor_tensor(z_abs[:, g, :], cs[:, g, 0:CAUSAL], 0.0, cst("addmask"), ALU.min, ALU.add)
                            last.then_inc(s_min, 1)

                        def pair_low(s):
                            ve.wait_ge(s_hi, c0 + s + 1)
                            v.tensor_tensor(m_lo[:, s, :], (bank6, bank7)[s % 2][:, 0:S], m_hi[:, s, :].bitcast(f32), ALU.subtract).then_inc(s_lo, 1)

                        for s in range(4):
                            ve.wait_ge(s_abs, 3 * (c0 + s) + 3)
                            z = down[0][:, :].rearrange("p (a b) -> p a b", a=2)
                            for g in range(2):
                                last = v.scalar_tensor_tensor(z_ln[:, g, :], z[:, g, 0:CAUSAL], 0.0, z_ln[:, g, :], ALU.max, ALU.add)
                            link(last)
                            for g in range(2):
                                last = v.tensor_tensor(z_lk[:, g, :], z_ln[:, g, :], cst("negmask"), ALU.mult)
                            last.then_inc(s_lk, 1)
                            if s:
                                pair_low(s - 1)
                            if s < 3:
                                pair_min(s)
                                low(b + 9 + s)
                        pair_min(3)
                        low(b + 12)
                        pair_low(3)
                        ve.wait_ge(evac, 4 + N_RET + 3 + 10 * sticks + 9)
                        ve.wait_ge(small_in, SMALL_FIRST + SMALL_STICK * (sticks + 1))
                        link(v.tensor_tensor(conv_u, gate_c, conv_h, ALU.mult))
                        for j in range(2):
                            link(v.tensor_scalar(conv_y[:, j, :], conv_u[:, j, :], small[:, j, 2:3], None, ALU.mult))
                            for tap, shift in ((1, 1), (0, 2)):
                                link(v.scalar_tensor_tensor(conv_y[:, j, shift:S], conv_u[:, j, 0:S - shift], small[:, j, tap:tap + 1],
                                                            conv_y[:, j, shift:S], ALU.mult, ALU.add))
                            v.tensor_tensor(conv_y[:, j, :], conv_y[:, j, :], gate_b[:, j, :], ALU.mult).then_inc(conv_done, 1)
                        ve.wait_ge(conv_hi, sticks + 1)
                        v.tensor_tensor(m_lo[:, 4:6, :], conv_y, m_hi[:, 4:6, :].bitcast(f32), ALU.subtract).then_inc(conv_lo, 1)
                        ve.wait_ge(pool_hi, 2 * (sticks + 1))
                        for j in range(2):
                            v.scalar_tensor_tensor(m_lo[:, 6 + j, :], bank0[:, j * S:(j + 1) * S], small[:, j, 3:4],
                                                   m_hi[:, 6 + j, :].bitcast(f32), ALU.mult, ALU.subtract).then_inc(pool_lo, 1)
                        sticks += 1
                        b += N_STICK
                    low(b + 3)
                between(u)

        @block.gpsimd
        def _(gp):
            g = nc.gpsimd
            link = linker(gp, pool_link)
            half = cst("minhalf")

            def pre_root(p, t):
                gp.wait_ge(pre_ss, 2 * p + t + 1)
                g.tensor_tensor(stat[:, 4 + t:5 + t], stat[:, t:t + 1], half[:, 0:1], ALU.pow).then_inc(pre_rs, 1)

            def post_root(u, t):
                gp.wait_ge(post_ss, 2 * u + t + 1)
                g.tensor_tensor(stat[:, 12 + t:13 + t], stat[:, 8 + t:9 + t], half[:, 0:1], ALU.pow).then_inc(post_rs, 1)

            def load_gain(buf, s, src):
                gp.dma_start(buf[:, :], src.partition_broadcast(P)).then_inc(s, 16)

            def gain_row(u, i):
                l, f = u // 3, u % 3
                return ins["norm_gains"][l, 2 * f + i, :] if l < 2 else ins["norm_g_2"][l - 2, 2 * f + i, :]

            def load_pre_gain(p):
                wait(gp, pre_xn, 4 * p)
                load_gain(pre_gain, pre_in, gain_row(p - 1, 0))

            def load_post_gain(u):
                wait(gp, x_new, 4 * u)
                load_gain(post_gain, post_in, gain_row(u, 1))

            load_gain(post_gain, pre_in, ins["mem_norm"])
            gp.wait_ge(const_in, 16)
            for t in range(T):
                pre_root(0, t)
            gp.wait_ge(pre_in, 16)
            load_gain(pre_gain, pre_in, gain_row(0, 0))
            for t in range(T):
                pre_root(1, t)
            gp.wait_ge(small_in, SMALL_FIRST)
            for h in range(HEADS_R):
                e = decay[:, h, :]
                g.tensor_scalar(e, offsets[:, 0, :], lgd[:, h:h + 1], None, ALU.mult)
                link(g.tensor_scalar(rope_t[:, :], offsets[:, 1, :], lgd[:, HEADS_R + h:HEADS_R + h + 1], None, ALU.mult))
                last = g.tensor_tensor(e, e, rope_t[:, :], ALU.add)
                last.then_inc(expo_ready, 1)
                gp.wait_ge(expo_ready, h + 1)
            g.memset(pool_w[:, :, :], 0.0).then_inc(pool_w_zero, 1)
            gp.wait_ge(pre_xn, 4)
            load_post_gain(0)
            load_pre_gain(2)
            gp.wait_ge(trig_ready, 2)
            g.tensor_scalar(trig[:, 1, 0:S], trig[:, 1, 0:S], cst("sign"), None, ALU.mult).then_inc(table_ready, 1)
            sticks = 0
            for u, kind in enumerate(SUBLAYERS):
                if kind == "ret":
                    for j in range(6):
                        gp.wait_ge(rope_swapped, j + 1)
                        gp.wait_ge(evac, N_MEM + 4 + j + 1)
                        gp.wait_ge(table_ready, 1)
                        link(g.tensor_tensor(rope_sw[:, :].rearrange("p (a b) -> p a b", a=2), rope_sw[:, :].rearrange("p (a b) -> p a b", a=2),
                                             trig[:, 1:2, 0:S].broadcast_to([P, 2, S]), ALU.mult))
                        gp.wait_ge(rope_cos, j + 1)
                        dst = (r_q if j < 3 else r_k)[:, 2 * (j % 3):2 * (j % 3) + 2, :]
                        g.tensor_tensor(dst, rope_t[:, :].rearrange("p (a b) -> p a b", a=2),
                                        rope_sw[:, :].rearrange("p (a b) -> p a b", a=2), ALU.add).then_inc(roped, 1)
                    for p in range(3):
                        gp.wait_ge(evac, N_MEM + 11 + p)
                        c = slice(p * SC, (p + 1) * SC)
                        for t in range(T):
                            last = g.tensor_tensor(r_g[:, t, c], r_g[:, t, c], hgain[:, c], ALU.mult)
                        last.then_inc(g_scaled, 1)
                        gp.wait_ge(r_var, p + 1)
                        r = r_rs[:, 4 * p:4 * p + 4]
                        g.tensor_tensor(r, r, half[:, 0:4], ALU.pow).then_inc(r_rs_ready, 1)
                elif kind == "mla":
                    gp.wait_ge(c_ss, 4)
                    g.tensor_tensor(stat[:, 24:28], stat[:, 16:20], half[:, 0:4], ALU.pow).then_inc(c_rs, 1)
                elif kind == "stick":
                    gp.wait_ge(evac, 4 + N_RET + 3 + 10 * (sticks + 1))
                    wait(gp, pool_mm, sticks)
                    sums = [pool_p, pool_a, pool_b, pool_a, pool_b]
                    for i, w in enumerate(WINDOWS):
                        src, dst, sh = sums[i], sums[i + 1], w // 2
                        g.tensor_copy(dst[:, :, 0:sh], src[:, :, 0:sh])
                        link(g.tensor_tensor(dst[:, :, sh:S], src[:, :, sh:S], src[:, :, 0:S - sh], ALU.add))
                        o = slice(64 * (i % 2), 64 * (i % 2) + 64)
                        link(g.tensor_copy(pool_c[o, i // 2, :], dst[o, i // 2, :]))
                    link(g.tensor_tensor(pool_c, pool_c, cst("poolrc").rearrange("p (a b) -> p a b", a=2), ALU.mult))
                    g.tensor_tensor(pool_e, pool_c, pool_p, ALU.subtract).then_inc(pool_d, 1)
                    sticks += 1
                post_root(u, 0)
                if u + 1 < U:
                    pre_root(u + 2, 0)
                post_root(u, 1)
                if u + 1 < U:
                    pre_root(u + 2, 1)
                    load_post_gain(u + 1)
                if u + 2 < U:
                    load_pre_gain(u + 3)


NAMES = ("x", "mem", "positions", "norm_gains", "ffn_w_gu", "ffn_w_down", "w_o", "mem_norm", "mem_w_kv", "ret_w_in",
         "ret_log_decay", "ret_head_norm", "mla_w_in", "mla_q_norm", "mla_kv_norm", "mla_w_uq", "mla_w_ukv",
         "norm_g_2", "ffn_w_gate_2", "ffn_w_up_2", "ffn_w_down_2", "w_in_2", "conv_w_2", "pool_w_2", "pool_scale_2",
         "w_out_2")


def kernel(**inputs):
    import concourse.bacc as bacc
    from concourse.bass_utils import run_bass_kernel_spmd

    nc = bacc.Bacc("TRN2", target_bir_lowering=False, num_devices=1)
    arrays = {f"in_{name}": np.ascontiguousarray(inputs[name]) for name in NAMES}
    arrays["in_const"] = constants()
    ins = {key[3:]: nc.dram_tensor(key, a.shape, mybir.dt.from_np(a.dtype), kind="ExternalInput").ap()
           for key, a in arrays.items()}
    out = nc.dram_tensor("out", (1, S, D), mybir.dt.float32, kind="ExternalOutput").ap()
    build(nc, ins, out)
    return run_bass_kernel_spmd(nc, [arrays], core_ids=[0]).results[0]["out"]
```

```python
import math
from contextlib import ExitStack

import numpy as np

import concourse.bass as bass
from concourse import mybir

P = 128
S = 256
T = S // P
D = 1024
KD = D // P
FF = 2816
SLOT = 2048
SC = SLOT // KD
RING = 3
CHUNKS = FF // SC
EPS = 1e-6
HEADS_R, HEADS_M, NOPE, ROPE, DV = 6, 6, 64, 32, 128
QR, KVR = 256, 128
QKW = NOPE + ROPE
MH, MD = 4, 64
TOK = 768
AH, AD = 8, 64
CAUSAL = 384
WINDOWS = (2, 4, 8, 16)
N_MEM, N_FFN, N_RET, N_MLA, N_STICK, N_WO = 4, 3 * CHUNKS, 13, 5, 10, 4
SUBLAYERS = ("ffn", "ret", "ffn", "ffn", "mla", "ffn", "ffn", "stick", "ffn", "ffn", "stick", "ffn")
SLOTS_OF = {"ffn": N_FFN, "ret": N_RET + N_WO, "mla": N_MLA + N_WO, "stick": N_STICK + N_WO}

CONST = {}
_at = 0
for _name, _width in (("ident", P), ("tri", P), ("ones", P),
                      ("negmask", CAUSAL), ("addmask", CAUSAL), ("poolrc", 2 * S), ("minhalf", 16),
                      ("invret", 1), ("sign", 1), ("invmla", 16),
                      ("fwd", 2 * S), ("bwd", 2 * S)):
    CONST[_name] = (_at, _at + _width)
    _at += _width
N_CONST = _at
TAIL = 3
KEPT = CONST["fwd"][0]
RET_ORDER = (6, 7, 8, 12, 0, 1, 2, 3, 4, 5, 9, 10, 11)
SOFT_AT = {(4, 0): 0, (4, 1): 1, (5, 0): 2, (5, 1): 3, (6, 0): 4, (6, 1): 5, (7, 0): 6, (7, 1): 7}
RET_AT = {(8, 1): 0, (9, 0): 1, (9, 1): 2, (10, 0): 3, (10, 1): 4, (11, 0): 5, (11, 1): 6}
TURN_AT = {(12, 0): 0, (12, 1): 1}
WO_ORDER = {"ret": (0, 1, 3, 2), "mla": (0, 1, 2, 3), "stick": (0, 3, 2, 1)}
STICK_ORDER = (4, 5, 0, 2, 9, 1, 3, 6, 7, 8)
BIG = 11264


def constants():
    c = np.zeros((P, N_CONST), np.float32)

    def put(name, value):
        a, b = CONST[name]
        c[:, a:b] = np.asarray(value, np.float32).reshape(P, b - a)

    p = np.arange(P)[:, None]
    put("ident", np.eye(P))
    s = p[:, :, None] + P * np.arange(2)[None, :, None]
    t = np.arange(S)[None, None, :]
    put("fwd", np.maximum(t - s, 0))
    put("bwd", np.maximum(s - t, 0))
    put("tri", p >= np.arange(P)[None, :])
    put("ones", np.ones((P, P)))
    diag = p < np.arange(P)[None, :]
    live = np.concatenate([diag, np.ones((P, P), bool), diag], axis=1)
    put("negmask", np.where(live, -1.0, 0.0))
    put("addmask", np.where(live, 0.0, -1e30))
    group = (p[:, :, None] + P * np.arange(2)[None, :, None]) // 64
    put("poolrc", 1.0 / np.minimum(t + 1, np.array(WINDOWS)[group]))
    put("minhalf", np.full((P, 16), -0.5))
    inv = lambda dim: (1.0 / (np.float32(10000.0) ** (np.arange(0, dim, 2, dtype=np.float32) / dim))).astype(np.float32)
    put("invret", inv(P)[np.arange(P) % 64])
    put("sign", np.where(np.arange(P) < 64, -1.0, 1.0))
    put("invmla", np.tile(inv(ROPE), (P, 1)))
    return c


def build(nc, ins, out):
    f32, f32r, i32 = mybir.dt.float32, mybir.dt.float32r, mybir.dt.int32
    ACT, ALU, AX = mybir.ActivationFunctionType, mybir.AluOpType, mybir.AxisListType
    ctx = ExitStack()
    with ctx:
        sb = lambda name, shape, dt=f32: ctx.enter_context(nc.sbuf_tensor(name, shape, dt))
        ps = lambda name, n: ctx.enter_context(nc.psum_tensor(name, [P, n], f32))
        sem = lambda name: ctx.enter_context(nc.semaphore(name))

        raw = sb("raw", [P, RING, SLOT])
        w_hi = sb("w_hi", [P, RING, SLOT], f32r)
        w_lo = sb("w_lo", [P, RING, SLOT], f32r)
        x = sb("x", [P, T, D])
        xn = sb("xn", [P, T, D])
        h_hi = sb("h_hi", [P, KD, S], f32r)
        h_lo = sb("h_lo", [P, KD, S], f32r)
        m_hi = sb("m_hi", [P, KD, S], f32r)
        m_lo = sb("m_lo", [P, KD, S], f32r)
        act_hi, act_lo = m_hi[:, 0:2, :], m_lo[:, 0:2, :]
        junk = sb("junk", [P, D], mybir.dt.bfloat16)
        upd = sb("upd", [P, D])
        pre_gain = sb("pre_gain", [P, D])
        post_gain = sb("post_gain", [P, D])
        stat = sb("stat", [P, 32])
        const = sb("const", [P, KEPT])
        mk_T = sb("mk_T", [P, 2, 2, S])
        mv = sb("mv", [P, 2, 2, S])
        nat = xn
        pos_row = sb("pos_row", [P, S], i32)
        pos_col = sb("pos_col", [P, T], i32)
        trig = sb("trig", [P, 2, S + 2 * 16])
        lgd = sb("lgd", [P, 2 * HEADS_R])
        big = sb("big", [P, BIG])

        cst = lambda name: const[:, CONST[name][0]:CONST[name][1]]
        ident = cst("ident")

        class Area:
            def __init__(self):
                self.at = 0

            def take(self, *shape):
                n = int(np.prod(shape))
                v = big[:, self.at:self.at + n]
                self.at += n
                assert self.at <= BIG
                if len(shape) == 2:
                    v = v.rearrange("p (a b) -> p a b", a=shape[0])
                if len(shape) == 3:
                    v = v.rearrange("p (a b c) -> p a b c", a=shape[0], b=shape[1])
                return v

        ar = Area()
        decay = ar.take(HEADS_R, 2 * S)
        r_q, r_k = ar.take(HEADS_R, S), ar.take(HEADS_R, S)
        r_v, r_g = ar.take(T, TOK), ar.take(T, TOK)
        r_sc = ar.take(2, 2 * S)
        ar_soft = ar.at
        qm_T = ar.take(2, S)
        prob = r_sc
        af = Area()
        af.take(HEADS_R, 2 * S)
        silu_g, act = af.take(2 * S), af.take(2 * S)
        mem_rows = af.take(T, D)
        ang = af.take(4, S + 2 * 16)
        posf = af.take(S + T)
        offsets = af.take(2, 2 * S)
        am = Area()
        q_nat = am.take(T, HEADS_M * QKW)
        kv_nat = am.take(T, HEADS_M * (NOPE + DV))
        k_nat = am.take(T, HEADS_M * QKW)
        mq_T, mk2_T = am.take(HEADS_M, S), am.take(HEADS_M, S)
        c_nat = am.take(T, QR + KVR)
        kr = am.take(T, ROPE)
        rt = am.take(4, HEADS_M * 16)
        assert am.at <= ar_soft
        prob_T = upd[:, :].rearrange("p (a b) -> p a b", a=2)
        as_ = Area()
        s_q, s_k = as_.take(4, S), as_.take(4, S)
        s_v = as_.take(T, AH * AD)
        gate_b, gate_c, conv_h, pool_p = (as_.take(2, S) for _ in range(4))
        z_abs = as_.take(2, CAUSAL)
        z_ln = as_.take(2, CAUSAL)
        z_lk = as_.take(2, CAUSAL)
        z_a = as_.take(2, CAUSAL)
        conv_u, conv_y = as_.take(2, S), as_.take(2, S)
        pool_a, pool_b, pool_c, pool_e = (as_.take(2, S) for _ in range(4))
        small = sb("small", [P, 2, 8])
        pool_w = sb("pool_w", [P, 2, P])
        c_gain = sb("c_gain", [P, QR + KVR])
        rope_sw = sb("rope_sw", [P, 2 * S])
        rope_t = sb("rope_t", [P, 2 * S])
        bn = sb("bn", [P, 2 * HEADS_R, 6])
        mean_var = sb("mean_var", [P, 2 * HEADS_R, 2])
        r_rs = sb("r_rs", [P, 2 * HEADS_R])
        sm = sb("sm", [P, 2, 2, 4])
        c_hi, c_lo = h_hi[:, 0:3, :], h_lo[:, 0:3, :]
        hgain = sb("hgain", [P, TOK])

        bank0, bank1 = ps("bank0", 512), ps("bank1", 512)
        down = [ps("down0", 1024), ps("down1", 1024)]
        bank6, bank7 = ps("bank6", 512), ps("bank7", 512)
        gemm_bank = [bank0, bank1]
        mid = [down[0][:, 0:512], down[0][:, 512:1024], down[1][:, 0:512], down[1][:, 512:1024]]
        ukv_banks = [bank0, bank1, bank6, bank7, mid[0], mid[1]]
        qk_banks = [mid[2], mid[3], bank0, bank1, bank6, bank7]

        raw_in = [sem(f"raw_in{r}") for r in range(RING)]
        hi_ready, lo_ready = sem("hi_ready"), sem("lo_ready")
        slot_done = sem("slot_done")
        silu_done, prod_done = sem("silu_done"), sem("prod_done")
        act_hi_done, act_lo_done, act_turned = sem("act_hi_done"), sem("act_lo_done"), sem("act_turned")
        down_done = sem("down_done")
        square, update = sem("square"), sem("update")
        post_ss, post_rs, x_new = sem("post_ss"), sem("post_rs"), sem("x_new")
        pre_ss, pre_rs, pre_xn = sem("pre_ss"), sem("pre_rs"), sem("pre_xn")
        turned, h_hi_done, h_lo_done = sem("turned"), sem("h_hi_done"), sem("h_lo_done")
        const_in, x_in, mem_in, small_in = sem("const_in"), sem("x_in"), sem("mem_in"), sem("small_in")
        pre_in, post_in = sem("pre_in"), sem("post_in")
        out_done = sem("out_done")
        dve_link, pool_link, act_link = sem("dve_link"), sem("pool_link"), sem("act_link")
        ang_ready, trig_ready, table_ready = sem("ang_ready"), sem("trig_ready"), sem("table_ready")
        expo_ready, decay_ready = sem("expo_ready"), sem("decay_ready")
        evac = sem("evac")
        rope_swapped, rope_cos, roped = sem("rope_swapped"), sem("rope_cos"), sem("roped")
        g_scaled = sem("g_scaled")
        r_scores, r_decayed, r_out, r_copied = sem("r_scores"), sem("r_decayed"), sem("r_out"), sem("r_copied")
        r_var, r_rs_ready, r_mix = sem("r_var"), sem("r_rs_ready"), sem("r_mix")
        m_turned, m_hi_done, m_lo_done = sem("m_turned"), sem("m_hi_done"), sem("m_lo_done")
        a_scores, a_max, a_exp, a_norm = sem("a_scores"), sem("a_max"), sem("a_exp"), sem("a_norm")
        a_turned, a_probT, a_out, a_hi, a_lo = (sem(n) for n in ("a_turned", "a_probT", "a_out", "a_hi", "a_lo"))
        c_ss, c_rs, c_xn = sem("c_ss"), sem("c_rs"), sem("c_xn")
        c_turned, c_hi_done, c_lo_done = sem("c_turned"), sem("c_hi_done"), sem("c_lo_done")
        uq_out, ukv_out = sem("uq_out"), sem("ukv_out")
        qk_ready, qk_turned, qk_T = sem("qk_ready"), sem("qk_turned"), sem("qk_T")
        s_z, s_abs, s_lk = sem("s_z"), sem("s_abs"), sem("s_lk")
        s_cs, s_min, s_exp, s_out, s_hi, s_lo = (sem(n) for n in ("s_cs", "s_min", "s_exp", "s_out", "s_hi", "s_lo"))
        conv_done, conv_hi, conv_lo = sem("conv_done"), sem("conv_hi"), sem("conv_lo")
        pool_d, pool_mm, pool_hi, pool_lo = sem("pool_d"), sem("pool_mm"), sem("pool_hi"), sem("pool_lo")
        pool_w_zero = sem("pool_w_zero")

        block = ctx.enter_context(nc.Block())

        first_slot, n = [], N_MEM
        for kind in SUBLAYERS:
            first_slot.append(n)
            n += SLOTS_OF[kind]
        N_SLOTS = n
        U = len(SUBLAYERS)

        def wait(eng, s, value):
            if value > 0:
                eng.wait_ge(s, value)

        def linker(eng, s):
            count = [0]

            def link(instruction):
                count[0] += 1
                instruction.then_inc(s, 1)
                eng.wait_ge(s, count[0])
            return link

        def cols(w, c0, width):
            return w[:, c0:c0 + width].rearrange("(k p) c -> p k c", p=P)

        @block.sync
        def _(sp):
            def slot(n, src, width=SLOT, at=None):
                r = n % RING
                m = n if at is None else at
                if at is not None or n >= RING:
                    sp.wait_ge(lo_ready, m - RING + 1)
                dst = raw[:, r, 0:width]
                if len(src.shape) == 3:
                    dst = dst.rearrange("p (a b) -> p a b", a=src.shape[1])
                sp.dma_start(dst, src).then_inc(raw_in[r], 16)

            def mem_w(j):
                return cols(ins["mem_w_kv"][j % 2], SC if j < 2 else 0, SC)

            for t in range(T):
                sp.dma_start(mem_rows[:, t, :], ins["mem"][0, t * P:(t + 1) * P, :]).then_inc(mem_in, 16)
            sp.dma_start(const[:, :], ins["const"][:, 0:KEPT]).then_inc(const_in, 16)
            for j in range(3):
                slot(j, mem_w(j))
            for t in range(T):
                sp.dma_start(x[:, t, :], ins["x"][0, t * P:(t + 1) * P, :]).then_inc(x_in, 16)
            slot(3, mem_w(3))
            sp.dma_start(offsets, ins["const"][:, KEPT:N_CONST].rearrange("p (a b) -> p a b", a=2)).then_inc(small_in, 16)
            sp.dma_start(pos_row[:, :], ins["positions"][0, :].partition_broadcast(P)).then_inc(small_in, 16)
            sp.dma_start(pos_col[:, :], ins["positions"][0, :].rearrange("(t p) -> p t", p=P), allow_slow_non_contiguous=True).then_inc(small_in, 16)
            sp.dma_start(lgd[:, :], ins["ret_log_decay"].rearrange("a b c -> (a b c)").partition_broadcast(P)).then_inc(small_in, 16)
            sp.dma_start(hgain[:, :], ins["ret_head_norm"].rearrange("a b c -> (a b c)").partition_broadcast(P)).then_inc(small_in, 16)
            sp.dma_start(c_gain[:, 0:QR], ins["mla_q_norm"][0, :].partition_broadcast(P)).then_inc(small_in, 16)
            sp.dma_start(c_gain[:, QR:QR + KVR], ins["mla_kv_norm"][0, :].partition_broadcast(P)).then_inc(small_in, 16)
            stick = 0
            for u, kind in enumerate(SUBLAYERS):
                b = first_slot[u]
                l = u // 3
                if kind == "ffn":
                    f = (u % 3) // 2
                    if l < 2:
                        gu = ins["ffn_w_gu"][l, f]
                        wg, wu, wd = gu[:, 0:FF], gu[:, FF:2 * FF], ins["ffn_w_down"][l, f]
                    else:
                        wg, wu, wd = ins["ffn_w_gate_2"][l - 2, f], ins["ffn_w_up_2"][l - 2, f], ins["ffn_w_down_2"][l - 2, f]
                    wgv = wg.rearrange("(k p) c -> p k c", p=P)
                    wuv = wu.rearrange("(k p) c -> p k c", p=P)
                    wdv = wd.rearrange("(i j p) c -> p i j c", j=2, p=P)
                    gate = lambda n, i, at=None: slot(n, wgv[:, :, bass.ds(i * SC, SC)], at=at)
                    up = lambda n, i, at=None: slot(n, wuv[:, :, bass.ds(i * SC, SC)], at=at)
                    lower = lambda n, i, at=None: slot(n, wdv[:, bass.ds(i, 1), :, :].rearrange("p a j c -> p (a j) c"), at=at)
                    gate(b, 0)
                    up(b + 1, 0)
                    gate(b + 2, 1)
                    up(b + 3, 1)
                    lower(b + 4, 0)
                    with sp.Fori(1, CHUNKS - TAIL) as i:
                        gate(b + 2, i + 1, b + 2 + 3 * i)
                        lower(b + 3, i, b + 3 + 3 * i)
                        up(b + 4, i + 1, b + 4 + 3 * i)
                    n = b + 2 + 3 * (CHUNKS - TAIL)
                    for i in range(CHUNKS - TAIL + 1, CHUNKS):
                        gate(n, i)
                        up(n + 1, i)
                        n += 2
                    for i in range(CHUNKS - TAIL, CHUNKS):
                        lower(n, i)
                        n += 1
                    continue
                if kind == "ret":
                    w, wo = ins["ret_w_in"][0], ins["w_o"][l]
                    for j in range(N_RET):
                        slot(b + j, cols(w, RET_ORDER[j] * SC, SC))
                    b += N_RET
                elif kind == "mla":
                    w, wo = ins["mla_w_in"][0], ins["w_o"][l]
                    slot(b, cols(w, 0, QR))
                    slot(b + 1, cols(w, QR, SC))
                    slot(b + 2, cols(w, QR + KVR + ROPE, SC))
                    slot(b + 3, cols(ins["mla_w_uq"][0], 0, HEADS_M * QKW), 2 * HEADS_M * QKW)
                    slot(b + 4, ins["mla_w_ukv"][0], HEADS_M * (NOPE + DV))
                    b += N_MLA
                else:
                    w, wo = ins["w_in_2"][l - 2], ins["w_out_2"][l - 2]
                    for a in range(3):
                        if stick:
                            wait(sp, conv_done, 2 * stick)
                        sp.dma_start(small[:, :, a:a + 1], ins["conv_w_2"][l - 2, a, :].rearrange("(j p) -> p j", p=P).unsqueeze(2), allow_slow_non_contiguous=True).then_inc(small_in, 16)
                    if stick:
                        wait(sp, pool_lo, 2 * stick)
                    sp.dma_start(small[:, :, 3:4], ins["pool_scale_2"][l - 2, :].rearrange("(j p) -> p j", p=P).unsqueeze(2), allow_slow_non_contiguous=True).then_inc(small_in, 16)
                    sp.wait_ge(pool_w_zero, 1)
                    for g in range(4):
                        o = 64 * (g % 2)
                        sp.dma_start(pool_w[o:o + 64, g // 2, o:o + 64], ins["pool_w_2"][l - 2, g]).then_inc(small_in, 16)
                    stick += 1
                    for j in range(N_STICK):
                        slot(b + j, cols(w, STICK_ORDER[j] * SC, SC))
                    b += N_STICK
                wov = wo.rearrange("(i j p) c -> p i j c", j=2, p=P)
                for j in range(N_WO):
                    slot(b + j, wov[:, WO_ORDER[kind][j], :, :])
            for t in range(T):
                sp.wait_ge(x_new, 4 * (U - 1) + 2 * t + 2)
                sp.dma_start(out[0, t * P:(t + 1) * P, :], x[:, t, :]).then_inc(out_done, 16)
            sp.wait_ge(out_done, 16 * T)

        SMALL_FIRST = 7 * 16
        SMALL_STICK = 8 * 16

        @block.tensor
        def _(pe):
            mm, tr = nc.tensor.matmul, nc.tensor.transpose

            def take(n, at=None):
                pe.wait_ge(lo_ready, (n if at is None else at) + 1)

            def cols_of(n, bank, hi=h_hi, lo=h_lo, tiles=range(2)):
                r = n % RING
                for j in tiles:
                    o = bank[:, j * S:(j + 1) * S]
                    for k in range(KD):
                        c = k * SC + j * P
                        mm(o, w_hi[:, r, c:c + P], hi[:, k, :], start=(k == 0), stop=False)
                        mm(o, w_hi[:, r, c:c + P], lo[:, k, :], start=False, stop=False)
                        last = mm(o, w_lo[:, r, c:c + P], hi[:, k, :], start=False, stop=(k == KD - 1))
                return last

            def gemm_cols(n, bank, at=None):
                take(n, at)
                cols_of(n, bank).then_inc(slot_done, 1)

            def gemm_rows_into(n, o, t, k_tiles, width, c0, n_cols, hi, lo):
                r = n % RING
                for i, k in enumerate(k_tiles):
                    c = i * width + c0
                    ts = slice(t * P, (t + 1) * P)
                    first, end = i == 0, i == len(k_tiles) - 1
                    mm(o, hi[:, k, ts], w_hi[:, r, c:c + n_cols], start=first, stop=False)
                    mm(o, hi[:, k, ts], w_lo[:, r, c:c + n_cols], start=False, stop=False)
                    last = mm(o, lo[:, k, ts], w_hi[:, r, c:c + n_cols], start=False, stop=end)
                return last

            def rows_of(n, bank, t, hi=h_hi, lo=h_lo):
                return gemm_rows_into(n, bank[:, t * S:(t + 1) * S], t, range(KD), SC, 0, SC, hi, lo)

            def gemm_rows(n, bank):
                take(n)
                for t in range(T):
                    last = rows_of(n, bank, t)
                last.then_inc(slot_done, 1)

            def high_passes(n, bank, p, t, hi, lo):
                pe.wait_ge(hi_ready, n + 1)
                o, ts = bank[:, t * S:(t + 1) * S], slice(t * P, (t + 1) * P)
                for k in range(KD):
                    c = k * SC
                    if k % 4 == 0:
                        pe.wait_ge(h_lo_done, 4 * p + 2 * t + k // 4 + 1)
                    mm(o, hi[:, k, ts], w_hi[:, n % RING, c:c + SC], start=(k == 0), stop=False)
                    mm(o, lo[:, k, ts], w_hi[:, n % RING, c:c + SC], start=False, stop=False)

            def low_pass(n, bank, t, hi):
                take(n)
                o, ts = bank[:, t * S:(t + 1) * S], slice(t * P, (t + 1) * P)
                for k in range(KD):
                    c = k * SC
                    last = mm(o, hi[:, k, ts], w_lo[:, n % RING, c:c + SC], start=False, stop=(k == KD - 1))
                return last

            def first_slots(p, parts, hi=h_hi, lo=h_lo, second=lambda: None):
                if p == 0:
                    turn(p, 0)
                for t in range(T):
                    for n, bank in parts:
                        if t == 0 and n == parts[1][0]:
                            second()
                        high_passes(n, bank, p, t, hi, lo)
                        if t == T - 1:
                            low_pass(n, bank, t, hi).then_inc(slot_done, 1)
                    if t == 0:
                        turn(p, 1)
                        for n, bank in parts:
                            low_pass(n, bank, t, hi)

            def down_of(n, k0, t, hi, lo, first, end, halves=range(2)):
                r, ts = n % RING, slice(t * P, (t + 1) * P)
                for j in range(2):
                    for part, (a, w) in enumerate(((hi, w_hi), (hi, w_lo), (lo, w_hi))):
                        for c in halves:
                            last = mm(down[t][:, c * 512:(c + 1) * 512], a[:, k0 + j, ts],
                                      w[:, r, j * D + c * 512:j * D + (c + 1) * 512],
                                      start=(first and j == 0 and part == 0), stop=(end and j == 1 and part == 2))
                return last

            def gemm_down(n, k0, first, at=None, second=lambda: None):
                take(n, at)
                for t in range(T):
                    if t == T - 1:
                        second()
                    last = down_of(n, k0, t, m_hi, m_lo, first, False)
                last.then_inc(slot_done, 1)

            def down_tail(n, k0s, p, ready=lambda i: None):
                for t in range(T):
                    for i in range(TAIL - 1):
                        if t == 0:
                            take(n + i)
                            ready(i)
                        last = down_of(n + i, k0s[i], t, m_hi, m_lo, False, False)
                        if t == T - 1:
                            last.then_inc(slot_done, 1)
                    i = TAIL - 1
                    if t == 0:
                        take(n + i)
                        ready(i)
                    for c in range(2):
                        last = down_of(n + i, k0s[i], t, m_hi, m_lo, False, True, (c,))
                        last.then_inc(*((slot_done, 1) if (t, c) == (T - 1, 1) else (down_done, 1)))
                        if (t, c) == (T - 1, 0) and p <= U:
                            turn(p, 0)

            def turn(p, t):
                for c in range(2):
                    pe.wait_ge(pre_xn, 4 * p + 2 * t + c + 1)
                    for k in range(4):
                        last = tr((bank6, bank7)[c][:, k * P:(k + 1) * P], xn[:, t, (4 * c + k) * P:(4 * c + k + 1) * P], ident)
                    last.then_inc(turned, 1)

            def soft_step(heads, i):
                if i < len(heads):
                    a, q, k, _, _ = heads[i]
                    wait(pe, a_exp, 2 * (a - 1))
                    for t in range(T):
                        last = mm(mid[a % 2][:, t * S:(t + 1) * S], q[:, t * P:(t + 1) * P], k, start=True, stop=True)
                    last.then_inc(a_scores, 1)
                if 0 <= i - 2 < len(heads):
                    a = heads[i - 2][0]
                    pe.wait_ge(a_norm, a + 1)
                    wait(pe, a_probT, a - 1)
                    for kt in range(2):
                        for t in range(T):
                            last = tr(mid[2 + a % 2][:, kt * S + t * P:kt * S + (t + 1) * P],
                                      prob[:, a % 2, t * S + kt * P:t * S + (kt + 1) * P], ident)
                    last.then_inc(a_turned, 1)
                if 0 <= i - 3 < len(heads):
                    a, _, _, value, (o0, o1) = heads[i - 3]
                    pe.wait_ge(a_probT, a + 1)
                    wait(pe, a_lo, a - 1)
                    for kt in range(2):
                        last = mm((bank6, bank7)[a % 2][o0:o1, 0:S], value(kt), prob_T[:, a % 2, kt * S:(kt + 1) * S],
                                  start=(kt == 0), stop=(kt == 1))
                    last.then_inc(a_out, 1)

            def ret_step(h):
                if h < HEADS_R:
                    pe.wait_ge(roped, 3 + h // 2 + 1)
                    wait(pe, r_decayed, h - 1)
                    for s in range(2):
                        last = mm(mid[h % 2][:, s * S:(s + 1) * S], r_k[:, h, s * P:(s + 1) * P], r_q[:, h, :], start=True, stop=True)
                    last.then_inc(r_scores, 1)
                if h:
                    g = h - 1
                    pe.wait_ge(r_decayed, g + 1)
                    wait(pe, r_copied, g - 1)
                    for t in range(T):
                        for s in range(2):
                            last = mm(mid[2 + g % 2][:, t * P:(t + 1) * P], r_sc[:, g % 2, s * S + t * P:s * S + (t + 1) * P],
                                      r_v[:, s, g * DV:(g + 1) * DV], start=(s == 0), stop=(s == 1))
                    last.then_inc(r_out, 1)

            def turn_pair(p):
                pe.wait_ge(r_mix, p + 1)
                wait(pe, m_lo_done, p - 1)
                for k in range(2):
                    for t in range(T):
                        last = tr((bank6, bank7)[p % 2][:, k * S + t * P:k * S + (t + 1) * P],
                                  nat[:, t, (2 * p + k) * P:(2 * p + k + 1) * P], ident)
                last.then_inc(m_turned, 1)

            def wo_ready(i):
                if i == 1:
                    turn_pair(2)
                    pe.wait_ge(a_lo, MH)
                else:
                    pe.wait_ge(m_lo_done, 2 if i == 0 else 3)

            def mem_heads(l, a0):
                for h in range(MH):
                    o = 64 * (h % 2)
                    yield (a0 + h, qm_T[o:o + 64, h // 2, :], mk_T[o:o + 64, l, h // 2, :],
                           lambda kt, h=h: mv[:, l, kt, h * MD:(h + 1) * MD], (o, o + 64))

            evacs = [0]

            def next_bank():
                e = evacs[0]
                evacs[0] += 1
                wait(pe, evac, e - 1)
                return gemm_bank[e % 2]

            pe.wait_ge(const_in, 16)
            first_slots(0, [(n, next_bank()) for n in range(2)], m_hi, m_lo)
            take(2)
            cols_of(2, next_bank(), m_hi, m_lo).then_inc(slot_done, 1)
            take(3)
            bank = next_bank()
            cols_of(3, bank, m_hi, m_lo, tiles=(0,))
            turn(1, 0)
            cols_of(3, bank, m_hi, m_lo, tiles=(1,)).then_inc(slot_done, 1)
            pe.wait_ge(evac, evacs[0] - 1)

            ffns, sticks = 0, 0
            for u, kind in enumerate(SUBLAYERS):
                b = first_slot[u]
                if kind == "ffn":
                    e = CHUNKS * ffns
                    first_slots(u + 1, [(b, bank0), (b + 1, bank1)], second=lambda: pe.wait_ge(evac, evacs[0]))

                    def chunk(n, i, at=None):
                        pe.wait_ge(silu_done, e + 1 + i)
                        gemm_cols(n, bank0, at)
                        pe.wait_ge(act_lo_done, e + 1 + i)
                        gemm_down(n + 1, 0, False, at + 1)
                        gemm_cols(n + 2, bank1, at + 2)

                    pe.wait_ge(silu_done, e + 1)
                    gemm_cols(b + 2, bank0)
                    pe.wait_ge(prod_done, e + 1)
                    for j in range(2):
                        for t in range(T):
                            last = tr(bank6[:, j * S + t * P:j * S + (t + 1) * P], act[:, t * SC + j * P:t * SC + (j + 1) * P], ident)
                    last.then_inc(act_turned, 1)
                    gemm_cols(b + 3, bank1)
                    pe.wait_ge(act_lo_done, e + 1)
                    gemm_down(b + 4, 2, True)
                    with pe.Fori(1, CHUNKS - TAIL) as i:
                        chunk(b + 2, i, at=b + 2 + 3 * i)
                    n = b + 2 + 3 * (CHUNKS - TAIL)
                    for i in range(CHUNKS - TAIL + 1, CHUNKS):
                        pe.wait_ge(silu_done, e + i)
                        gemm_cols(n, bank0)
                        pe.wait_ge(prod_done, e + i)
                        gemm_cols(n + 1, bank1)
                        n += 2
                    down_tail(n, range(0, 2 * TAIL, 2), u + 2, lambda i: pe.wait_ge(act_lo_done, e + CHUNKS - TAIL + i + 1))
                    ffns += 1
                    continue
                if kind == "ret":
                    mem = list(mem_heads(0, 0))
                    first_slots(u + 1, [(b + j, next_bank()) for j in range(2)])
                    for j in range(2, N_RET):
                        if 6 <= j < 12:
                            pe.wait_ge(rope_cos, j - 5)
                        bank = next_bank()
                        take(b + j)
                        for half in range(2):
                            if j < 3 or j >= 10:
                                last = rows_of(b + j, bank, half)
                            else:
                                last = cols_of(b + j, bank, tiles=(half,))
                            if half == 1:
                                last.then_inc(slot_done, 1)
                            at = (j, half)
                            if at == (4, 0):
                                pe.wait_ge(evac, N_MEM + 4)
                            if at in SOFT_AT:
                                soft_step(mem, SOFT_AT[at])
                            if at in RET_AT:
                                ret_step(RET_AT[at])
                            if at in TURN_AT:
                                turn_pair(TURN_AT[at])
                    pe.wait_ge(m_lo_done, 1)
                    b += N_RET
                elif kind == "mla":
                    first_slots(u + 1, [(b + j, next_bank()) for j in range(2)])
                    gemm_cols(b + 2, next_bank())
                    pe.wait_ge(c_xn, 2)
                    for t in range(T):
                        for k in range(3):
                            bank, kk = (bank6, k) if k < 2 else (bank7, 0)
                            last = tr(bank[:, kk * S + t * P:kk * S + (t + 1) * P], c_nat[:, t, k * P:(k + 1) * P], ident)
                    last.then_inc(c_turned, 1)
                    pe.wait_ge(c_lo_done, 2)
                    take(b + 3)
                    half = HEADS_M * QKW // 2
                    for t in range(T):
                        for c in range(2):
                            last = gemm_rows_into(b + 3, mid[2 * t + c][:, 0:half], t, range(2), 2 * half, c * half, half, c_hi, c_lo)
                    last.then_inc(slot_done, 1)
                    pe.wait_ge(evac, evacs[0])
                    take(b + 4)
                    third = HEADS_M * (NOPE + DV) // 3
                    for t in range(T):
                        for c in range(3):
                            if (t, c) == (1, 1):
                                pe.wait_ge(uq_out, 2)
                            bank = ukv_banks[3 * t + c]
                            last = gemm_rows_into(b + 4, bank[:, 0:third], t, (2,), 3 * third, c * third, third, c_hi, c_lo)
                    last.then_inc(slot_done, 1)
                    pe.wait_ge(uq_out, 4)
                    pe.wait_ge(qk_ready, 1)
                    for i in range(6):
                        if i == 2:
                            pe.wait_ge(ukv_out, 1)
                        if i == 3:
                            pe.wait_ge(ukv_out, 6)
                            pe.wait_ge(qk_ready, 2)
                        src = q_nat if i < 3 else k_nat
                        bank = qk_banks[i]
                        for g in range(2):
                            h = 2 * (i % 3) + g
                            for t in range(T):
                                last = tr(bank[0:QKW, g * S + t * P:g * S + (t + 1) * P], src[:, t, h * QKW:(h + 1) * QKW], ident)
                        last.then_inc(qk_turned, 1)
                    pe.wait_ge(qk_T, 6)
                    heads = [(MH + h, mq_T[0:QKW, h, :], mk2_T[0:QKW, h, :],
                                  lambda kt, h=h: kv_nat[:, kt, h * (NOPE + DV) + NOPE:(h + 1) * (NOPE + DV)], (0, P))
                                 for h in range(HEADS_M)]
                    heads += mem_heads(1, MH + HEADS_M)
                    for i in range(len(heads) + 1):
                        soft_step(heads, i)
                    pe.wait_ge(a_exp, 2 * (2 * MH + HEADS_M))
                    pe.wait_ge(a_lo, MH + 2)
                    b += N_MLA
                else:
                    c0 = 4 * sticks

                    def logits(s, banks, start, stop):
                        for g in range(2):
                            o = 64 * g
                            k, q = s_k[o:o + 64, s, :], s_q[o:o + 64, s, :]
                            yield g, 0, mm(banks[g][:, 0:S], k[:, 0:P], q, start=start, stop=stop)
                            yield g, 1, mm(banks[g][:, S:CAUSAL], k[:, P:S], q[:, P:S], start=start, stop=stop)

                    def pair_logits(s):
                        for _, _, last in logits(s, mid[0:2], True, True):
                            pass
                        last.then_inc(s_z, 1)

                    def pair_sums(s):
                        pe.wait_ge(s_lk, c0 + s + 1)
                        wait(pe, s_min, c0 + s)
                        tri, ones = cst("tri"), cst("ones")
                        for g in range(2):
                            o = 64 * g
                            k, q = s_k[o:o + 64, s, :], s_q[o:o + 64, s, :]
                            lk = z_lk[:, g, :]
                            first, second = mid[2 + g][:, 0:S], mid[2 + g][:, S:CAUSAL]
                            mm(first, k[:, 0:P], q, start=True, stop=False)
                            mm(first, tri, lk[:, 0:S], start=False, stop=False)
                            mm(mid[2 + g][:, P:S], ones, lk[:, S:CAUSAL], start=False, stop=True)
                            mm(second, k[:, P:S], q[:, P:S], start=True, stop=False)
                            last = mm(second, tri, lk[:, S:CAUSAL], start=False, stop=True)
                        last.then_inc(s_cs, 1)

                    def pair_out(s):
                        pe.wait_ge(s_exp, c0 + s + 1)
                        wait(pe, s_lo, c0 + s - 1)
                        bank = (bank6, bank7)[s % 2]
                        for g in range(2):
                            h = 2 * s + g
                            o = slice(64 * g, 64 * g + 64)
                            mm(bank[o, 0:S], s_v[:, 0, h * AD:(h + 1) * AD], z_a[:, g, 0:S], start=True, stop=False)
                            last = mm(bank[o, P:S], s_v[:, 1, h * AD:(h + 1) * AD], z_a[:, g, S:CAUSAL], start=False, stop=True)
                        last.then_inc(s_out, 1)

                    first_slots(u + 1, [(b + j, next_bank()) for j in range(2)])
                    for j in (2, 3):
                        gemm_cols(b + j, next_bank())

                    def half_slot(j, tile, bank):
                        if tile == 0:
                            take(b + j)
                        last = cols_of(b + j, bank, tiles=(tile,))
                        if tile == 1:
                            last.then_inc(slot_done, 1)

                    bank = next_bank()
                    half_slot(4, 0, bank)
                    pe.wait_ge(evac, evacs[0] - 1)
                    pair_logits(0)
                    half_slot(4, 1, bank)
                    gemm_cols(b + 5, next_bank())
                    pair_sums(0)
                    pair_logits(1)
                    gemm_cols(b + 6, next_bank())
                    pair_out(0)
                    bank = next_bank()
                    half_slot(7, 0, bank)
                    pair_sums(1)
                    pe.wait_ge(evac, evacs[0] - 1)
                    pair_logits(2)
                    half_slot(7, 1, bank)
                    pair_out(1)
                    gemm_cols(b + 8, next_bank())
                    pair_sums(2)
                    pair_logits(3)
                    gemm_cols(b + 9, next_bank())
                    pair_out(2)
                    pair_sums(3)
                    pe.wait_ge(evac, evacs[0])
                    pe.wait_ge(pool_d, sticks + 1)
                    pe.wait_ge(small_in, SMALL_FIRST + SMALL_STICK * (sticks + 1))
                    for j in range(2):
                        last = mm(bank0[:, j * S:(j + 1) * S], pool_w[:, j, :], pool_e[:, j, :], start=True, stop=True)
                    last.then_inc(pool_mm, 1)
                    pe.wait_ge(s_lo, c0 + 2)
                    sticks += 1
                    b += N_STICK
                def second():
                    if kind == "stick":
                        pe.wait_ge(s_min, 4 * sticks)
                    elif kind == "mla":
                        soft_step(heads, len(heads) + 1)
                        soft_step(heads, len(heads) + 2)

                gemm_down(b, 2 * WO_ORDER[kind][0], True, second=second)
                if kind == "stick":
                    pair_out(3)

                def stick_ready(i):
                    s, count = ((pool_lo, 2 * sticks), (conv_lo, sticks), (s_lo, 4 * sticks))[i]
                    pe.wait_ge(s, count)

                def mla_ready(i):
                    pe.wait_ge(a_lo, MH + (4, 6, HEADS_M + MH)[i])

                down_tail(b + 1, [2 * k for k in WO_ORDER[kind][1:]], u + 2,
                          {"ret": wo_ready, "stick": stick_ready, "mla": mla_ready}[kind])

        @block.scalar
        def _(sc):
            act_fn = nc.scalar.activation
            link = linker(sc, act_link)

            def square_sum(src, dst, s, scale, bias):
                junk_free()
                act_fn(junk[:, 0:src.shape[1]], src, ACT.Square, scale=scale, accum_out=dst).then_inc(square, 1)
                squares[0] += 1
                junk_free()
                act_fn(dst, dst, ACT.Copy, bias=bias).then_inc(s, 1)

            def half_sum(src, c, parts, scale, bias):
                junk_free()
                act_fn(junk[:, c * 512:(c + 1) * 512], src[:, c * 512:(c + 1) * 512], ACT.Square, scale=scale,
                       accum_out=parts[c]).then_inc(square, 1)
                squares[0] += 1
                if c == 0:
                    junk_free()
                    act_fn(parts[0], parts[0], ACT.Copy, bias=bias).then_inc(square, 1)
                    squares[0] += 1

            def both_halves(parts, dst, s):
                junk_free()
                act_fn(dst, parts[1], ACT.Identity, bias=parts[0]).then_inc(s, 1)

            def junk_free():
                wait(sc, square, squares[0])

            squares = [0]

            def high(n, at=None, base=None):
                m = n if at is None else at
                if at is None:
                    sc.wait_ge(raw_in[n % RING], 16 * (n // RING + 1))
                    wait(sc, slot_done, n - RING + 1)
                else:
                    i, n0 = base
                    sc.wait_ge(raw_in[n0 % RING], i * 16 + 16 * (n0 // RING + 1))
                    sc.wait_ge(slot_done, m - RING + 1)
                r = n % RING
                act_fn(w_hi[:, r, :], raw[:, r, :], ACT.Copy).then_inc(hi_ready, 1)

            def pre_sum(p, t):
                parts = [stat[:, i + t:i + t + 1] for i in (2, 6)]
                for c in range(2):
                    if p == 0:
                        sc.wait_ge(mem_in, 16 * T)
                    elif p == 1:
                        sc.wait_ge(x_in, 16 * T)
                    else:
                        sc.wait_ge(x_new, 4 * (p - 2) + 2 * t + c + 1)
                    half_sum((mem_rows if p == 0 else x)[:, t, :], c, parts, D ** -0.5, EPS)
                both_halves(parts, stat[:, t:t + 1], pre_ss)

            def pre_high(p, t):
                dst = m_hi if p == 0 else h_hi
                for c in range(2):
                    sc.wait_ge(turned, 4 * p + 2 * t + c + 1)
                    act_fn(dst[:, 4 * c:4 * c + 4, t * P:(t + 1) * P],
                           (bank6, bank7)[c][:, :].rearrange("p (k t) -> p k t", k=4), ACT.Copy).then_inc(h_hi_done, 1)

            def post_half(u, t, c):
                if (t, c) == (T - 1, 1):
                    sc.wait_ge(slot_done, first_slot[u] + SLOTS_OF[SUBLAYERS[u]])
                else:
                    sc.wait_ge(down_done, 3 * u + 2 * t + c + 1)
                half = 1.0 if u % 3 == 1 else 0.5
                parts = [stat[:, i + t:i + t + 1] for i in (10, 14)]
                half_sum(down[t][:, :], c, parts, D ** -0.5 / half, EPS / half ** 2)
                if c == 1:
                    both_halves(parts, stat[:, 8 + t:9 + t], post_ss)

            def between(u):
                b = first_slot[u] + SLOTS_OF[SUBLAYERS[u]]
                post_half(u, 0, 0)
                post_half(u, 0, 1)
                if u + 1 == U:
                    post_half(u, 1, 0)
                    post_half(u, 1, 1)
                    return
                pre_sum(u + 2, 0)
                high(b)
                post_half(u, 1, 0)
                pre_high(u + 2, 0)
                post_half(u, 1, 1)
                high(b + 1)
                pre_sum(u + 2, 1)
                high(b + 2)
                pre_high(u + 2, 1)

            evacs = [0]

            def copy_out(n, dst, func=ACT.Copy, scale=1.0, width=SC):
                sc.wait_ge(slot_done, n + 1)
                src = gemm_bank[evacs[0] % 2][:, :].rearrange("p (a b) -> p a b", a=2)[:, :, 0:width]
                act_fn(dst, src, func, scale=scale).then_inc(evac, 1)
                evacs[0] += 1

            def soft_step(heads, i):
                if 0 <= i - 4 < len(heads):
                    a, _, parts, k = heads[i - 4]
                    sc.wait_ge(a_out, a + 1)
                    act_fn(m_hi[parts, k, :], (bank6, bank7)[a % 2][parts, 0:S], ACT.Copy).then_inc(a_hi, 1)
                if i < len(heads):
                    a, scale, _, _ = heads[i]
                    sc.wait_ge(a_max, a + 1)
                    wait(sc, a_turned, a - 1)
                    for t in range(T):
                        act_fn(prob[:, a % 2, t * S:(t + 1) * S], mid[a % 2][:, t * S:(t + 1) * S], ACT.Exp,
                               bias=sm[:, a % 2, t, 1:2], scale=scale, accum_out=sm[:, a % 2, t, 2:3]).then_inc(a_exp, 1)
                if 0 <= i - 2 < len(heads):
                    a = heads[i - 2][0]
                    sc.wait_ge(a_turned, a + 1)
                    wait(sc, a_out, a - 1)
                    act_fn(prob_T[:, a % 2, :], mid[2 + a % 2], ACT.Copy).then_inc(a_probT, 1)

            def mem_heads(a0):
                return [(a0 + h, 1.0, slice(64 * (h % 2), 64 * (h % 2) + 64), 6 + h // 2) for h in range(MH)]

            for t in range(T):
                pre_sum(0, t)
            pre_high(0, 0)
            high(0)
            high(1)
            pre_high(0, 1)
            high(2)
            for n in range(N_MEM):
                if n == 3:
                    pre_high(1, 0)
                copy_out(n, (mv if n < 2 else mk_T)[:, n % 2, :, :])
                high(n + 3)
                if n == 1:
                    for t in range(T):
                        pre_sum(1, t)
            pre_high(1, 1)

            def tables():
                sc.wait_ge(ang_ready, 1)
                act_fn(trig[:, 0, :], ang[:, 3, :], ACT.Sin).then_inc(trig_ready, 1)
                act_fn(trig[:, 1, :], ang[:, 2, :], ACT.Sin).then_inc(trig_ready, 1)
                sc.wait_ge(expo_ready, HEADS_R)
                act_fn(decay, decay, ACT.Exp).then_inc(decay_ready, 1)

            ffns, sticks = 0, 0
            for u, kind in enumerate(SUBLAYERS):
                b = first_slot[u]
                if kind == "ffn":
                    e = CHUNKS * ffns

                    def silu(n):
                        sc.wait_ge(slot_done, n)
                        act_fn(silu_g, bank0[:, :], ACT.Silu).then_inc(silu_done, 1)

                    def act_high(i, k0=0):
                        sc.wait_ge(prod_done, e + 1 + i)
                        act_fn(m_hi[:, k0:k0 + 2, :], act.rearrange("p (a b) -> p a b", a=2), ACT.Copy).then_inc(act_hi_done, 1)

                    silu(b + 1)
                    high(b + 3)
                    high(b + 4)
                    sc.wait_ge(prod_done, e + 1)
                    silu(b + 3)
                    sc.wait_ge(act_turned, ffns + 1)
                    act_fn(m_hi[:, 2:4, :], bank6[:, :].rearrange("p (a b) -> p a b", a=2), ACT.Copy).then_inc(act_hi_done, 1)
                    high(b + 5)
                    high(b + 6)
                    act_high(1)
                    high(b + 7)
                    with sc.Fori(1, CHUNKS - TAIL) as i:
                        silu(b + 3 + 3 * i)
                        high(b + 5, b + 5 + 3 * i, (i, b + 5))
                        high(b + 6, b + 6 + 3 * i, (i, b + 6))
                        act_high(i + 1)
                        high(b + 7, b + 7 + 3 * i, (i, b + 7))
                    if u == 0:
                        tables()
                    n = b + 2 + 3 * (CHUNKS - TAIL)
                    for i in range(1, TAIL):
                        silu(n + 1)
                        high(n + 3)
                        if i == TAIL - 1:
                            high(n + 4)
                        act_high(CHUNKS - TAIL + i, 2 * i)
                        if i < TAIL - 1:
                            high(n + 4)
                        n += 2
                    b += N_FFN
                    ffns += 1
                else:
                    if kind == "ret":
                        mem = mem_heads(0)

                        def pair_high(p):
                            sc.wait_ge(m_turned, p + 1)
                            act_fn(m_hi[:, 2 * p:2 * p + 2, :], (bank6, bank7)[p % 2][:, :].rearrange("p (k t) -> p k t", k=2),
                                   ACT.Copy).then_inc(m_hi_done, 1)

                        def steps(at):
                            if at in SOFT_AT:
                                soft_step(mem, SOFT_AT[at])
                            if RET_AT.get(at, 0):
                                g = RET_AT[at] - 1
                                sc.wait_ge(r_out, g + 1)
                                act_fn(nat[:, :, g * DV:(g + 1) * DV], mid[2 + g % 2][:, 0:2 * P].rearrange("p (t d) -> p t d", t=2),
                                       ACT.Copy).then_inc(r_copied, 1)
                            if at in TURN_AT:
                                pair_high(TURN_AT[at])

                        for j in range(N_RET):
                            steps((j, 0))
                            if 4 <= j < 10:
                                sc.wait_ge(slot_done, b + j + 1)
                                wait(sc, roped, j - 4)
                                bank = gemm_bank[evacs[0] % 2]
                                act_fn(rope_sw[0:64, :], bank[64:P, :], ACT.Copy).then_inc(rope_swapped, 1)
                                act_fn(rope_sw[64:P, :], bank[0:64, :], ACT.Copy).then_inc(evac, 1)
                                evacs[0] += 1
                            elif j < 3:
                                copy_out(b + j, r_v[:, :, j * SC:(j + 1) * SC])
                            elif j == 3:
                                copy_out(b + j, qm_T, scale=MD ** -0.5)
                            else:
                                copy_out(b + j, r_g[:, :, (j - 10) * SC:(j - 9) * SC], ACT.Silu)
                            steps((j, 1))
                            high(b + j + 3)
                        b += N_RET
                    elif kind == "mla":
                        copy_out(b, c_nat[:, :, 0:QR])
                        high(b + 3)
                        sc.wait_ge(slot_done, b + 2)
                        src = gemm_bank[evacs[0] % 2][:, :].rearrange("p (a b) -> p a b", a=2)
                        link(act_fn(c_nat[:, :, QR:QR + KVR], src[:, :, 0:KVR], ACT.Copy))
                        act_fn(kr, src[:, :, KVR:KVR + ROPE], ACT.Copy).then_inc(evac, 1)
                        evacs[0] += 1
                        sc.wait_ge(evac, evacs[0])
                        for t in range(T):
                            square_sum(c_nat[:, t, 0:QR], stat[:, 16 + t:17 + t], c_ss, QR ** -0.5, EPS)
                            square_sum(c_nat[:, t, QR:QR + KVR], stat[:, 18 + t:19 + t], c_ss, KVR ** -0.5, EPS)
                        high(b + 4)
                        copy_out(b + 2, qm_T, scale=MD ** -0.5)
                        sc.wait_ge(c_turned, 1)
                        act_fn(c_hi[:, 0:2, :], bank6[:, :].rearrange("p (a b) -> p a b", a=2), ACT.Copy).then_inc(c_hi_done, 1)
                        act_fn(c_hi[:, 2, :], bank7[:, 0:S], ACT.Copy).then_inc(c_hi_done, 1)
                        high(b + 5)
                        half = HEADS_M * QKW // 2
                        sc.wait_ge(slot_done, b + 4)
                        for t in range(T):
                            for c in range(2):
                                act_fn(q_nat[:, t, c * half:(c + 1) * half], mid[2 * t + c][:, 0:half], ACT.Copy).then_inc(uq_out, 1)
                        high(b + 6)
                        third = HEADS_M * (NOPE + DV) // 3
                        sc.wait_ge(slot_done, b + 5)
                        for t in range(T):
                            for c in range(3):
                                act_fn(kv_nat[:, t, c * third:(c + 1) * third], ukv_banks[3 * t + c][:, 0:third],
                                       ACT.Copy).then_inc(ukv_out, 1)
                        for i in range(6):
                            sc.wait_ge(qk_turned, i + 1)
                            dst = (mq_T if i < 3 else mk2_T)[0:QKW, 2 * (i % 3):2 * (i % 3) + 2, :]
                            act_fn(dst, qk_banks[i][0:QKW, :].rearrange("p (a b) -> p a b", a=2), ACT.Copy).then_inc(qk_T, 1)
                        heads = [(MH + h, QKW ** -0.5, slice(0, P), h) for h in range(HEADS_M)] + mem_heads(MH + HEADS_M)
                        for i in range(len(heads) + 4):
                            soft_step(heads, i)
                            if i == len(heads):
                                high(b + 7)
                        b += N_MLA
                    else:
                        c0 = 4 * sticks
                        places = (s_v[:, :, 0:SC], s_v[:, :, SC:2 * SC], s_q[:, 0:2, :], s_k[:, 0:2, :], pool_p,
                                  s_q[:, 2:4, :], s_k[:, 2:4, :], gate_b, gate_c, conv_h)

                        def slot_out(j):
                            copy_out(b + j, places[j], scale=AD ** -0.5 if j in (2, 5) else 1.0)

                        for j in range(4):
                            slot_out(j)
                            high(b + j + 3)

                        def pair_exp(s):
                            sc.wait_ge(s_min, c0 + s + 1)
                            wait(sc, s_out, c0 + s)
                            act_fn(z_a, z_abs, ACT.Exp).then_inc(s_exp, 1)

                        def pair_high(s):
                            sc.wait_ge(s_out, c0 + s + 1)
                            act_fn(m_hi[:, s, :], (bank6, bank7)[s % 2][:, 0:S], ACT.Copy).then_inc(s_hi, 1)

                        def pair_log(s):
                            sc.wait_ge(s_z, c0 + s + 1)
                            z = down[0][:, :].rearrange("p (a b) -> p a b", a=2)[:, :, 0:CAUSAL]
                            if s:
                                sc.wait_ge(s_exp, c0 + s)
                            act_fn(z_abs, z, ACT.Abs).then_inc(s_abs, 1)
                            sc.wait_ge(s_abs, 3 * (c0 + s) + 1)
                            act_fn(z_abs, z_abs, ACT.Exp, scale=-1.0).then_inc(s_abs, 1)
                            sc.wait_ge(s_abs, 3 * (c0 + s) + 2)
                            wait(sc, s_lk, c0 + s)
                            act_fn(z_ln, z_abs, ACT.Ln, bias=1.0).then_inc(s_abs, 1)

                        pair_log(0)
                        slot_out(4)
                        high(b + 7)
                        slot_out(5)
                        high(b + 8)
                        pair_exp(0)
                        pair_log(1)
                        slot_out(6)
                        pair_high(0)
                        high(b + 9)
                        pair_exp(1)
                        pair_log(2)
                        slot_out(7)
                        high(b + 10)
                        pair_high(1)
                        slot_out(8)
                        high(b + 11)
                        pair_exp(2)
                        pair_log(3)
                        slot_out(9)
                        pair_high(2)
                        high(b + 12)
                        pair_exp(3)
                        sc.wait_ge(small_in, SMALL_FIRST + SMALL_STICK * (sticks + 1))
                        sc.wait_ge(pool_mm, sticks + 1)
                        for j in range(2):
                            act_fn(m_hi[:, 6 + j, :], bank0[:, j * S:(j + 1) * S], ACT.Copy, scale=small[:, j, 3:4]).then_inc(pool_hi, 1)
                        sc.wait_ge(conv_done, 2 * (sticks + 1))
                        act_fn(m_hi[:, 4:6, :], conv_y, ACT.Copy).then_inc(conv_hi, 1)
                        pair_high(3)
                        sticks += 1
                        b += N_STICK
                    high(b + 3)
                    if kind == "ret":
                        pair_high(2)
                between(u)

        @block.vector
        def _(ve):
            v = nc.vector
            link = linker(ve, dve_link)

            def low(n, at=None):
                ve.wait_ge(hi_ready, (n if at is None else at) + 1)
                r = n % RING
                v.tensor_tensor(w_lo[:, r, :], raw[:, r, :], w_hi[:, r, :].bitcast(f32), ALU.subtract).then_inc(lo_ready, 1)

            def low_half(n, c):
                ve.wait_ge(hi_ready, n + 1)
                r, h = n % RING, slice(c * SLOT // 2, (c + 1) * SLOT // 2)
                last = v.tensor_tensor(w_lo[:, r, h], raw[:, r, h], w_hi[:, r, h].bitcast(f32), ALU.subtract)
                if c == 1:
                    last.then_inc(lo_ready, 1)

            def pre_scale(p, t):
                ve.wait_ge(pre_in, 16 * (p + 1))
                ve.wait_ge(pre_rs, 2 * p + t + 1)
                for c in range(2):
                    h = slice(c * 512, (c + 1) * 512)
                    wait(ve, turned, 4 * (p - 1) + 2 * t + c + 1)
                    v.scalar_tensor_tensor(xn[:, t, h], (mem_rows if p == 0 else x)[:, t, h], stat[:, 4 + t:5 + t],
                                           (post_gain if p == 0 else pre_gain)[:, h], ALU.mult, ALU.mult).then_inc(pre_xn, 1)

            def pre_low(p, t):
                hi, lo = (m_hi, m_lo) if p == 0 else (h_hi, h_lo)
                for c in range(2):
                    ve.wait_ge(h_hi_done, 4 * p + 2 * t + c + 1)
                    sl = (slice(None), slice(4 * c, 4 * c + 4), slice(t * P, (t + 1) * P))
                    v.tensor_tensor(lo[sl], (bank6, bank7)[c][:, :].rearrange("p (k t) -> p k t", k=4),
                                    hi[sl].bitcast(f32), ALU.subtract).then_inc(h_lo_done, 1)

            def post_norm(u, t):
                ve.wait_ge(post_in, 16 * (u + 1))
                ve.wait_ge(post_rs, 2 * u + t + 1)
                first_update = updates[0]
                for c in range(2):
                    h = slice(c * 512, (c + 1) * 512)
                    if t == 1:
                        ve.wait_ge(x_new, 4 * u + c + 1)
                    v.scalar_tensor_tensor(upd[:, h], down[t][:, h], stat[:, 12 + t:13 + t], post_gain[:, h],
                                           ALU.mult, ALU.mult).then_inc(update, 1)
                    updates[0] += 1
                for c in range(2):
                    h = slice(c * 512, (c + 1) * 512)
                    ve.wait_ge(update, first_update + c + 1)
                    v.tensor_tensor(x[:, t, h], x[:, t, h], upd[:, h], ALU.add).then_inc(x_new, 1)

            updates = [0]

            def between(u):
                b = first_slot[u] + SLOTS_OF[SUBLAYERS[u]]
                post_norm(u, 0)
                if u + 1 == U:
                    post_norm(u, 1)
                    return
                pre_scale(u + 2, 0)
                low_half(b, 0)
                pre_low(u + 2, 0)
                low_half(b, 1)
                post_norm(u, 1)
                low_half(b + 1, 0)
                pre_scale(u + 2, 1)
                low_half(b + 1, 1)
                pre_low(u + 2, 1)
                low(b + 2)

            def soft_step(heads, i):
                if 0 <= i - 4 < len(heads):
                    a, _, parts, k = heads[i - 4]
                    ve.wait_ge(a_hi, a + 1)
                    v.tensor_tensor(m_lo[parts, k, :], (bank6, bank7)[a % 2][parts, 0:S], m_hi[parts, k, :].bitcast(f32),
                                    ALU.subtract).then_inc(a_lo, 1)
                if i < len(heads):
                    a, scale, _, _ = heads[i]
                    ve.wait_ge(a_scores, a + 1)
                    link(v.reduce_max(sm[:, a % 2, :, 0], mid[a % 2].rearrange("p (a b) -> p a b", a=2), AX.X))
                    v.tensor_scalar(sm[:, a % 2, :, 1], sm[:, a % 2, :, 0], -scale, None, ALU.mult).then_inc(a_max, 1)
                if 0 <= i - 1 < len(heads):
                    a = heads[i - 1][0]
                    ve.wait_ge(a_exp, 2 * a + 2)
                    link(v.reciprocal(sm[:, a % 2, :, 3], sm[:, a % 2, :, 2]))
                    for t in range(T):
                        row = prob[:, a % 2, t * S:(t + 1) * S]
                        last = v.tensor_scalar(row, row, sm[:, a % 2, t, 3:4], None, ALU.mult)
                    last.then_inc(a_norm, 1)

            def mem_heads(a0):
                return [(a0 + h, 1.0, slice(64 * (h % 2), 64 * (h % 2) + 64), 6 + h // 2) for h in range(MH)]

            def angles():
                ve.wait_ge(small_in, SMALL_FIRST)
                ve.wait_ge(const_in, 16)
                link(v.tensor_copy(posf[:, 0:S], pos_row[:, :]))
                link(v.tensor_copy(posf[:, S:S + T], pos_col[:, :]))
                a0, a1, a2, a3 = (ang[:, j, :] for j in range(4))
                link(v.tensor_scalar(a0[:, 0:S], posf[:, 0:S], cst("invret"), None, ALU.mult))
                for t in range(T):
                    link(v.tensor_scalar(a0[:, S + 16 * t:S + 16 * t + 16], cst("invmla"), posf[:, S + t:S + t + 1], None, ALU.mult))
                magic = 1.5 * 2.0 ** 23
                link(v.tensor_scalar(a1, a0, 1.0 / (2.0 * math.pi), magic, ALU.mult, ALU.add))
                link(v.tensor_scalar(a1, a1, magic, None, ALU.subtract))
                turn1 = 6.28125
                turn2 = round((2.0 * math.pi - turn1) * 2.0 ** 21) / 2.0 ** 21
                turn3 = 2.0 * math.pi - turn1 - turn2
                link(v.scalar_tensor_tensor(a2, a1, -turn1, a0, ALU.mult, ALU.add))
                link(v.scalar_tensor_tensor(a0, a1, -turn2, a2, ALU.mult, ALU.add))
                link(v.scalar_tensor_tensor(a2, a1, -turn3, a0, ALU.mult, ALU.add))
                pi = float(np.nextafter(np.float32(math.pi), np.float32(0)))
                link(v.tensor_scalar(a2, a2, -pi, pi, ALU.max, ALU.min))
                link(v.tensor_scalar(a1, a2, -1.0, None, ALU.mult))
                link(v.tensor_tensor(a1, a1, a2, ALU.max))
                v.tensor_scalar(a3, a1, -1.0, math.pi / 2, ALU.mult, ALU.add).then_inc(ang_ready, 1)

            for t in range(T):
                pre_scale(0, t)
            pre_low(0, 0)
            low(0)
            low(1)
            pre_low(0, 1)
            low(2)
            low(3)
            low(4)
            for t in range(T):
                pre_scale(1, t)
            low(5)
            for t in range(T):
                pre_low(1, t)
            low(6)

            ffns, sticks = 0, 0
            for u, kind in enumerate(SUBLAYERS):
                b = first_slot[u]
                if kind == "ffn":
                    e = CHUNKS * ffns

                    def product(i, n):
                        ve.wait_ge(silu_done, e + 1 + i)
                        ve.wait_ge(slot_done, n)
                        v.tensor_tensor(act, bank1[:, :], silu_g, ALU.mult).then_inc(prod_done, 1)

                    def act_low(i, k0=0):
                        ve.wait_ge(act_hi_done, e + 1 + i)
                        v.tensor_tensor(m_lo[:, k0:k0 + 2, :], act.rearrange("p (a b) -> p a b", a=2),
                                        m_hi[:, k0:k0 + 2, :].bitcast(f32), ALU.subtract).then_inc(act_lo_done, 1)

                    product(0, b + 2)
                    low(b + 3)
                    low(b + 4)
                    ve.wait_ge(act_hi_done, e + 1)
                    v.tensor_tensor(m_lo[:, 2:4, :], bank6[:, :].rearrange("p (a b) -> p a b", a=2),
                                    m_hi[:, 2:4, :].bitcast(f32), ALU.subtract).then_inc(act_lo_done, 1)
                    low(b + 5)
                    product(1, b + 4)
                    low(b + 6)
                    act_low(1)
                    low(b + 7)
                    if u == 0:
                        angles()
                    with ve.Fori(1, CHUNKS - TAIL) as i:
                        low(b + 5, b + 5 + 3 * i)
                        low(b + 6, b + 6 + 3 * i)
                        product(i + 1, b + 5 + 3 * i)
                        act_low(i + 1)
                        low(b + 7, b + 7 + 3 * i)
                    n = b + 2 + 3 * (CHUNKS - TAIL)
                    for i in range(1, TAIL):
                        low(n + 3)
                        ve.wait_ge(act_lo_done, e + CHUNKS - TAIL + i)
                        product(CHUNKS - TAIL + i, n + 2)
                        if i == TAIL - 1:
                            low(n + 4)
                        act_low(CHUNKS - TAIL + i, 2 * i)
                        if i < TAIL - 1:
                            low(n + 4)
                        n += 2
                    b += N_FFN
                    ffns += 1
                else:
                    if kind == "ret":
                        mem = mem_heads(0)

                        def statistics(h):
                            ve.wait_ge(r_copied, h + 1)
                            for t in range(T):
                                last = v.bn_stats(bn[:, 2 * h + t, :], nat[:, t, h * DV:(h + 1) * DV])
                            link(last)
                            for t in range(T):
                                last = v.bn_aggr(mean_var[:, 2 * h + t, :], bn[:, 2 * h + t, :])
                            link(last)
                            if h % 2:
                                v.tensor_scalar(r_rs[:, 2 * h - 2:2 * h + 2], mean_var[:, 2 * h - 2:2 * h + 2, 1], EPS, None,
                                                ALU.add).then_inc(r_var, 1)

                        def gate_pair(p):
                            ve.wait_ge(r_rs_ready, p + 1)
                            for h in (2 * p, 2 * p + 1):
                                for t in range(T):
                                    i = 2 * h + t
                                    y = nat[:, t, h * DV:(h + 1) * DV]
                                    last = v.tensor_scalar(y, y, mean_var[:, i, 0:1], r_rs[:, i:i + 1], ALU.subtract, ALU.mult)
                            link(last)
                            ve.wait_ge(g_scaled, p + 1)
                            y = nat[:, :, p * SC:(p + 1) * SC]
                            v.tensor_tensor(y, y, r_g[:, :, p * SC:(p + 1) * SC], ALU.mult).then_inc(r_mix, 1)

                        def pair_low(p):
                            ve.wait_ge(m_hi_done, p + 1)
                            v.tensor_tensor(m_lo[:, 2 * p:2 * p + 2, :], (bank6, bank7)[p % 2][:, :].rearrange("p (k t) -> p k t", k=2),
                                            m_hi[:, 2 * p:2 * p + 2, :].bitcast(f32), ALU.subtract).then_inc(m_lo_done, 1)

                        def steps(at):
                            if at in SOFT_AT:
                                soft_step(mem, SOFT_AT[at])
                            h = RET_AT.get(at)
                            if h is not None and h < HEADS_R:
                                ve.wait_ge(r_scores, h + 1)
                                ve.wait_ge(decay_ready, 1)
                                wait(ve, r_out, h - 1)
                                v.scalar_tensor_tensor(r_sc[:, h % 2, :], mid[h % 2], P ** -0.5, decay[:, h, :],
                                                       ALU.mult, ALU.mult).then_inc(r_decayed, 1)
                            if h is not None and h >= 2:
                                statistics(h - 2)
                            if h == HEADS_R - 1:
                                gate_pair(0)
                            if at == (12, 0):
                                statistics(HEADS_R - 1)
                                gate_pair(1)
                                pair_low(0)

                        for j in range(N_RET):
                            if j < 3:
                                low(b + j + 3)
                            if j < 4:
                                continue
                            steps((j, 0))
                            low(b + j + 2)
                            if 4 <= j < 10:
                                ve.wait_ge(slot_done, b + j + 1)
                                ve.wait_ge(table_ready, 1)
                                wait(ve, roped, j - 4)
                                ve.wait_ge(rope_swapped, j - 3)
                                ve.wait_ge(evac, N_MEM + j + 1)
                                v.tensor_tensor(rope_t[:, :].rearrange("p (a b) -> p a b", a=2),
                                                gemm_bank[j % 2][:, :].rearrange("p (a b) -> p a b", a=2),
                                                trig[:, 0:1, 0:S].broadcast_to([P, 2, S]), ALU.mult).then_inc(rope_cos, 1)
                            steps((j, 1))
                        pair_low(1)
                        low(b + 15)
                        gate_pair(2)
                        b += N_RET
                    elif kind == "mla":
                        low(b + 3)
                        ve.wait_ge(c_rs, 1)
                        for t in range(T):
                            v.scalar_tensor_tensor(c_nat[:, t, 0:QR], c_nat[:, t, 0:QR], stat[:, 24 + t:25 + t], c_gain[:, 0:QR], ALU.mult, ALU.mult)
                            last = v.scalar_tensor_tensor(c_nat[:, t, QR:QR + KVR], c_nat[:, t, QR:QR + KVR], stat[:, 26 + t:27 + t],
                                                          c_gain[:, QR:QR + KVR], ALU.mult, ALU.mult)
                            last.then_inc(c_xn, 1)
                        ve.wait_ge(c_hi_done, 1)
                        v.tensor_tensor(c_lo[:, 0:2, :], bank6[:, :].rearrange("p (a b) -> p a b", a=2), c_hi[:, 0:2, :].bitcast(f32), ALU.subtract).then_inc(c_lo_done, 1)
                        ve.wait_ge(c_hi_done, 2)
                        v.tensor_tensor(c_lo[:, 2, :], bank7[:, 0:S], c_hi[:, 2, :].bitcast(f32), ALU.subtract).then_inc(c_lo_done, 1)
                        low(b + 4)

                        def rotate(x1, x2, t, heads):
                            n = heads * 16
                            tmp = [rt[:, j, 0:n].rearrange("p (a b) -> p a b", a=heads) for j in range(4)]
                            at = S + 16 * t
                            c = trig[:, 0:1, at:at + 16].broadcast_to([P, heads, 16])
                            s = trig[:, 1:2, at:at + 16].broadcast_to([P, heads, 16])
                            v.tensor_tensor(tmp[0], x1, c, ALU.mult)
                            v.tensor_tensor(tmp[1], x2, s, ALU.mult)
                            v.tensor_tensor(tmp[2], x1, s, ALU.mult)
                            link(v.tensor_tensor(tmp[3], x2, c, ALU.mult))
                            v.tensor_tensor(x1, tmp[0], tmp[1], ALU.subtract)
                            link(v.tensor_tensor(x2, tmp[2], tmp[3], ALU.add))

                        for t in range(T):
                            rotate(kr[:, t:t + 1, 0:16], kr[:, t:t + 1, 16:32], t, 1)
                        ve.wait_ge(uq_out, 4)
                        for t in range(T):
                            q = q_nat[:, t, :].rearrange("p (h d) -> p h d", h=HEADS_M)
                            rotate(q[:, :, NOPE:NOPE + 16], q[:, :, NOPE + 16:QKW], t, HEADS_M)
                        v.tensor_copy(k_nat[:, 0, 0:1], q_nat[:, 0, 0:1]).then_inc(qk_ready, 1)
                        ve.wait_ge(ukv_out, 6)
                        ve.wait_ge(qk_ready, 1)
                        for t in range(T):
                            k = k_nat[:, t, :].rearrange("p (h d) -> p h d", h=HEADS_M)
                            kv = kv_nat[:, t, :].rearrange("p (h d) -> p h d", h=HEADS_M)
                            v.tensor_copy(k[:, :, 0:NOPE], kv[:, :, 0:NOPE])
                            last = v.tensor_copy(k[:, :, NOPE:QKW], kr[:, t:t + 1, :].broadcast_to([P, HEADS_M, ROPE]))
                        last.then_inc(qk_ready, 1)
                        low(b + 5)
                        low(b + 6)
                        heads = [(MH + h, QKW ** -0.5, slice(0, P), h) for h in range(HEADS_M)] + mem_heads(MH + HEADS_M)
                        for i in range(len(heads) + 4):
                            soft_step(heads, i)
                            if i == len(heads):
                                low(b + 7)
                        b += N_MLA
                    else:
                        c0 = 4 * sticks
                        for j in range(4):
                            low(b + j + 3)

                        def pair_min(s):
                            ve.wait_ge(s_cs, c0 + s + 1)
                            cs = down[1][:, :].rearrange("p (a b) -> p a b", a=2)
                            for g in range(2):
                                last = v.scalar_tensor_tensor(z_abs[:, g, :], cs[:, g, 0:CAUSAL], 0.0, cst("addmask"), ALU.min, ALU.add)
                            last.then_inc(s_min, 1)

                        def pair_low(s):
                            ve.wait_ge(s_hi, c0 + s + 1)
                            v.tensor_tensor(m_lo[:, s, :], (bank6, bank7)[s % 2][:, 0:S], m_hi[:, s, :].bitcast(f32), ALU.subtract).then_inc(s_lo, 1)

                        def pair_keep(s):
                            ve.wait_ge(s_abs, 3 * (c0 + s) + 3)
                            z = down[0][:, :].rearrange("p (a b) -> p a b", a=2)
                            for g in range(2):
                                last = v.scalar_tensor_tensor(z_ln[:, g, :], z[:, g, 0:CAUSAL], 0.0, z_ln[:, g, :], ALU.max, ALU.add)
                            link(last)
                            for g in range(2):
                                last = v.tensor_tensor(z_lk[:, g, :], z_ln[:, g, :], cst("negmask"), ALU.mult)
                            last.then_inc(s_lk, 1)

                        pair_keep(0)
                        low(b + 7)
                        pair_min(0)
                        low(b + 8)
                        pair_keep(1)
                        pair_low(0)
                        pair_min(1)
                        low(b + 9)
                        pair_keep(2)
                        low(b + 10)
                        pair_low(1)
                        pair_min(2)
                        low(b + 11)
                        pair_keep(3)
                        pair_low(2)

                        def convolve(j):
                            link(v.tensor_scalar(conv_y[:, j, :], conv_u[:, j, :], small[:, j, 2:3], None, ALU.mult))
                            for tap, shift in ((1, 1), (0, 2)):
                                link(v.scalar_tensor_tensor(conv_y[:, j, shift:S], conv_u[:, j, 0:S - shift], small[:, j, tap:tap + 1],
                                                            conv_y[:, j, shift:S], ALU.mult, ALU.add))
                            v.tensor_tensor(conv_y[:, j, :], conv_y[:, j, :], gate_b[:, j, :], ALU.mult).then_inc(conv_done, 1)

                        ve.wait_ge(evac, 4 + N_RET + 3 + 10 * (sticks + 1))
                        ve.wait_ge(small_in, SMALL_FIRST + SMALL_STICK * (sticks + 1))
                        link(v.tensor_tensor(conv_u, gate_c, conv_h, ALU.mult))
                        convolve(0)
                        pair_min(3)
                        convolve(1)
                        ve.wait_ge(pool_hi, 2 * (sticks + 1))
                        for j in range(2):
                            v.scalar_tensor_tensor(m_lo[:, 6 + j, :], bank0[:, j * S:(j + 1) * S], small[:, j, 3:4],
                                                   m_hi[:, 6 + j, :].bitcast(f32), ALU.mult, ALU.subtract).then_inc(pool_lo, 1)
                        low(b + 12)
                        ve.wait_ge(conv_hi, sticks + 1)
                        v.tensor_tensor(m_lo[:, 4:6, :], conv_y, m_hi[:, 4:6, :].bitcast(f32), ALU.subtract).then_inc(conv_lo, 1)
                        pair_low(3)
                        sticks += 1
                        b += N_STICK
                    low(b + 3)
                    if kind == "ret":
                        pair_low(2)
                between(u)

        @block.gpsimd
        def _(gp):
            g = nc.gpsimd
            link = linker(gp, pool_link)
            half = cst("minhalf")

            def pre_root(p, t):
                gp.wait_ge(pre_ss, 2 * p + t + 1)
                g.tensor_tensor(stat[:, 4 + t:5 + t], stat[:, t:t + 1], half[:, 0:1], ALU.pow).then_inc(pre_rs, 1)

            def post_root(u, t):
                gp.wait_ge(post_ss, 2 * u + t + 1)
                g.tensor_tensor(stat[:, 12 + t:13 + t], stat[:, 8 + t:9 + t], half[:, 0:1], ALU.pow).then_inc(post_rs, 1)

            def load_gain(buf, s, src):
                gp.dma_start(buf[:, :], src.partition_broadcast(P)).then_inc(s, 16)

            def gain_row(u, i):
                l, f = u // 3, u % 3
                return ins["norm_gains"][l, 2 * f + i, :] if l < 2 else ins["norm_g_2"][l - 2, 2 * f + i, :]

            def load_pre_gain(p):
                wait(gp, pre_xn, 4 * p)
                load_gain(pre_gain, pre_in, gain_row(p - 1, 0))

            def load_post_gain(u):
                wait(gp, x_new, 4 * u)
                load_gain(post_gain, post_in, gain_row(u, 1))

            load_gain(post_gain, pre_in, ins["mem_norm"])
            gp.wait_ge(const_in, 16)
            for t in range(T):
                pre_root(0, t)
            gp.wait_ge(pre_in, 16)
            load_gain(pre_gain, pre_in, gain_row(0, 0))
            for t in range(T):
                pre_root(1, t)
            gp.wait_ge(small_in, SMALL_FIRST)
            for h in range(HEADS_R):
                e = decay[:, h, :]
                g.tensor_scalar(e, offsets[:, 0, :], lgd[:, h:h + 1], None, ALU.mult)
                link(g.tensor_scalar(rope_t[:, :], offsets[:, 1, :], lgd[:, HEADS_R + h:HEADS_R + h + 1], None, ALU.mult))
                last = g.tensor_tensor(e, e, rope_t[:, :], ALU.add)
                last.then_inc(expo_ready, 1)
                gp.wait_ge(expo_ready, h + 1)
            g.memset(pool_w[:, :, :], 0.0).then_inc(pool_w_zero, 1)
            gp.wait_ge(pre_xn, 4)
            load_post_gain(0)
            load_pre_gain(2)
            gp.wait_ge(trig_ready, 2)
            g.tensor_scalar(trig[:, 1, 0:S], trig[:, 1, 0:S], cst("sign"), None, ALU.mult).then_inc(table_ready, 1)
            sticks = 0
            for u, kind in enumerate(SUBLAYERS):
                if kind == "ret":
                    for j in range(6):
                        gp.wait_ge(rope_swapped, j + 1)
                        gp.wait_ge(evac, N_MEM + 4 + j + 1)
                        gp.wait_ge(table_ready, 1)
                        link(g.tensor_tensor(rope_sw[:, :].rearrange("p (a b) -> p a b", a=2), rope_sw[:, :].rearrange("p (a b) -> p a b", a=2),
                                             trig[:, 1:2, 0:S].broadcast_to([P, 2, S]), ALU.mult))
                        gp.wait_ge(rope_cos, j + 1)
                        dst = (r_q if j < 3 else r_k)[:, 2 * (j % 3):2 * (j % 3) + 2, :]
                        g.tensor_tensor(dst, rope_t[:, :].rearrange("p (a b) -> p a b", a=2),
                                        rope_sw[:, :].rearrange("p (a b) -> p a b", a=2), ALU.add).then_inc(roped, 1)
                    for p in range(3):
                        gp.wait_ge(evac, N_MEM + 11 + p)
                        c = slice(p * SC, (p + 1) * SC)
                        for t in range(T):
                            last = g.tensor_tensor(r_g[:, t, c], r_g[:, t, c], hgain[:, c], ALU.mult)
                        last.then_inc(g_scaled, 1)
                        gp.wait_ge(r_var, p + 1)
                        r = r_rs[:, 4 * p:4 * p + 4]
                        g.tensor_tensor(r, r, half[:, 0:4], ALU.pow).then_inc(r_rs_ready, 1)
                elif kind == "mla":
                    gp.wait_ge(c_ss, 4)
                    g.tensor_tensor(stat[:, 24:28], stat[:, 16:20], half[:, 0:4], ALU.pow).then_inc(c_rs, 1)
                elif kind == "stick":
                    gp.wait_ge(evac, 4 + N_RET + 3 + 10 * sticks + 5)
                    wait(gp, pool_mm, sticks)
                    sums = [pool_p, pool_a, pool_b, pool_a, pool_b]
                    for i, w in enumerate(WINDOWS):
                        src, dst, sh = sums[i], sums[i + 1], w // 2
                        g.tensor_copy(dst[:, :, 0:sh], src[:, :, 0:sh])
                        link(g.tensor_tensor(dst[:, :, sh:S], src[:, :, sh:S], src[:, :, 0:S - sh], ALU.add))
                        o = slice(64 * (i % 2), 64 * (i % 2) + 64)
                        link(g.tensor_copy(pool_c[o, i // 2, :], dst[o, i // 2, :]))
                    link(g.tensor_tensor(pool_c, pool_c, cst("poolrc").rearrange("p (a b) -> p a b", a=2), ALU.mult))
                    g.tensor_tensor(pool_e, pool_c, pool_p, ALU.subtract).then_inc(pool_d, 1)
                    sticks += 1
                post_root(u, 0)
                if u + 1 < U:
                    pre_root(u + 2, 0)
                post_root(u, 1)
                if u + 1 < U:
                    pre_root(u + 2, 1)
                    load_post_gain(u + 1)
                if u + 2 < U:
                    load_pre_gain(u + 3)


NAMES = ("x", "mem", "positions", "norm_gains", "ffn_w_gu", "ffn_w_down", "w_o", "mem_norm", "mem_w_kv", "ret_w_in",
         "ret_log_decay", "ret_head_norm", "mla_w_in", "mla_q_norm", "mla_kv_norm", "mla_w_uq", "mla_w_ukv",
         "norm_g_2", "ffn_w_gate_2", "ffn_w_up_2", "ffn_w_down_2", "w_in_2", "conv_w_2", "pool_w_2", "pool_scale_2",
         "w_out_2")


def kernel(**inputs):
    import concourse.bacc as bacc
    from concourse.bass_utils import run_bass_kernel_spmd

    nc = bacc.Bacc("TRN2", target_bir_lowering=False, num_devices=1)
    arrays = {f"in_{name}": np.ascontiguousarray(inputs[name]) for name in NAMES}
    arrays["in_const"] = constants()
    ins = {key[3:]: nc.dram_tensor(key, a.shape, mybir.dt.from_np(a.dtype), kind="ExternalInput").ap()
           for key, a in arrays.items()}
    out = nc.dram_tensor("out", (1, S, D), mybir.dt.float32, kind="ExternalOutput").ap()
    build(nc, ins, out)
    return run_bass_kernel_spmd(nc, [arrays], core_ids=[0]).results[0]["out"]
```
